# Optimizing a Trainium2 kernel written in Bass

```python
import jax
import jax.numpy as jnp
from jax import lax
import numpy as np

D_MODEL = 1024
BATCH = 1
SEQ = 256
DEPTH = 1

BRANCH_WIDTH = D_MODEL // 2
N_BRANCH = 3
ATTN_HEADS = 8
ATTN_HEAD_DIM = BRANCH_WIDTH // ATTN_HEADS
ATTN_WIDTH = ATTN_HEADS * ATTN_HEAD_DIM
MOBA_BLOCK = 256
MOBA_TOPK = 3
QUERY_CHUNK = 128
RWKV_HEAD_DIM = 64
RWKV_HEADS = BRANCH_WIDTH // RWKV_HEAD_DIM
RWKV_WIDTH = RWKV_HEADS * RWKV_HEAD_DIM
DECAY_LORA = 64
ICLR_LORA = 64
GATE_LORA = 128
VMIX_LORA = 32
LNX_EPS = 64e-5
POOL_WINDOWS = (2, 4, 8, 16)
POOL_GROUPS = 4
POOL_GROUP_DIM = BRANCH_WIDTH // POOL_GROUPS
POOL_WIDTH = POOL_GROUPS * POOL_GROUP_DIM
N_GROUPS = 4
EXPERTS_PER_GROUP = 8
N_EXPERTS = N_GROUPS * EXPERTS_PER_GROUP
EXPERT_TOPK = 2
EXPERT_HIDDEN = 512
EXPERT_ROW_BLOCK = 128
RMS_EPS = 1e-6
ATTN_OFF = 0
ATTN_COLS = 3 * ATTN_WIDTH
GATE_OFF = ATTN_OFF + ATTN_COLS
GATE_COLS = N_BRANCH * D_MODEL
POOL_OFF = GATE_OFF + GATE_COLS
RWKV_OFF = POOL_OFF + POOL_WIDTH
RWKV_COLS = 3 * RWKV_WIDTH + DECAY_LORA + ICLR_LORA + GATE_LORA
IN_COLS = RWKV_OFF + RWKV_COLS

kernel_name = 'hybrid_moba_rwkv7_pool_hiermoe'

def rmsnorm(x, g):
    xf = x.astype(jnp.float32)
    y = xf * lax.rsqrt(jnp.mean(xf * xf, axis=-1, keepdims=True) + RMS_EPS)
    return (y * g.astype(jnp.float32)).astype(x.dtype)

def alibi_slopes(n_heads):
    return jnp.asarray([2.0 ** (-8.0 * (i + 1) / n_heads) for i in range(n_heads)], dtype=jnp.float32)

def token_shift(z, mu):
    prev = jnp.pad(z[:, :-1], ((0, 0), (1, 0), (0, 0)))
    return z + (prev - z) * mu

def moba_attention(q, k, v, slopes):
    B, H, S, Dh = q.shape
    L = MOBA_BLOCK
    nb = -(-S // L)
    n_cand = max(nb, MOBA_TOPK)
    pad = nb * L - S
    kp = jnp.pad(k, ((0, 0), (0, 0), (0, pad), (0, 0)))
    vp = jnp.pad(v, ((0, 0), (0, 0), (0, pad), (0, 0)))
    kb = kp.reshape(B, H, nb, L, Dh)
    vb = vp.reshape(B, H, nb, L, Dh)
    kmean = jnp.mean(kb.astype(jnp.float32), axis=3)
    kmean = jnp.pad(kmean, ((0, 0), (0, 0), (0, n_cand - nb), (0, 0)))
    scale = Dh ** -0.5
    bi = jnp.arange(B)[:, None, None, None]
    hi = jnp.arange(H)[None, :, None, None]
    cand = jnp.arange(n_cand)
    offs = jnp.arange(L)
    slope5 = slopes[None, :, None, None, None]
    slope4 = slopes[None, :, None, None]

    def one_chunk(c):
        q0 = c * QUERY_CHUNK
        own = q0 // L
        qc = lax.dynamic_slice_in_dim(q, q0, QUERY_CHUNK, axis=2).astype(jnp.float32)
        tq = q0 + jnp.arange(QUERY_CHUNK)
        gate = jnp.einsum('bhqd,bhnd->bhqn', qc, kmean)
        gate = jnp.where(cand < own, gate, -jnp.inf)
        _, sel = lax.top_k(gate, MOBA_TOPK)
        valid = sel < own
        sel = jnp.minimum(sel, nb - 1)
        k_sel = kb[bi, hi, sel].astype(jnp.float32)
        dist = (tq[:, None, None] - (sel[..., None] * L + offs)).astype(jnp.float32)
        s_sel = jnp.einsum('bhqd,bhqjld->bhqjl', qc, k_sel) * scale - slope5 * dist
        s_sel = jnp.where(valid[..., None], s_sel, -jnp.inf)
        s_sel = s_sel.reshape(B, H, QUERY_CHUNK, MOBA_TOPK * L)
        k_own = lax.dynamic_slice_in_dim(kp, own * L, L, axis=2).astype(jnp.float32)
        v_own = lax.dynamic_slice_in_dim(vp, own * L, L, axis=2).astype(jnp.float32)
        dist_own = tq[:, None] - (own * L + offs)[None, :]
        s_own = jnp.einsum('bhqd,bhld->bhql', qc, k_own) * scale - slope4 * dist_own.astype(jnp.float32)
        s_own = jnp.where(dist_own >= 0, s_own, -jnp.inf)
        p = jax.nn.softmax(jnp.concatenate([s_sel, s_own], axis=-1), axis=-1)
        p_sel = p[..., :MOBA_TOPK * L].reshape(B, H, QUERY_CHUNK, MOBA_TOPK, L)
        v_sel = vb[bi, hi, sel].astype(jnp.float32)
        o = (jnp.einsum('bhqjl,bhqjld->bhqd', p_sel, v_sel)
             + jnp.einsum('bhql,bhld->bhqd', p[..., MOBA_TOPK * L:], v_own))
        return o.astype(q.dtype)

    out = lax.map(one_chunk, jnp.arange(S // QUERY_CHUNK))
    return jnp.moveaxis(out, 0, 2).reshape(B, H, S, Dh)

def wkv7_scan(r, w, k, v, a, b):
    B, S, H, N = r.shape

    def step(state, inp):
        r_t, w_t, k_t, v_t, a_t, b_t = inp
        sa = jnp.einsum('bhvk,bhk->bhv', state, a_t)
        state = (state * w_t[:, :, None, :] + sa[..., None] * b_t[:, :, None, :]
                 + v_t[..., None] * k_t[:, :, None, :])
        return state, jnp.einsum('bhvk,bhk->bhv', state, r_t)

    xs = (jnp.swapaxes(r, 0, 1), jnp.swapaxes(w, 0, 1), jnp.swapaxes(k, 0, 1),
          jnp.swapaxes(v, 0, 1), jnp.swapaxes(a, 0, 1), jnp.swapaxes(b, 0, 1))
    _, y = lax.scan(step, jnp.zeros((B, H, N, N), jnp.float32), xs)
    return jnp.swapaxes(y, 0, 1)

def rwkv7_time_mix(cols, v_first, w0, w_decay_up, a0, w_iclr_up, w_gate_up, k_k, k_a, r_k,
                   lnx_g, lnx_b, vmix):
    B, S, _ = cols.shape
    W = RWKV_WIDTH
    c = cols.astype(jnp.float32)
    o1 = 3 * W
    o2 = o1 + DECAY_LORA
    o3 = o2 + ICLR_LORA
    o4 = o3 + GATE_LORA
    r, k, v = c[..., :W], c[..., W:2 * W], c[..., 2 * W:o1]
    w_lo, a_lo, g_lo = c[..., o1:o2], c[..., o2:o3], c[..., o3:o4]

    def heads(t):
        return t.reshape(B, S, RWKV_HEADS, RWKV_HEAD_DIM)

    w_log = -jax.nn.softplus(-(w0 + jnp.tanh(w_lo) @ w_decay_up)) - 0.5
    decay = jnp.exp(-jnp.exp(w_log))
    if vmix is None:
        v_first = v
    else:
        vm_lo, v0, w_vmix_up = vmix
        v = v + (v_first - v) * jax.nn.sigmoid(v0 + vm_lo.astype(jnp.float32) @ w_vmix_up)
    a = jax.nn.sigmoid(a0 + a_lo @ w_iclr_up)
    g = jax.nn.sigmoid(g_lo) @ w_gate_up
    kk = heads(k * k_k)
    kk = kk / jnp.maximum(jnp.sqrt(jnp.sum(kk * kk, axis=-1, keepdims=True)), 1e-12)
    k = k * (1.0 + (a - 1.0) * k_a)
    r_h, k_h, v_h, a_h = heads(r), heads(k), heads(v), heads(a)
    y = wkv7_scan(r_h, heads(decay), k_h, v_h, -kk, kk * a_h)
    mu = jnp.mean(y, axis=-1, keepdims=True)
    var = jnp.mean(jnp.square(y - mu), axis=-1, keepdims=True)
    y = ((y - mu) * lax.rsqrt(var + LNX_EPS)).reshape(B, S, W) * lnx_g + lnx_b
    bonus = jnp.sum(r_h * k_h * r_k, axis=-1, keepdims=True) * v_h
    y = (y + bonus.reshape(B, S, W)) * g
    return y.astype(cols.dtype), v_first

def multiscale_pool(z, pool_w, pool_scale):
    B, S, _ = z.shape
    zf = z.astype(jnp.float32).reshape(B, S, POOL_GROUPS, POOL_GROUP_DIM)
    cum = jnp.cumsum(zf, axis=1)
    t1 = jnp.arange(1, S + 1, dtype=jnp.float32)[None, :, None]
    outs = []
    for gi, win in enumerate(POOL_WINDOWS):
        cg = cum[:, :, gi]
        lagged = jnp.pad(cg, ((0, 0), (win, 0), (0, 0)))[:, :S]
        outs.append((cg - lagged) / jnp.minimum(t1, float(win)) - zf[:, :, gi])
    p = jnp.stack(outs, axis=2)
    y = jnp.einsum('bsgc,gcd->bsgd', p, pool_w.astype(jnp.float32)).reshape(B, S, POOL_WIDTH)
    return (y * pool_scale).astype(z.dtype)

def hier_moe(h, rg_w, rg_b, re_w, re_b, w1, w3, w2):
    B, S, D = h.shape
    T = B * S
    hf = h.reshape(T, D)
    glog = (hf @ rg_w).astype(jnp.float32) + rg_b
    gprob = jax.nn.softmax(glog, axis=-1)
    grp = jnp.argmax(glog, axis=-1)
    elog = ((hf @ re_w).astype(jnp.float32) + re_b).reshape(T, N_GROUPS, EXPERTS_PER_GROUP)
    elog_g = jnp.take_along_axis(elog, grp[:, None, None], axis=1)[:, 0]
    top_v, top_i = lax.top_k(elog_g, EXPERT_TOPK)
    wts = jax.nn.softmax(top_v, axis=-1) * jnp.take_along_axis(gprob, grp[:, None], axis=1)
    eid = (grp[:, None] * EXPERTS_PER_GROUP + top_i).reshape(-1)
    tok = jnp.repeat(jnp.arange(T), EXPERT_TOPK)
    wts = wts.reshape(-1)
    A = T * EXPERT_TOPK
    blk = EXPERT_ROW_BLOCK
    order = jnp.argsort(eid)
    e_s, tok_s, w_s = eid[order], tok[order], wts[order]
    counts = jnp.bincount(eid, length=N_EXPERTS)
    starts = jnp.cumsum(counts) - counts
    padded = (counts + blk - 1) // blk * blk
    pends = jnp.cumsum(padded)
    pstarts = pends - padded
    dest = pstarts[e_s] + (jnp.arange(A) - starts[e_s])
    R = -(-(A + N_EXPERTS * (blk - 1)) // blk) * blk
    nblk = R // blk
    buf = jnp.zeros((R, D), h.dtype).at[dest].set(hf[tok_s])
    blk_e = jnp.minimum(jnp.searchsorted(pends, jnp.arange(nblk) * blk, side='right'), N_EXPERTS - 1)

    def expert_block(args):
        xb, e = args
        return (jax.nn.silu(xb @ w1[e]) * (xb @ w3[e])) @ w2[e]

    yb = lax.map(expert_block, (buf.reshape(nblk, blk, D), blk_e)).reshape(R, D)
    y = yb[dest] * w_s[:, None].astype(yb.dtype)
    out = jax.ops.segment_sum(y, tok_s, num_segments=T)
    return out.reshape(B, S, D).astype(h.dtype)

def setup_inputs(seed: int = 0) -> dict:
    key = jax.random.key(seed)
    ks = jax.random.split(key, 32)
    f32 = jnp.float32
    L = DEPTH
    Lr = DEPTH - 1

    def nrm(k, shape, scale):
        return jax.random.normal(k, shape, f32) * scale

    def near_one(k, shape):
        return 1.0 + 0.1 * jax.random.normal(k, shape, f32)

    return {
        'x': nrm(ks[0], (BATCH, SEQ, D_MODEL), 1.0),
        'norm1_g': near_one(ks[1], (L, D_MODEL)),
        'w_in': nrm(ks[2], (L, D_MODEL, IN_COLS), D_MODEL ** -0.5),
        'w_vmix': nrm(ks[3], (Lr, D_MODEL, VMIX_LORA), D_MODEL ** -0.5),
        'rwkv_mu': jax.random.uniform(ks[4], (L, RWKV_COLS), f32),
        'vmix_mu': jax.random.uniform(ks[5], (Lr, VMIX_LORA), f32),
        'w0': jax.random.uniform(ks[6], (L, RWKV_WIDTH), f32, minval=-3.0, maxval=1.0),
        'w_decay_up': nrm(ks[7], (L, DECAY_LORA, RWKV_WIDTH), 0.1),
        'a0': nrm(ks[8], (L, RWKV_WIDTH), 0.5),
        'w_iclr_up': nrm(ks[9], (L, ICLR_LORA, RWKV_WIDTH), ICLR_LORA ** -0.5),
        'w_gate_up': nrm(ks[10], (L, GATE_LORA, RWKV_WIDTH), GATE_LORA ** -0.5),
        'k_k': 0.85 + 0.1 * jax.random.normal(ks[11], (L, RWKV_WIDTH), f32),
        'k_a': near_one(ks[12], (L, RWKV_WIDTH)),
        'r_k': nrm(ks[13], (L, RWKV_HEADS, RWKV_HEAD_DIM), 0.1),
        'lnx_g': near_one(ks[14], (L, RWKV_WIDTH)),
        'lnx_b': nrm(ks[15], (L, RWKV_WIDTH), 0.01),
        'v0': nrm(ks[16], (Lr, RWKV_WIDTH), 0.5),
        'w_vmix_up': nrm(ks[17], (Lr, VMIX_LORA, RWKV_WIDTH), VMIX_LORA ** -0.5),
        'pool_w': nrm(ks[18], (L, POOL_GROUPS, POOL_GROUP_DIM, POOL_GROUP_DIM), POOL_GROUP_DIM ** -0.5),
        'pool_scale': near_one(ks[19], (L, POOL_WIDTH)),
        'w_branch': nrm(ks[20], (L, N_BRANCH, BRANCH_WIDTH, D_MODEL), BRANCH_WIDTH ** -0.5),
        'w_out': nrm(ks[21], (L, D_MODEL, D_MODEL), D_MODEL ** -0.5),
        'norm2_g': near_one(ks[22], (L, D_MODEL)),
        'router_grp_w': nrm(ks[23], (L, D_MODEL, N_GROUPS), D_MODEL ** -0.5),
        'router_grp_b': nrm(ks[24], (L, N_GROUPS), 0.01),
        'router_exp_w': nrm(ks[25], (L, D_MODEL, N_EXPERTS), D_MODEL ** -0.5),
        'router_exp_b': nrm(ks[26], (L, N_EXPERTS), 0.01),
        'exp_w1': nrm(ks[27], (L, N_EXPERTS, D_MODEL, EXPERT_HIDDEN), D_MODEL ** -0.5),
        'exp_w3': nrm(ks[28], (L, N_EXPERTS, D_MODEL, EXPERT_HIDDEN), D_MODEL ** -0.5),
        'exp_w2': nrm(ks[29], (L, N_EXPERTS, EXPERT_HIDDEN, D_MODEL), EXPERT_HIDDEN ** -0.5),
        'final_norm_g': near_one(ks[30], (D_MODEL,)),
    }

def reference(x, norm1_g, w_in, w_vmix, rwkv_mu, vmix_mu, w0, w_decay_up, a0, w_iclr_up,
              w_gate_up, k_k, k_a, r_k, lnx_g, lnx_b, v0, w_vmix_up, pool_w, pool_scale,
              w_branch, w_out, norm2_g, router_grp_w, router_grp_b, router_exp_w, router_exp_b,
              exp_w1, exp_w3, exp_w2, final_norm_g):
    B, S, D = x.shape
    slopes = alibi_slopes(ATTN_HEADS)
    v_first = None

    def attn_heads(t):
        return t.reshape(B, S, ATTN_HEADS, ATTN_HEAD_DIM).transpose(0, 2, 1, 3)

    for l in range(DEPTH):
        h = rmsnorm(x, norm1_g[l])
        if l == 0:
            w_cols, mu = w_in[l], rwkv_mu[l]
        else:
            w_cols = jnp.concatenate([w_in[l], w_vmix[l - 1]], axis=1)
            mu = jnp.concatenate([rwkv_mu[l], vmix_mu[l - 1]], axis=0)
        z = h @ w_cols
        q = attn_heads(z[..., ATTN_OFF:ATTN_OFF + ATTN_WIDTH])
        k = attn_heads(z[..., ATTN_OFF + ATTN_WIDTH:ATTN_OFF + 2 * ATTN_WIDTH])
        v = attn_heads(z[..., ATTN_OFF + 2 * ATTN_WIDTH:ATTN_OFF + 3 * ATTN_WIDTH])
        y_attn = moba_attention(q, k, v, slopes).transpose(0, 2, 1, 3).reshape(B, S, ATTN_WIDTH)
        rw = token_shift(z[..., RWKV_OFF:], mu)
        vmix = None if l == 0 else (rw[..., RWKV_COLS:], v0[l - 1], w_vmix_up[l - 1])
        y_rwkv, v_first = rwkv7_time_mix(rw[..., :RWKV_COLS], v_first, w0[l], w_decay_up[l], a0[l],
                                         w_iclr_up[l], w_gate_up[l], k_k[l], k_a[l], r_k[l],
                                         lnx_g[l], lnx_b[l], vmix)
        y_pool = multiscale_pool(z[..., POOL_OFF:POOL_OFF + POOL_WIDTH], pool_w[l], pool_scale[l])
        gates = jax.nn.sigmoid(z[..., GATE_OFF:GATE_OFF + GATE_COLS].astype(jnp.float32))
        gates = gates.reshape(B, S, N_BRANCH, D)
        ys = jnp.stack([y_attn.astype(x.dtype), y_rwkv.astype(x.dtype), y_pool.astype(x.dtype)], axis=2)
        proj = jnp.einsum('bsiw,iwd->bsid', ys, w_branch[l])
        merged = jnp.sum(gates * proj, axis=2).astype(x.dtype)
        x = x + merged @ w_out[l]
        h2 = rmsnorm(x, norm2_g[l])
        x = x + hier_moe(h2, router_grp_w[l], router_grp_b[l], router_exp_w[l], router_exp_b[l],
                         exp_w1[l], exp_w3[l], exp_w2[l])
    return rmsnorm(x, final_norm_g)


_drawn_inputs = setup_inputs


def setup_inputs(seed=0):
    import zlib

    import numpy as np

    out = dict(_drawn_inputs(seed))
    spreads = {}
    factors = {'k_k': 8.454, 'lnx_b': 9.267, 'router_grp_b': 6.21, 'router_exp_b': 4.077}
    for name, (base, spread) in spreads.items():
        noise = np.random.default_rng([zlib.crc32(name.encode()), seed]).standard_normal(out[name].shape)
        drawn = base * np.exp(spread * noise) if base else spread * noise
        out[name] = jnp.asarray(drawn.astype(out[name].dtype))
    for name, factor in factors.items():
        out[name] = (out[name] * factor).astype(out[name].dtype)
    return out
```

```python
from contextlib import ExitStack

import concourse.bass as bass
from concourse import mybir

ALU = mybir.AluOpType
ACT = mybir.ActivationFunctionType
AX = mybir.AxisListType
F32 = mybir.dt.float32
I32 = mybir.dt.int32

P = 128
T = 256
TT = T // P
D = 1024
KD = D // P
BW = 512
CT = BW // P
H = 8
DH = 64
NG, EPG = 4, 8
NE = NG * EPG
HID = 512
HC = HID // P
CAP = 64
ROUNDS = T // CAP
RMS_EPS = 1e-6
LNX_EPS = 64e-5
DECAY_SCALE = 0.6065306597126334
FAR = 1e30
PIECE = 4096

Q_COL, K_COL, V_COL = 0, BW, 2 * BW
GATE_COL = 3 * BW
POOL_COL = GATE_COL + 3 * D
R_COL = POOL_COL + BW
RK_COL, RV_COL, LORA_COL = R_COL + BW, R_COL + 2 * BW, R_COL + 3 * BW

PAR_ROWS = (("norm1_g", 8), ("rwkv_mu", 14), ("w0", 4), ("a0", 4), ("k_k", 4), ("k_a", 4),
            ("r_k", 4), ("lnx_g", 4), ("lnx_b", 4), ("pool_scale", 4))

PIECES = ["lora", "rk", "rr", "rv", "aq", "ak", "av", "pool", "gC0", "gC1", "pC",
          "gA0", "gA1", "pA", "gB0", "gB1", "pB", "wo0", "wo1"]
TRUNK_SLOTS = 4
SLOTS = 6

LEVELS = (2, 4, 8, 16, 32, 64)


def fill_plan():
    plan = [("par", 1)] + [(f"hT{n}", 0) for n in range(4)]
    plan += [("lora", 0), ("rk0", 0), ("rk1", 0)]
    plan += [("u0", 1), ("u1", 1), ("a0", 1), ("a1", 1)]
    plan += [("rr0", 0), ("rr1", 0), ("rv0", 0), ("rv1", 0), ("ss0", 1), ("ss1", 1)]
    plan += [("aq0", 0), ("aq1", 0), ("ak0", 0), ("ak1", 0), ("av0", 0), ("av1", 0), ("pool0", 0), ("pool1", 0)]
    plan += [("vn0", 1), ("vn1", 1), ("bn", 1), ("kn", 1), ("bon0", 1), ("bon1", 1)]
    plan += [(f"sc{n}", 1) for n in range(16)]
    plan += [(f"at{n}", 0) for n in range(6)]
    plan += [(f"L{g}", 1) for g in range(4)] + [(f"G1_{g}", 1) for g in range(4)]
    for b in LEVELS:
        plan += [(f"A{b}_{g}", 1) for g in range(4)]
        plan += [(f"T{b}_{g}", 1) for g in range(4)]
        plan += [(f"G{b}_{g}", 1) for g in range(4)]
    plan += [(f"pt{h}", 0) for h in range(5)] + [("o0", 1)]
    plan += [(f"pt{h}", 0) for h in range(5, 8)] + [("o1", 1)]
    plan += [("pw", 1), ("pw1", 1)]
    plan += [("X0", 1), ("gC0a", 0), ("gC0b", 0), ("SA0", 1), ("gC1a", 0), ("gC1b", 0), ("St", 1)]
    plan += [(f"pC{n}", 0) for n in range(4)]
    plan += [("X1e", 1), ("X1o", 1), ("gA0a", 0), ("gA0b", 0), ("SA1", 1), ("gA1a", 0), ("gA1b", 0)]
    plan += [("Y0", 1), ("Y1e", 1), ("Y1o", 1)]
    plan += [(f"pA{n}", 0) for n in range(4)]
    plan += [("mu0", 1), ("mu1", 1), ("gB0a", 0), ("gB0b", 0), ("va0", 1), ("va1", 1)]
    plan += [("gg0", 1), ("gg1", 1), ("gB1a", 0), ("gB1b", 0)]
    plan += [(f"pB{n}", 0) for n in range(4)]
    plan += [(f"wo{n}", 0) for n in range(4)]
    plan += [(f"h2T{n}", 0) for n in range(4)] + [("rt", 1), ("cs", 1)]
    return [n for n, _ in plan], dict(plan)


FILLS, RING_OF = fill_plan()
BANK, USE, seen = {}, {}, [0, 0]
for _name in FILLS:
    _r = RING_OF[_name]
    BANK[_name] = 4 * _r + seen[_r] % 4
    USE[_name] = seen[_r] // 4
    seen[_r] += 1
FULL = {n: i + 1 for i, n in enumerate(FILLS)}


def trunk_and_experts(nc, x, norm1_g, w_in, rwkv_mu, w0, w_decay_up, a0, w_iclr_up, w_gate_up, k_k, k_a, r_k,
                      lnx_g, lnx_b, pool_w, pool_scale, w_branch, w_out, norm2_g, router_grp_w, router_grp_b,
                      router_exp_w, router_exp_b, exp_w1, exp_w3, exp_w2, final_norm_g, out):
    with ExitStack() as ctx:
        def sb(name, shape, dt=F32):
            return ctx.enter_context(nc.sbuf_tensor(name, shape, dt))

        ring = sb("ring", [P, TRUNK_SLOTS * PIECE])
        arena = sb("arena", [P, 14 * 1024])
        hT = sb("hT", [P, KD, T])
        qk = sb("qk", [P, 2, CT, T])
        va = sb("va", [P, TT, BW])
        pz = sb("pz", [P, CT, T])
        ar = sb("ar", [P, CT, TT, 2, P])
        bt = sb("bt", [P, CT, T])
        kt = sb("kt", [P, CT, T])
        vn = sb("vn", [P, TT, BW])
        bkn = sb("bkn", [P, 2, BW])
        bonus = sb("bonus", [P, CT, T])
        sig_g = sb("sig_g", [P, T])
        gm = sb("gm", [P, 2, KD, T])
        par_rows = bkn[0:64, 1, 0:P]
        par = sb("par", [P, 54])
        ident = sb("ident", [P, P])
        ones = sb("ones", [P, P])
        head_ones = sb("head_ones", [P, P])
        causal = sb("causal", [P, 4, P])
        level_mask = sb("level_mask", [P, 7, P])
        dist = sb("dist", [P, T])
        count_inv = sb("count_inv", [P, CT, 16])
        lora_up = sb("lora_up", [P, BW])
        gate_up = sb("gate_up", [P, BW])
        poolw = sb("poolw", [P, CT, P])
        router_w = sb("router_w", [P, KD, NG + NE])
        router_b = sb("router_b", [P, NG + NE])
        router_b_row = sb("router_b_row", [1, NG + NE])
        small = sb("small", [P, 64])
        slopes = sb("slopes", [P, TT, H])
        amax = sb("amax", [P, TT, H])
        asum = sb("asum", [P, TT, H])
        state = sb("state", [P, CT, DH])
        iota_slot = sb("iota_slot", [P, CAP])
        iota_e = sb("iota_e", [P, TT, NE])
        pairs_i = sb("pairs_i", [P, 1], I32)

        ps = ctx.enter_context(nc.psum_tensor("ps", [P, 8, 512], F32))

        def blk(n, m=1):
            return arena[:, n * 1024:(n + m) * 1024]

        def slot(n):
            return ring[:, n * PIECE:(n + 1) * PIECE] if n < TRUNK_SLOTS else arena[:, (n - 4) * PIECE:(n - 3) * PIECE]

        def ch(ap):
            return ap.rearrange("p (c t) -> p c t", c=CT)

        def chunks(ap):
            return ap.rearrange("p (c t) -> p c t", c=CT * TT)

        x_sb = blk(0, 2).rearrange("p (t d) -> p t d", t=TT)
        xn = blk(2, 2).rearrange("p (t d) -> p t d", t=TT)
        k_, r_, v_, dz, kprime = ch(blk(4)), ch(blk(1)), ch(blk(2)), ch(blk(3)), ch(blk(3))
        lora = blk(0)[:, 0:2 * T].rearrange("p (c t) -> p c t", c=2)
        dlora = blk(0)[:, 2 * T:4 * T].rearrange("p (c t) -> p c t", c=2)
        logw, iclr, lp, lpm, ep, en, kk, sq, tmp = (ch(blk(n)) for n in range(5, 14))
        tanh_w = bkn[0:64, 0, 0:T]
        sc = blk(0, 8).rearrange("p (n m t) -> p n m t", n=16, m=4)
        tri = blk(8, 2).rearrange("p (n t) -> p n t", n=16)
        triT = blk(10, 2).rearrange("p (n t) -> p n t", n=16)
        triA = blk(12, 2).rearrange("p (n t) -> p n t", n=16)
        xs = [blk(12)[:, 0:512], blk(13)[:, 0:512]]
        sa = [blk(12)[:, 512:1024], blk(13)[:, 512:1024]]
        y_raw, y_cen, y_sq, y_rstd = ch(blk(8)), ch(blk(9)), ch(blk(12)), ch(blk(13))
        flat_gm = gm[:, :, :, :].rearrange("p a k t -> p (a k t)")
        prob = flat_gm[:, 0:H * 384].rearrange("p (h k) -> p h k", h=H)
        probT = flat_gm[:, 3072:3072 + 2 * 384].rearrange("p (b k) -> p b k", b=2)
        scan_ones = flat_gm[:, 0:1024]
        ptmp = flat_gm[:, 3840:4096]
        pool_a, pool_b = blk(13)[:, 0:T], blk(13)[:, T:2 * T]
        gates, merged = gm[:, 0], gm[:, 1]
        y_attn, y_rwkv, y_pool = bt, kt, pz
        x2 = qk[:, :, :, :].rearrange("p a c t -> p (a c t)").rearrange("p (t d) -> p t d", t=TT)
        h2 = gm[:, 0].rearrange("p k t -> p (k t)").rearrange("p (t d) -> p t d", t=TT)
        h2n = gm[:, 1].rearrange("p k t -> p (k t)").rearrange("p (t d) -> p t d", t=TT)
        flat_ar = ar[:, :, :, :, :].rearrange("p a b c d -> p (a b c d)")
        norm2_b, final_b = flat_ar[:, 0:D], flat_ar[:, D:2 * D]
        out_sb = gm[:, 1].rearrange("p k t -> p (k t)").rearrange("p (t d) -> p t d", t=TT)
        NPOS = NE * ROUNDS + 2
        pos = blk(8)[:, 0:TT * NPOS].rearrange("p (t n) -> p t n", t=TT)
        wts = blk(8)[:, 512:512 + TT * NPOS].rearrange("p (t n) -> p t n", t=TT)
        sel = [blk(9)[:, b * 128:(b + 1) * 128].rearrange("p (t c) -> p t c", t=TT) for b in range(2)]
        selw = blk(9)[:, 256:512].rearrange("p (t b c) -> p t b c", t=TT, b=2)
        selwT = blk(9)[:, 512:768]
        xg = [blk(10)[:, b * 512:(b + 1) * 512].rearrange("p (k c) -> p k c", k=KD) for b in range(2)]
        silu = [blk(11)[:, b * 256:(b + 1) * 256] for b in range(2)]
        hid = [blk(11)[:, 512 + b * 256:768 + b * 256].rearrange("p (k c) -> p k c", k=HC) for b in range(2)]
        yT = blk(12).rearrange("p (k b c) -> p k b c", k=KD, b=2)
        yn = blk(13)
        lg = vn[:, 0, 0:TT * 36].rearrange("p (t n) -> p t n", t=TT)
        rtmp = vn[:, 1, :]

        full = ctx.enter_context(nc.semaphore("full"))
        drained = [ctx.enter_context(nc.semaphore(f"drained{b}")) for b in range(8)]
        loaded = [ctx.enter_context(nc.semaphore(f"loaded{n}")) for n in range(SLOTS)]
        SEMS = ("x_in par_in x_again pairs_ok out_ok out_done pool_chain ident_ok lora_in gateup_in pool_in "
                "rw_in rb_in ones_ok masks_ok levels_ok dist_ok misc_ok rbcast_ok n2_in nf_in bcast2_ok "
                "bcastf_ok xn_ok tanh_ok lora_ok sq_ok v_ok bonin_ok ar_ok prob_ok pool_ok ysq_ok sigg_ok "
                "merged_ok h2_ok cs_in sel_ok gathered xg_ok hid_ok yT_ok y_full swT_full yn_full swT_ok "
                "scattered const_ok ssq k_ok norm_ok logw_ok exps_ok smax_ok exp_ok x2ssq eexp_in eexp_ok "
                "h1_full silu_ok yn0_ok fssq dve kk_ok r_ok bt_ok kt_ok sel_table h3_full yn1_ok ").split()
        s = {n: ctx.enter_context(nc.semaphore(n)) for n in SEMS}

        def bank(name):
            return ps[:, BANK[name], :]

        def wait_full(eng, *names):
            for name in names:
                eng.wait_ge(full, FULL[name])

        def wait_drained(eng, *names):
            for name in names:
                eng.wait_ge(drained[BANK[name]], USE[name] + 1)

        pc, at = {}, 0
        for n, rows in PAR_ROWS:
            pc[n] = at
            at += rows

        def pcol(name, i):
            return par[:, pc[name] + i:pc[name] + i + 1]

        block = ctx.enter_context(nc.Block())

        piece_src = {
            "lora": w_in[0, :, LORA_COL:LORA_COL + 256], "rk": w_in[0, :, RK_COL:RK_COL + BW],
            "rr": w_in[0, :, R_COL:R_COL + BW], "rv": w_in[0, :, RV_COL:RV_COL + BW],
            "aq": w_in[0, :, Q_COL:Q_COL + BW], "ak": w_in[0, :, K_COL:K_COL + BW],
            "av": w_in[0, :, V_COL:V_COL + BW], "pool": w_in[0, :, POOL_COL:POOL_COL + BW],
            "wo0": w_out[0, :, 0:BW], "wo1": w_out[0, :, BW:D],
        }
        for br, b in (("A", 0), ("B", 1), ("C", 2)):
            for half in range(2):
                c0 = GATE_COL + b * D + half * BW
                piece_src[f"g{br}{half}"] = w_in[0, :, c0:c0 + BW]
            piece_src[f"p{br}"] = w_branch[0, b]
        last_fill = {"lora": "lora", "rk": "rk1", "rr": "rr1", "rv": "rv1", "aq": "aq1", "ak": "ak1", "av": "av1",
                     "pool": "pool1", "gC0": "gC0b", "gC1": "gC1b", "pC": "pC3", "gA0": "gA0b", "gA1": "gA1b",
                     "pA": "pA3", "gB0": "gB0b", "gB1": "gB1b", "pB": "pB3", "wo0": "wo1", "wo1": "wo3"}

        def piece(name):
            n = PIECES.index(name)
            cols = {"lora": 256}.get(name, D if name[0] == "p" and name != "pool" else BW)
            k = 4 if cols == D else KD
            return slot(n % TRUNK_SLOTS)[:, 0:k * cols].rearrange("p (k c) -> p k c", k=k)

        def trunk_loads(n):
            return 16 * (n // TRUNK_SLOTS + 1)

        TRUNK_USES = [len([n for n in range(len(PIECES)) if n % TRUNK_SLOTS == b]) if b < TRUNK_SLOTS else 0
                      for b in range(SLOTS)]
        SLOT_FREE = [last_fill[[p for n, p in enumerate(PIECES) if n % TRUNK_SLOTS == b][-1]]
                     if b < TRUNK_SLOTS else "Y1o" for b in range(SLOTS)]

        def expert_dma(sp, b, j, e):
            dst = slot(3 * b + j)
            src = (exp_w1, exp_w3, exp_w2)[j]
            if isinstance(e, int):
                src = src[0, e]
                k = src.shape[0] // P
                return sp.dma_start(dst.rearrange("p (k c) -> p k c", k=k), src.rearrange("(k p) c -> p k c", p=P))
            src = src[0, bass.ds(e, 1)]
            k = src.shape[1] // P
            return sp.dma_start(dst.rearrange("p (k c) -> p k c", k=k),
                                src.rearrange("o (k p) c -> p (o k) c", p=P))

        @block.sync
        def _(sp):
            sp.dma_start(x_sb, x[0].rearrange("(t p) d -> p t d", p=P)).then_inc(s["x_in"], 16)
            row = 0
            for name, src in (("norm1_g", norm1_g), ("rwkv_mu", rwkv_mu), ("w0", w0), ("a0", a0), ("k_k", k_k),
                              ("k_a", k_a), ("r_k", r_k), ("lnx_g", lnx_g), ("lnx_b", lnx_b),
                              ("pool_scale", pool_scale)):
                rows = dict(PAR_ROWS)[name]
                flat = src[0].rearrange("h d -> (h d)") if name == "r_k" else src[0]
                sp.dma_start(par_rows[row:row + rows, :], flat.rearrange("(r c) -> r c", c=P)).then_inc(s["par_in"], 16)
                row += rows
            for n, name in enumerate(PIECES):
                if n >= TRUNK_SLOTS:
                    sp.wait_ge(full, FULL[last_fill[PIECES[n - TRUNK_SLOTS]]])
                sp.dma_start(piece(name), piece_src[name].rearrange("(k p) c -> p k c", p=P)).then_inc(
                    loaded[n % TRUNK_SLOTS], 16)
                if name == "gA0":
                    sp.wait_ge(full, FULL["at5"])
                    sp.dma_start(x2, x[0].rearrange("(t p) d -> p t d", p=P)).then_inc(s["x_again"], 16)
            for b in (1, 0):
                for j in range(3):
                    n = 3 * b + j
                    sp.wait_ge(full, FULL[SLOT_FREE[n]])
                    expert_dma(sp, b, j, b).then_inc(loaded[n], 16)
            sp.wait_ge(s["pairs_ok"], 1)
            pairs = sp.value_load(pairs_i[0:1, 0:1], min_val=16, max_val=16 * ROUNDS)
            with sp.Fori(1, pairs) as i:
                for b in range(2):
                    e = sp.snap((i % 16) * 2 + b, min_val=0, max_val=NE - 1)
                    for j, sem in enumerate(("h1_full", "h3_full", "y_full")):
                        sp.wait_ge(s[sem], i * 2 + (b - 1))
                        expert_dma(sp, b, j, e).then_inc(loaded[3 * b + j], 16)
            for t in range(TT):
                sp.wait_ge(s["out_ok"], t + 1)
                sp.dma_start(out[0, t * P:(t + 1) * P, :], out_sb[:, t, :]).then_inc(s["out_done"], 16)
            sp.wait_ge(s["out_done"], 16 * TT)

        @block.gpsimd
        def _(g):
            chain = [0]

            def link(ins):
                chain[0] += 1
                ins.then_inc(s["pool_chain"], 1)
                g.wait_ge(s["pool_chain"], chain[0])

            link(nc.gpsimd.memset(ident[:], 0.0))
            nc.gpsimd.affine_select(out=ident[:], in_=ident[:], compare_op=ALU.not_equal, fill=1.0, base=0,
                                    pattern=[[-1, P]], channel_multiplier=1).then_inc(s["ident_ok"], 1)
            g.dma_start(lora_up[0:64, :], w_decay_up[0]).then_inc(s["lora_in"], 16)
            g.dma_start(lora_up[64:P, :], w_iclr_up[0]).then_inc(s["lora_in"], 16)
            g.dma_start(gate_up[:], w_gate_up[0]).then_inc(s["gateup_in"], 16)
            g.dma_start(poolw[:], pool_w[0].rearrange("g c d -> c g d")).then_inc(s["pool_in"], 16)
            g.dma_start(router_w[:, :, 0:NG], router_grp_w[0].rearrange("(k p) n -> p k n", p=P)).then_inc(s["rw_in"], 16)
            g.dma_start(router_w[:, :, NG:], router_exp_w[0].rearrange("(k p) n -> p k n", p=P)).then_inc(s["rw_in"], 16)
            g.dma_start(router_b_row[:, 0:NG], router_grp_b).then_inc(s["rb_in"], 16)
            g.dma_start(router_b_row[:, NG:], router_exp_b).then_inc(s["rb_in"], 16)
            nc.gpsimd.memset(ones[:], 1.0).then_inc(s["ones_ok"], 1)
            link(nc.gpsimd.memset(head_ones[:], 1.0))
            nc.gpsimd.affine_select(out=head_ones[:, 0:DH], in_=head_ones[:, 0:DH], compare_op=ALU.is_ge, fill=0.0,
                                    base=DH - 1, pattern=[[0, DH]], channel_multiplier=-1)
            nc.gpsimd.affine_select(out=head_ones[:, DH:P], in_=head_ones[:, DH:P], compare_op=ALU.is_ge, fill=0.0,
                                    base=-DH, pattern=[[0, DH]], channel_multiplier=1).then_inc(s["ones_ok"], 1)
            nc.gpsimd.memset(scan_ones, 1.0).then_inc(s["ones_ok"], 1)
            g.wait_ge(s["ones_ok"], 3)
            nc.gpsimd.memset(scan_ones.rearrange("p (n t) -> p n t", t=P)[:, :, 0:1], 0.0).then_inc(s["ones_ok"], 1)
            link(nc.gpsimd.memset(causal[:], 1.0))
            for m in range(4):
                nc.gpsimd.affine_select(out=causal[:, m, :], in_=causal[:, m, :], compare_op=ALU.is_ge, fill=0.0,
                                        base=-1 if m % 2 == 0 else 0, pattern=[[1, P]],
                                        channel_multiplier=-1).then_inc(s["masks_ok"], 1)
            link(nc.gpsimd.memset(level_mask[:], 0.0))
            for lev in range(7):
                b = 1 << lev
                view = level_mask[:, lev, :].rearrange("p (n c) -> p n c", c=2 * b)[:, :, 0:b]
                nb = P // (2 * b)
                link(nc.gpsimd.memset(view, 1.0))
                link(nc.gpsimd.affine_select(out=view, in_=view, compare_op=ALU.is_ge, fill=0.0, base=-b,
                                             pattern=[[-2 * b, nb], [0, b]], channel_multiplier=1))
                nc.gpsimd.affine_select(out=view, in_=view, compare_op=ALU.is_ge, fill=0.0, base=2 * b - 1,
                                        pattern=[[2 * b, nb], [0, b]], channel_multiplier=-1).then_inc(s["levels_ok"], 1)
            link(nc.gpsimd.iota(dist[:], [[-1, T]], base=P, channel_multiplier=1, allow_small_or_imprecise_dtypes=True))
            nc.gpsimd.affine_select(out=dist[:], in_=dist[:], compare_op=ALU.is_ge, fill=FAR, base=P,
                                    pattern=[[-1, T]], channel_multiplier=1).then_inc(s["dist_ok"], 1)
            for h in range(H):
                nc.gpsimd.memset(slopes[:, :, h:h + 1], -(2.0 ** -(h + 1))).then_inc(s["misc_ok"], 1)
            nc.gpsimd.iota(iota_slot[:], [[1, CAP]], base=0, channel_multiplier=0,
                           allow_small_or_imprecise_dtypes=True).then_inc(s["misc_ok"], 1)
            nc.gpsimd.iota(iota_e[:], [[0, TT], [1, NE]], base=0, channel_multiplier=0,
                           allow_small_or_imprecise_dtypes=True).then_inc(s["misc_ok"], 1)
            link(nc.gpsimd.iota(count_inv[:], [[0, CT], [1, 16]], base=1, channel_multiplier=0,
                                allow_small_or_imprecise_dtypes=True))
            for i in range(CT):
                nc.gpsimd.tensor_scalar(count_inv[:, i, :], count_inv[:, i, :], float(2 << i), None,
                                        ALU.min).then_inc(s["misc_ok"], 1)
            g.wait_ge(s["rb_in"], 32)
            nc.gpsimd.partition_broadcast(router_b[:], router_b_row[:]).then_inc(s["rbcast_ok"], 1)
            g.wait_ge(full, FULL["Y1o"])
            g.dma_start(norm2_b[0:1, :], norm2_g).then_inc(s["n2_in"], 16)
            g.dma_start(final_b[0:1, :], final_norm_g.rearrange("(o d) -> o d", o=1)).then_inc(s["nf_in"], 16)
            g.wait_ge(s["n2_in"], 16)
            nc.gpsimd.partition_broadcast(norm2_b, norm2_b[0:1, :]).then_inc(s["bcast2_ok"], 1)
            g.wait_ge(s["nf_in"], 16)
            nc.gpsimd.partition_broadcast(final_b, final_b[0:1, :]).then_inc(s["bcastf_ok"], 1)

        @block.tensor
        def _(pe):
            order = iter(FILLS)

            def open_fill(name):
                if USE[name]:
                    pe.wait_ge(drained[BANK[name]], USE[name])
                return bank(name)

            def close_fill(name, ins):
                assert next(order) == name, name
                ins.then_inc(full, 1)

            def need_piece(name):
                n = PIECES.index(name)
                pe.wait_ge(loaded[n % TRUNK_SLOTS], trunk_loads(n))
                return piece(name)

            def need(sem, n):
                pe.wait_ge(s[sem], n)

            def project(fill, w, tiles, c0, rhs, nk):
                b = open_fill(fill)
                for i in range(tiles):
                    for k in range(nk):
                        mm = pe.matmul(b[:, i * T:(i + 1) * T], w[:, k, (c0 + i) * P:(c0 + i + 1) * P], rhs[:, k, :],
                                       start=(k == 0), stop=(k == nk - 1))
                close_fill(fill, mm)

            need("ident_ok", 1)
            need("par_in", 160)
            b = open_fill("par")
            close_fill("par", pe.transpose(b[:, 0:54], par_rows[0:54, :], ident[0:54, 0:54]))
            for n in range(4):
                b = open_fill(f"hT{n}")
                for i in range(2):
                    for t in range(TT):
                        need("xn_ok", t + 1)
                        k = 2 * n + i
                        mm = pe.transpose(b[:, i * T + t * P:i * T + (t + 1) * P], xn[:, t, k * P:(k + 1) * P], ident[:])
                close_fill(f"hT{n}", mm)
            wait_drained(pe, "hT0", "hT1", "hT2", "hT3")
            project("lora", need_piece("lora"), 2, 0, hT, KD)
            w = need_piece("rk")
            for i in range(2):
                project(f"rk{i}", w, 2, 2 * i, hT, KD)
            need("lora_in", 32)
            need("tanh_ok", 1)
            for i in range(2):
                b = open_fill(f"u{i}")
                for c in range(2):
                    mm = pe.matmul(b[:, c * T:(c + 1) * T], lora_up[0:64, (2 * i + c) * P:(2 * i + c + 1) * P], tanh_w,
                                   start=True, stop=True)
                close_fill(f"u{i}", mm)
            need("lora_ok", 2)
            for i in range(2):
                b = open_fill(f"a{i}")
                for c in range(2):
                    mm = pe.matmul(b[:, c * T:(c + 1) * T], lora_up[64:P, (2 * i + c) * P:(2 * i + c + 1) * P],
                                   lora[64:P, 0, :], start=True, stop=True)
                close_fill(f"a{i}", mm)
            for name in ("rr", "rv"):
                w = need_piece(name)
                for i in range(2):
                    project(f"{name}{i}", w, 2, 2 * i, hT, KD)
            need("ones_ok", 2)
            need("sq_ok", 4)
            for i in range(2):
                b = open_fill(f"ss{i}")
                close_fill(f"ss{i}", pe.matmul(b, head_ones[:], blk(12)[:, i * 512:(i + 1) * 512], start=True, stop=True))
            for name in ("aq", "ak"):
                w = need_piece(name)
                for i in range(2):
                    project(f"{name}{i}", w, 2, 2 * i, hT, KD)
            w = need_piece("av")
            for t in range(TT):
                b = open_fill(f"av{t}")
                for k in range(KD):
                    mm = pe.matmul(b, hT[:, k, t * P:(t + 1) * P], w[:, k, :], start=(k == 0), stop=(k == KD - 1))
                close_fill(f"av{t}", mm)
            w = need_piece("pool")
            for i in range(2):
                project(f"pool{i}", w, 2, 2 * i, hT, KD)
            need("v_ok", 4)
            for c in range(TT):
                b = open_fill(f"vn{c}")
                for t in range(CT):
                    mm = pe.transpose(b[:, t * P:(t + 1) * P], v_[:, t, c * P:(c + 1) * P], ident[:])
                close_fill(f"vn{c}", mm)
            for name, src, sem in (("bn", bt, "bt_ok"), ("kn", kt, "kt_ok")):
                need(sem, 1)
                b = open_fill(name)
                for t in range(CT):
                    mm = pe.transpose(b[:, t * P:(t + 1) * P], src[:, t, 0:P], ident[:])
                close_fill(name, mm)
            need("bonin_ok", 4)
            for i in range(2):
                b = open_fill(f"bon{i}")
                close_fill(f"bon{i}", pe.matmul(b, head_ones[:], blk(13)[:, i * 512:(i + 1) * 512], start=True, stop=True))
            need("ar_ok", 2)
            for n in range(16):
                c, h = divmod(n, H)
                rows = slice(64 * (h % 2), 64 * (h % 2) + 64)
                b = open_fill(f"sc{n}")
                both = ar[rows, h // 2, c, :, :].rearrange("p m t -> p (m t)")
                for m, left in enumerate((bt, kt)):
                    mm = pe.matmul(b[:, m * T:(m + 1) * T], left[rows, h // 2, c * P:(c + 1) * P], both,
                                   start=True, stop=True)
                close_fill(f"sc{n}", mm)
            wait_drained(pe, "aq0", "aq1", "ak0", "ak1")
            for n in range(6):
                b = open_fill(f"at{n}")
                for i, h in enumerate(attn_heads(n)):
                    rows = slice(64 * (h % 2), 64 * (h % 2) + 64)
                    if n < 4:
                        mm = pe.matmul(b[:, i * T:(i + 1) * T], qk[rows, 0, h // 2, P:T], qk[rows, 1, h // 2, :],
                                       start=True, stop=True)
                    else:
                        mm = pe.matmul(b[:, i * P:(i + 1) * P], qk[rows, 0, h // 2, 0:P], qk[rows, 1, h // 2, 0:P],
                                       start=True, stop=True)
                close_fill(f"at{n}", mm)
            for g in range(4):
                b = open_fill(f"L{g}")
                for i in range(4):
                    n = 4 * g + i
                    wait_drained(pe, f"sc{n}")
                    mm = pe.transpose(b[:, i * P:(i + 1) * P], sc[:, n, 0, :], ident[:])
                close_fill(f"L{g}", mm)

            def transpose_tri(name, g, source):
                b = open_fill(name)
                wait_drained(pe, source)
                for i in range(4):
                    mm = pe.transpose(b[:, i * P:(i + 1) * P], tri[:, 4 * g + i, :], ident[:])
                close_fill(name, mm)

            for g in range(4):
                transpose_tri(f"G1_{g}", g, f"L{g}")
            for size in LEVELS:
                for g in range(4):
                    b = open_fill(f"A{size}_{g}")
                    for i in range(4):
                        n = 4 * g + i
                        mm = pe.matmul(b[:, i * P:(i + 1) * P], sc[:, n, 0, :], tri[:, n, :], start=True, stop=True)
                    close_fill(f"A{size}_{g}", mm)
                for g in range(4):
                    b = open_fill(f"T{size}_{g}")
                    wait_drained(pe, f"G{size // 2}_{g}", f"A{size}_{g}")
                    for i in range(4):
                        n = 4 * g + i
                        mm = pe.matmul(b[:, i * P:(i + 1) * P], triT[:, n, :], triA[:, n, :], start=True, stop=True)
                    close_fill(f"T{size}_{g}", mm)
                for g in range(4):
                    transpose_tri(f"G{size}_{g}", g, f"T{size}_{g}")

            def pT(h):
                b = open_fill(f"pt{h}")
                need("prob_ok", 2)
                for j in range(3):
                    mm = pe.transpose(b[:, j * P:(j + 1) * P], prob[:, h, j * P:(j + 1) * P], ident[:])
                close_fill(f"pt{h}", mm)

            def pv(h):
                b = bank(f"o{h // 4}")
                if h % 4 == 0:
                    open_fill(f"o{h // 4}")
                wait_drained(pe, f"pt{h}")
                orow = slice(64 * (h % 2), 64 * (h % 2) + 64)
                c0 = (h // 2 % 2) * T
                head = slice(h * DH, (h + 1) * DH)
                if h == 0:
                    wait_drained(pe, "av0", "av1")
                pe.matmul(b[orow, c0:c0 + P], va[:, 0, head], probT[:, h % 2, 0:P], start=True, stop=True)
                for j in range(2):
                    mm = pe.matmul(b[orow, c0 + P:c0 + T], va[:, j, head], probT[:, h % 2, (1 + j) * P:(2 + j) * P],
                                   start=(j == 0), stop=(j == 1))
                return mm

            pT(0)
            pT(1)
            for h in range(H):
                mm = pv(h)
                if h % 4 == 3:
                    close_fill(f"o{h // 4}", mm)
                if h + 2 < H:
                    pT(h + 2)
            need("pool_in", 16)
            need("pool_ok", 4)
            for i, name in enumerate(("pw", "pw1")):
                b = open_fill(name)
                for c in range(2):
                    mm = pe.matmul(b[:, c * T:(c + 1) * T], poolw[:, 2 * i + c, :], pz[:, 2 * i + c, :],
                                   start=True, stop=True)
                close_fill(name, mm)

            def heads_out(b, h):
                return b[:, h * DH:(h + 1) * DH]

            wait_drained(pe, "vn0", "vn1")
            b = open_fill("X0")
            for h in range(H):
                mm = pe.matmul(heads_out(b, h), sc[:, h, 2, :], vn[:, 0, h * DH:(h + 1) * DH], start=True, stop=True)
            close_fill("X0", mm)

            def gate_half(br, half):
                w = need_piece(f"g{br}{half}")
                for i, part in enumerate("ab"):
                    project(f"g{br}{half}{part}", w, 2, 2 * i, hT, KD)

            def branch(br, y):
                w = need_piece(f"p{br}")
                for n in range(4):
                    project(f"p{br}{n}", w, 2, 2 * n, y, CT)

            gate_half("C", 0)
            wait_drained(pe, "X0", "G64_0", "G64_1", "G64_2", "G64_3")
            b = open_fill("SA0")
            for h in range(H):
                mm = pe.matmul(heads_out(b, h), triT[:, h, :], xs[0][:, h * DH:(h + 1) * DH], start=True, stop=True)
            close_fill("SA0", mm)
            gate_half("C", 1)
            wait_drained(pe, "SA0", "bn", "kn")
            b = open_fill("St")
            for h in range(H):
                o = b[64 * (h % 2):64 * (h % 2) + 64, (h // 2) * DH:(h // 2 + 1) * DH]
                head = slice(h * DH, (h + 1) * DH)
                pe.matmul(o, bkn[:, 0, head], sa[0][:, head], start=True, stop=False)
                mm = pe.matmul(o, bkn[:, 1, head], vn[:, 0, head], start=False, stop=True)
            close_fill("St", mm)
            wait_drained(pe, "pw", "pw1")
            branch("C", y_pool)
            wait_drained(pe, "St")
            for parity, name in enumerate(("X1e", "X1o")):
                b = open_fill(name)
                rows = slice(64 * parity, 64 * parity + 64)
                for i in range(4):
                    h = 2 * i + parity
                    pe.matmul(b[:, i * DH:(i + 1) * DH], sc[:, H + h, 2, :], vn[:, 1, h * DH:(h + 1) * DH],
                              start=True, stop=False)
                    mm = pe.matmul(b[:, i * DH:(i + 1) * DH], ar[rows, i, 1, 0, :], state[rows, i, :],
                                   start=False, stop=True)
                close_fill(name, mm)
            gate_half("A", 0)
            wait_drained(pe, "X1e", "X1o")
            b = open_fill("SA1")
            for h in range(H):
                mm = pe.matmul(heads_out(b, h), triT[:, H + h, :], xs[1][:, h * DH:(h + 1) * DH], start=True, stop=True)
            close_fill("SA1", mm)
            gate_half("A", 1)
            wait_drained(pe, "SA1")
            b = open_fill("Y0")
            for h in range(H):
                o = b[64 * (h % 2):64 * (h % 2) + 64, (h // 2) * P:(h // 2 + 1) * P]
                head = slice(h * DH, (h + 1) * DH)
                pe.matmul(o, sa[0][:, head], sc[:, h, 1, :], start=True, stop=False)
                mm = pe.matmul(o, vn[:, 0, head], sc[:, h, 3, :], start=False, stop=True)
            close_fill("Y0", mm)
            for parity, name in enumerate(("Y1e", "Y1o")):
                b = open_fill(name)
                rows = slice(64 * parity, 64 * parity + 64)
                for i in range(4):
                    h = 2 * i + parity
                    o = b[rows, i * P:(i + 1) * P]
                    head = slice(h * DH, (h + 1) * DH)
                    pe.matmul(o, sa[1][:, head], sc[:, H + h, 1, :], start=True, stop=False)
                    pe.matmul(o, vn[:, 1, head], sc[:, H + h, 3, :], start=False, stop=False)
                    mm = pe.matmul(o, state[rows, i, :], ar[rows, i, 1, 1, :], start=False, stop=True)
                close_fill(name, mm)
            wait_drained(pe, "o0", "o1")
            branch("A", y_attn)
            wait_drained(pe, "Y0", "Y1e", "Y1o")
            for i in range(2):
                b = open_fill(f"mu{i}")
                close_fill(f"mu{i}", pe.matmul(b, head_ones[:], blk(8)[:, i * 512:(i + 1) * 512], start=True, stop=True))
            gate_half("B", 0)
            need("ysq_ok", 1)
            for i in range(2):
                b = open_fill(f"va{i}")
                close_fill(f"va{i}", pe.matmul(b, head_ones[:], blk(12)[:, i * 512:(i + 1) * 512], start=True, stop=True))
            need("gateup_in", 16)
            need("sigg_ok", 1)
            for i in range(2):
                b = open_fill(f"gg{i}")
                for c in range(2):
                    mm = pe.matmul(b[:, c * T:(c + 1) * T], gate_up[:, (2 * i + c) * P:(2 * i + c + 1) * P], sig_g[:],
                                   start=True, stop=True)
                close_fill(f"gg{i}", mm)
            gate_half("B", 1)
            wait_drained(pe, "gg0", "gg1")
            branch("B", y_rwkv)
            need("merged_ok", 8)
            for half in range(2):
                w = need_piece(f"wo{half}")
                for t in range(TT):
                    name = f"wo{2 * half + t}"
                    b = open_fill(name)
                    for k in range(KD):
                        mm = pe.matmul(b, merged[:, k, t * P:(t + 1) * P], w[:, k, :], start=(k == 0), stop=(k == KD - 1))
                    close_fill(name, mm)
            for n in range(4):
                b = open_fill(f"h2T{n}")
                for i in range(2):
                    for t in range(TT):
                        need("h2_ok", t + 1)
                        k = 2 * n + i
                        mm = pe.transpose(b[:, i * T + t * P:i * T + (t + 1) * P], h2[:, t, k * P:(k + 1) * P], ident[:])
                close_fill(f"h2T{n}", mm)
            wait_drained(pe, "h2T0", "h2T1", "h2T2", "h2T3")
            need("rw_in", 32)
            b = open_fill("rt")
            for t in range(TT):
                for k in range(KD):
                    mm = pe.matmul(b[:, t * 36:(t + 1) * 36], hT[:, k, t * P:(t + 1) * P], router_w[:, k, :],
                                   start=(k == 0), stop=(k == KD - 1))
            close_fill("rt", mm)
            for t in range(TT):
                for half in range(2):
                    mm = pe.matmul(ps[:, 2 * t + half, :], ident[:], x2[:, t, half * 512:(half + 1) * 512],
                                   start=True, stop=False, skip_group_check=True)
            need("cs_in", 1)
            b = open_fill("cs")
            assigned = rtmp[:, 0:TT * NE].rearrange("p (t n) -> p t n", t=TT)
            pe.matmul(b[:, 0:32], causal[:, 0, :], assigned[:, 0, :], start=True, stop=True)
            pe.matmul(b[:, 32:64], causal[:, 0, :], assigned[:, 1, :], start=True, stop=False)
            pe.matmul(b[:, 32:64], ones[:], assigned[:, 0, :], start=False, stop=True)
            pe.matmul(b[:, 64:96], ones[:], assigned[:, 0, :], start=True, stop=False)
            mm = pe.matmul(b[:, 64:96], ones[:], assigned[:, 1, :], start=False, stop=True)
            close_fill("cs", mm)
            assert next(order, None) is None

            XG, H1, YB, H3 = 4, 5, 6, 7

            def gather(b, count):
                pe.wait_ge(s["sel_ok"], count)
                for k in range(KD):
                    for t in range(TT):
                        mm = pe.matmul(ps[:, XG, k * CAP:(k + 1) * CAP], h2[:, t, k * P:(k + 1) * P], sel[b][:, t, :],
                                       start=(t == 0), stop=(t == TT - 1))
                mm.then_inc(s["gathered"], 1)

            def w_slot(b, j, k):
                return slot(3 * b + j).rearrange("p (k c) -> p k c", k=k)

            pe.wait_ge(s["pairs_ok"], 1)
            pairs = pe.value_load(pairs_i[0:1, 0:1], min_val=16, max_val=16 * ROUNDS)
            gather(0, 1)
            with pe.Fori(0, pairs) as i:
                for b in range(2):
                    n = i * 2 + b
                    pe.wait_ge(s["xg_ok"], n + 1)
                    for j, sem in enumerate(("h1_full", "h3_full")):
                        base = TRUNK_USES[3 * b + j]
                        pe.wait_ge(loaded[3 * b + j], i * 16 + 16 * (base + 1))
                        w = w_slot(b, j, KD)
                        for m in range(HC):
                            o = ps[:, (H1, H3)[j], m * CAP:(m + 1) * CAP]
                            for k in range(KD):
                                mm = pe.matmul(o, w[:, k, m * P:(m + 1) * P], xg[b][:, k, :],
                                               start=(k == 0), stop=(k == KD - 1))
                        mm.then_inc(s[sem], 1)
                    gather(1 - b, n + 2)
                    pe.wait_ge(loaded[3 * b + 2], i * 16 + 16 * (TRUNK_USES[3 * b + 2] + 1))
                    pe.wait_ge(s["hid_ok"], n + 1)
                    if b == 1:
                        pe.wait_ge(s["yT_ok"], n)
                    w = w_slot(b, 2, HC)
                    for m in range(KD):
                        for k in range(HC):
                            mm = pe.matmul(ps[:, YB, m * CAP:(m + 1) * CAP], w[:, k, m * P:(m + 1) * P], hid[b][:, k, :],
                                           start=(k == 0), stop=(k == HC - 1))
                    mm.then_inc(s["y_full"], 1)
                pe.wait_ge(s["xg_ok"], i * 2 + 3)
                for t in range(TT):
                    mm = pe.transpose(ps[:, XG, t * P:(t + 1) * P], selw[:, t, :, :].rearrange("p b c -> p (b c)"),
                                      ident[:])
                mm.then_inc(s["swT_full"], 1)
                pe.wait_ge(s["yT_ok"], i * 2 + 2)
                for half, dst in enumerate((H3, H1)):
                    for m in range(4):
                        mm = pe.transpose(ps[:, dst, m * P:(m + 1) * P],
                                          yT[:, 4 * half + m, :, :].rearrange("p b c -> p (b c)"), ident[:])
                    mm.then_inc(s["yn_full"], 1)
                pe.wait_ge(s["swT_ok"], i + 1)
                for half, sem in enumerate(("yn0_ok", "yn1_ok")):
                    pe.wait_ge(s[sem], i + 1)
                    for t in range(TT):
                        mm = pe.matmul(ps[:, 2 * t + half, :], selwT[:, t * P:(t + 1) * P],
                                       yn[:, half * 512:(half + 1) * 512], start=False, stop=False,
                                       skip_group_check=True)
                mm.then_inc(s["scattered"], 1)

        @block.scalar
        def _(a):
            def free(ins, name):
                ins.then_inc(drained[BANK[name]], 1)

            def need(sem, n):
                a.wait_ge(s[sem], n)

            def move(dst, name, cols=512):
                wait_full(a, name)
                free(a.activation(dst, bank(name)[:, 0:cols], ACT.Copy), name)

            need("x_in", 16)
            need("const_ok", 1)
            for t in range(TT):
                a.activation(blk(4 + t), x_sb[:, t, :], ACT.Square, accum_out=small[:, t:t + 1]).then_inc(s["ssq"], 1)
            need("ssq", 2)
            a.activation(small[:, 2:4], small[:, 0:2], ACT.Sqrt, scale=1.0 / D, bias=small[:, 4:5]).then_inc(s["ssq"], 1)
            wait_drained(a, "par")
            for n in (0, 2):
                wait_full(a, f"hT{n}")
                for i in range(2):
                    k = 2 * n + i
                    ins = a.activation(hT[:, k, :], bank(f"hT{n}")[:, i * T:(i + 1) * T], ACT.Copy, scale=pcol("norm1_g", k))
                free(ins, f"hT{n}")
            for n in range(4):
                wait_full(a, f"hT{n}")
            move(blk(0)[:, 0:512], "lora")
            for i in range(2):
                move(blk(4)[:, i * 512:(i + 1) * 512], f"rk{i}")
            need("lora_ok", 2)
            a.activation(tanh_w, lora[0:64, 0, :], ACT.Tanh).then_inc(s["tanh_ok"], 1)
            a.activation(sig_g[:], lora[:, 1, :], ACT.Sigmoid).then_inc(s["sigg_ok"], 1)
            for i in range(2):
                wait_full(a, f"u{i}")
                for c in range(2):
                    ct = 2 * i + c
                    ins = a.activation(logw[:, ct, :], bank(f"u{i}")[:, c * T:(c + 1) * T], ACT.Sigmoid, bias=pcol("w0", ct))
                free(ins, f"u{i}")
            for i in range(2):
                wait_full(a, f"a{i}")
                for c in range(2):
                    ct = 2 * i + c
                    ins = a.activation(iclr[:, ct, :], bank(f"a{i}")[:, c * T:(c + 1) * T], ACT.Sigmoid, bias=pcol("a0", ct))
                free(ins, f"a{i}")
            need("k_ok", 4)
            for ct in range(CT):
                a.activation(sq[:, ct, :], k_[:, ct, :], ACT.Square, scale=pcol("k_k", ct)).then_inc(s["sq_ok"], 1)
            for i in range(2):
                move(blk(1)[:, i * 512:(i + 1) * 512], f"rr{i}")
            for i in range(2):
                move(blk(2)[:, i * 512:(i + 1) * 512], f"rv{i}")
            wait_drained(a, "ss0", "ss1")
            a.activation(blk(12), blk(12), ACT.Sqrt).then_inc(s["norm_ok"], 1)
            need("logw_ok", 2)
            a.activation(blk(9), blk(8), ACT.Exp).then_inc(s["exps_ok"], 1)
            a.activation(blk(10), blk(8), ACT.Exp, scale=-1.0).then_inc(s["exps_ok"], 1)
            a.activation(blk(7), blk(7), ACT.Exp).then_inc(s["exps_ok"], 1)
            a.activation(small[:, 8:12], small[:, 8:12], ACT.Exp).then_inc(s["exps_ok"], 1)
            for i in range(2):
                move(qk[:, 0, 2 * i:2 * i + 2, :].rearrange("p c t -> p (c t)"), f"aq{i}")
            for i in range(2):
                move(qk[:, 1, 2 * i:2 * i + 2, :].rearrange("p c t -> p (c t)"), f"ak{i}")
            for t in range(TT):
                move(va[:, t, :], f"av{t}")
            for i in range(2):
                move(pz[:, 2 * i:2 * i + 2, :].rearrange("p c t -> p (c t)"), f"pool{i}")
            for c in range(2):
                move(vn[:, c, :], f"vn{c}")
            move(bkn[:, 0, :], "bn")
            move(bkn[:, 1, :], "kn")
            need("smax_ok", 3)
            for c in range(TT):
                for h in range(H):
                    p = prob[:, h, 0:P] if c == 0 else prob[:, h, P:3 * P]
                    ins = a.activation(p, p, ACT.Exp, scale=2.0 ** -(h + 1), bias=amax[:, c, h:h + 1],
                                       accum_out=asum[:, c, h:h + 1])
            ins.then_inc(s["exp_ok"], 1)

            for g in range(4):
                wait_full(a, f"G1_{g}")
                free(a.activation(blk(10 + g // 2)[:, (g % 2) * 512:(g % 2 + 1) * 512], bank(f"G1_{g}"), ACT.Copy),
                     f"G1_{g}")
            for size in LEVELS:
                for g in range(4):
                    wait_full(a, f"A{size}_{g}")
                    free(a.activation(blk(12 + g // 2)[:, (g % 2) * 512:(g % 2 + 1) * 512], bank(f"A{size}_{g}"), ACT.Copy),
                         f"A{size}_{g}")
                for g in range(4):
                    wait_full(a, f"G{size}_{g}")
                    free(a.activation(blk(10 + g // 2)[:, (g % 2) * 512:(g % 2 + 1) * 512], bank(f"G{size}_{g}"), ACT.Copy),
                         f"G{size}_{g}")
            need("prob_ok", 2)
            for h in range(H):
                wait_full(a, f"pt{h}")
                free(a.activation(probT[:, h % 2, :], bank(f"pt{h}")[:, 0:384], ACT.Copy), f"pt{h}")
            for i in range(2):
                move(bt[:, 2 * i:2 * i + 2, :].rearrange("p c t -> p (c t)"), f"o{i}")
            for i, name in enumerate(("pw", "pw1")):
                wait_full(a, "pw1")
                for c in range(2):
                    ct = 2 * i + c
                    ins = a.activation(pz[:, ct, :], bank(name)[:, c * T:(c + 1) * T], ACT.Copy, scale=pcol("pool_scale", ct))
                free(ins, name)
            move(xs[0], "X0")

            def gate(br, half):
                for i, part in enumerate("ab"):
                    name = f"g{br}{half}{part}"
                    wait_full(a, name)
                    k = 4 * half + 2 * i
                    free(a.activation(gates[:, k:k + 2, :].rearrange("p k t -> p (k t)"), bank(name), ACT.Sigmoid), name)

            gate("C", 0)
            move(sa[0], "SA0")
            gate("C", 1)
            for parity, name in enumerate(("X1e", "X1o")):
                wait_full(a, name)
                free(a.activation(xs[1].rearrange("p (i q d) -> p i q d", q=2, d=DH)[:, :, parity, :],
                                  bank(name)[:, 0:256].rearrange("p (i d) -> p i d", d=DH), ACT.Copy), name)
            wait_drained(a, "pC0", "pC1", "pC2", "pC3")
            gate("A", 0)
            move(sa[1], "SA1")
            gate("A", 1)
            wait_full(a, "Y0")
            free(a.activation(y_raw[:, :, 0:P], bank("Y0").rearrange("p (c t) -> p c t", c=CT), ACT.Copy), "Y0")
            for parity, name in enumerate(("Y1e", "Y1o")):
                rows = slice(64 * parity, 64 * parity + 64)
                wait_full(a, name)
                free(a.activation(y_raw[rows, :, P:T], ps[rows, BANK[name], :].rearrange("p (c t) -> p c t", c=CT), ACT.Copy),
                     name)
            need("merged_ok", 4)
            gate("B", 0)
            wait_drained(a, "mu0", "mu1")
            a.activation(blk(12), blk(9), ACT.Square).then_inc(s["ysq_ok"], 1)
            for i in range(2):
                wait_full(a, f"va{i}")
                free(a.activation(blk(13)[:, i * 512:(i + 1) * 512], bank(f"va{i}"), ACT.Sqrt, scale=1.0 / DH,
                                  bias=small[:, 5:6]), f"va{i}")
            gate("B", 1)
            wait_drained(a, "wo0", "wo1", "wo2", "wo3")
            for t in range(TT):
                a.activation(h2n[:, t, :], x2[:, t, :], ACT.Square, accum_out=small[:, 12 + t:13 + t]).then_inc(s["x2ssq"], 1)
            need("x2ssq", 2)
            a.activation(small[:, 14:16], small[:, 12:14], ACT.Sqrt, scale=1.0 / D, bias=small[:, 4:5]).then_inc(s["x2ssq"], 1)
            for n in range(4):
                wait_full(a, f"h2T{n}")
                free(a.activation(hT[:, 2 * n:2 * n + 2, :].rearrange("p k t -> p (k t)"), bank(f"h2T{n}"), ACT.Copy),
                     f"h2T{n}")
            need("eexp_in", 1)
            a.activation(small[:, 32:40], small[:, 32:40], ACT.Exp).then_inc(s["eexp_ok"], 1)
            need("eexp_in", 2)
            a.activation(small[:, 24:26], small[:, 24:26], ACT.Exp).then_inc(s["eexp_ok"], 1)
            need("pairs_ok", 1)
            pairs = a.value_load(pairs_i[0:1, 0:1], min_val=16, max_val=16 * ROUNDS)

            def move_gathered(b, count):
                a.wait_ge(s["gathered"], count)
                a.activation(xg[b].rearrange("p k c -> p (k c)"), ps[:, 4, :], ACT.Copy).then_inc(s["xg_ok"], 1)

            move_gathered(0, 1)
            with a.Fori(0, pairs) as i:
                for b in range(2):
                    n = i * 2 + b
                    a.wait_ge(s["h1_full"], n + 1)
                    a.activation(silu[b], ps[:, 5, 0:256], ACT.Silu).then_inc(s["silu_ok"], 1)
                    move_gathered(1 - b, n + 2)
                    a.wait_ge(s["y_full"], n + 1)
                    a.activation(yT[:, :, b, :], ps[:, 6, :].rearrange("p (k c) -> p k c", c=CAP), ACT.Copy).then_inc(
                        s["yT_ok"], 1)
                a.wait_ge(s["yn_full"], i * 2 + 1)
                a.activation(yn[:, 0:512], ps[:, 7, :], ACT.Copy).then_inc(s["yn0_ok"], 1)
            a.wait_ge(s["scattered"], pairs)
            for t in range(TT):
                a.activation(h2[:, t, :], ps[:, 2 * t:2 * t + 2, :].rearrange("p b c -> p (b c)"), ACT.Square,
                             accum_out=small[:, 16 + t:17 + t]).then_inc(s["fssq"], 1)
            need("fssq", 2)
            a.activation(small[:, 18:20], small[:, 16:18], ACT.Sqrt, scale=1.0 / D, bias=small[:, 4:5]).then_inc(s["fssq"], 1)

        @block.vector
        def _(v):
            chain = [0]

            def link(ins):
                chain[0] += 1
                ins.then_inc(s["dve"], 1)
                v.wait_ge(s["dve"], chain[0])

            def free(ins, name):
                ins.then_inc(drained[BANK[name]], 1)

            def need(sem, n):
                v.wait_ge(s[sem], n)

            v.memset(small[:, 4:5], RMS_EPS)
            v.memset(small[:, 5:6], LNX_EPS).then_inc(s["const_ok"], 1)
            wait_full(v, "par")
            free(v.tensor_copy(par[:], bank("par")[:, 0:54]), "par")
            wait_drained(v, "par")
            link(v.tensor_scalar(small[:, 20:24], par[:, pc["k_a"]:pc["k_a"] + 4], -1.0, 1.0, ALU.mult, ALU.add))
            need("x_in", 16)
            need("ssq", 3)
            link(v.reciprocal(small[:, 6:8], small[:, 2:4]))
            for t in range(TT):
                v.tensor_scalar(xn[:, t, :], x_sb[:, t, :], small[:, 6 + t:7 + t], None, ALU.mult).then_inc(s["xn_ok"], 1)
            for n in (1, 3):
                wait_full(v, f"hT{n}")
                for i in range(2):
                    k = 2 * n + i
                    ins = v.tensor_scalar(hT[:, k, :], bank(f"hT{n}")[:, i * T:(i + 1) * T], pcol("norm1_g", k), None, ALU.mult)
                free(ins, f"hT{n}")

            def token_shift(z, d, tiles, mu0, sem):
                v.tensor_tensor(d[:, :, 1:T], z[:, :, 0:T - 1], z[:, :, 1:T], ALU.subtract)
                link(v.tensor_scalar(d[:, :, 0:1], z[:, :, 0:1], -1.0, None, ALU.mult))
                for c in range(tiles):
                    v.scalar_tensor_tensor(out=z[:, c, :], in0=d[:, c, :], scalar=pcol("rwkv_mu", mu0 + c),
                                           in1=z[:, c, :], op0=ALU.mult, op1=ALU.add).then_inc(s[sem], 1)

            wait_drained(v, "lora")
            token_shift(lora, dlora, 2, 12, "lora_ok")
            wait_drained(v, "rk0")
            wait_drained(v, "rk1")
            token_shift(k_, dz, CT, 4, "k_ok")
            wait_drained(v, "u0")
            wait_drained(v, "u1")
            need("ones_ok", 4)
            link(v.tensor_scalar(blk(5), blk(5), -DECAY_SCALE, None, ALU.mult))
            link(v.tensor_tensor_scan(blk(7), scan_ones, blk(5), 0.0, ALU.mult, ALU.add))
            lp8 = chunks(blk(7))
            v.tensor_tensor(chunks(blk(8)), lp8, lp8[:, :, 63:64].to_broadcast([P, 8, P]), ALU.subtract).then_inc(
                s["logw_ok"], 1)
            need("logw_ok", 1)
            v4 = lambda ap: ap.rearrange("p (c k t) -> p c k t", c=CT, k=TT)
            link(v.tensor_tensor(small[:, 8:12], v4(blk(8))[:, :, 0, P - 1], v4(blk(7))[:, :, 1, 63], ALU.add))
            v.tensor_tensor(blk(7), blk(8), blk(5), ALU.subtract).then_inc(s["logw_ok"], 1)
            need("k_ok", 4)
            for ct in range(CT):
                v.tensor_scalar(kk[:, ct, :], k_[:, ct, :], pcol("k_k", ct), None, ALU.mult).then_inc(s["kk_ok"], 1)
            wait_drained(v, "rr0")
            wait_drained(v, "rr1")
            token_shift(r_, dz, CT, 0, "r_ok")
            wait_drained(v, "rv0")
            wait_drained(v, "rv1")
            need("r_ok", 4)
            token_shift(v_, dz, CT, 8, "v_ok")
            for i in range(2):
                wait_full(v, f"ss{i}")
                if i == 0:
                    wait_full(v, "ss1")
                ins = v.tensor_scalar(blk(12)[:, i * 512:(i + 1) * 512], bank(f"ss{i}"), 1e-24, None, ALU.max)
                free(ins, f"ss{i}")
            need("norm_ok", 1)
            link(v.reciprocal(blk(12), blk(12)))
            need("kk_ok", 4)
            link(v.tensor_tensor(blk(11), blk(11), blk(12), ALU.mult))
            need("exps_ok", 4)
            ar8 = ar[:, :, :, :, :].rearrange("p c k m t -> p (c k) m t")
            v.scalar_tensor_tensor(out=ar8[:, :, 0, :], in0=chunks(blk(11)), scalar=-1.0, in1=chunks(blk(7)),
                                   op0=ALU.mult, op1=ALU.mult).then_inc(s["ar_ok"], 1)
            v.tensor_tensor(ar8[:, :, 1, :], chunks(blk(1)), chunks(blk(9)), ALU.mult).then_inc(s["ar_ok"], 1)
            wait_drained(v, "a0")
            wait_drained(v, "a1")
            link(v.tensor_tensor(blk(13), blk(11), blk(6), ALU.mult))
            flat = lambda t3: t3[:, :, :].rearrange("p c t -> p (c t)")
            v.tensor_tensor(flat(bt), blk(13), blk(10), ALU.mult).then_inc(s["bt_ok"], 1)
            need("v_ok", 4)
            for ct in range(CT):
                ins = v.tensor_scalar(kprime[:, ct, :], iclr[:, ct, :], pcol("k_a", ct), small[:, 20 + ct:21 + ct],
                                      ALU.mult, ALU.add)
            link(ins)
            link(v.tensor_tensor(blk(3), blk(3), blk(4), ALU.mult))
            v.tensor_tensor(flat(kt), blk(3), blk(10), ALU.mult).then_inc(s["kt_ok"], 1)
            for ct in range(CT):
                v.scalar_tensor_tensor(out=tmp[:, ct, :], in0=r_[:, ct, :], scalar=pcol("r_k", ct), in1=kprime[:, ct, :],
                                       op0=ALU.mult, op1=ALU.mult).then_inc(s["bonin_ok"], 1)
            for i in range(2):
                wait_full(v, f"bon{i}")
                ins = v.tensor_tensor(flat(bonus)[:, i * 512:(i + 1) * 512], bank(f"bon{i}"),
                                      blk(2)[:, i * 512:(i + 1) * 512], ALU.mult)
                free(ins, f"bon{i}")
            wait_drained(v, "pool0")
            wait_drained(v, "pool1")
            need("misc_ok", 14)
            link(v.reciprocal(count_inv[:], count_inv[:]))
            for gi in range(CT):
                src, bufs, step = pz[:, gi, :], (pool_a, pool_b), 1
                for j in range(gi + 1):
                    dst = bufs[j % 2]
                    v.tensor_tensor(dst[:, step:T], src[:, step:T], src[:, 0:T - step], ALU.add)
                    link(v.tensor_copy(dst[:, 0:step], src[:, 0:step]))
                    src, step = dst, 2 * step
                win = step
                other = bufs[(gi + 1) % 2]
                link(v.tensor_tensor(other[:, 0:win], src[:, 0:win], count_inv[:, gi, 0:win], ALU.mult))
                v.tensor_tensor(pz[:, gi, 0:win], other[:, 0:win], pz[:, gi, 0:win], ALU.subtract)
                v.scalar_tensor_tensor(out=pz[:, gi, win:T], in0=src[:, win:T], scalar=1.0 / win,
                                       in1=pz[:, gi, win:T], op0=ALU.mult, op1=ALU.subtract).then_inc(s["pool_ok"], 1)
                need("pool_ok", gi + 1)
            need("masks_ok", 4)
            flat_mask = causal[:, :, :].rearrange("p m t -> p (m t)")
            wait_full(v, "bon1")
            need("tanh_ok", 1)
            need("sigg_ok", 1)
            need("sq_ok", 4)
            for n in range(16):
                wait_full(v, f"sc{n}")
                ins = v.tensor_tensor(sc[:, n, :, :].rearrange("p m t -> p (m t)"), bank(f"sc{n}"), flat_mask, ALU.mult)
                free(ins, f"sc{n}")
            need("dist_ok", 1)
            for n in range(6):
                wait_full(v, f"at{n}")
                for i, h in enumerate(attn_heads(n)):
                    slope = 2.0 ** -(h + 1)
                    if n < 4:
                        ins = v.scalar_tensor_tensor(out=prob[:, h, P:3 * P], in0=bank(f"at{n}")[:, i * T:(i + 1) * T],
                                                     scalar=DH ** -0.5 / slope, in1=dist[:], op0=ALU.mult, op1=ALU.subtract)
                    else:
                        ins = v.scalar_tensor_tensor(out=prob[:, h, 0:P], in0=bank(f"at{n}")[:, i * P:(i + 1) * P],
                                                     scalar=DH ** -0.5 / slope, in1=dist[:, P:T], op0=ALU.mult,
                                                     op1=ALU.subtract)
                free(ins, f"at{n}")
            wait_drained(v, *(f"at{n}" for n in range(2, 6)))
            v.tensor_reduce(amax[:, 0, :], prob[:, :, 0:P], AX.X, ALU.max).then_inc(s["smax_ok"], 1)
            v.tensor_reduce(amax[:, 1, :], prob[:, :, P:3 * P], AX.X, ALU.max).then_inc(s["smax_ok"], 1)
            need("smax_ok", 2)
            v.tensor_tensor(amax[:], amax[:], slopes[:], ALU.mult).then_inc(s["smax_ok"], 1)
            need("levels_ok", 7)

            def fill_blocks(name, g, lev):
                wait_full(v, name)
                mask = level_mask[:, lev, :].bitcast(I32).unsqueeze(1).to_broadcast([P, 4, P])
                return v.copy_predicated(tri[:, 4 * g:4 * g + 4, :], mask, bank(name).rearrange("p (n t) -> p n t", n=4))

            for g in range(4):
                link(v.tensor_copy(tri[:, 4 * g:4 * g + 4, :], ident[:, :].unsqueeze(1).to_broadcast([P, 4, P])))
            for g in range(4):
                free(fill_blocks(f"L{g}", g, 0), f"L{g}")
            need("exp_ok", 1)
            link(v.reciprocal(asum[:], asum[:]))
            rs = asum[:, :, :]
            v.tensor_tensor(prob[:, :, 0:P], prob[:, :, 0:P], rs[:, 0, :].unsqueeze(2).to_broadcast([P, H, P]),
                            ALU.mult).then_inc(s["prob_ok"], 1)
            v.tensor_tensor(prob[:, :, P:3 * P], prob[:, :, P:3 * P], rs[:, 1, :].unsqueeze(2).to_broadcast([P, H, 2 * P]),
                            ALU.mult).then_inc(s["prob_ok"], 1)
            for lev, size in enumerate(LEVELS):
                for g in range(4):
                    free(fill_blocks(f"T{size}_{g}", g, lev + 1), f"T{size}_{g}")
            wait_full(v, "St")
            for ct in range(CT):
                ins = v.tensor_scalar(state[:, ct, :], bank("St")[:, ct * DH:(ct + 1) * DH], small[:, 8 + ct:9 + ct], None,
                                      ALU.mult)
            free(ins, "St")

            def merge(br):
                for n in range(4):
                    name = f"p{br}{n}"
                    wait_full(v, name)
                    gsl = gates[:, 2 * n:2 * n + 2, :].rearrange("p k t -> p (k t)")
                    msl = merged[:, 2 * n:2 * n + 2, :].rearrange("p k t -> p (k t)")
                    wait_drained(v, f"g{br}{n // 2}{'ab'[n % 2]}")
                    if br == "C":
                        free(v.tensor_tensor(msl, gsl, bank(name), ALU.mult), name)
                        continue
                    free(v.tensor_tensor(gsl, gsl, bank(name), ALU.mult), name)
                    wait_drained(v, name)
                    v.tensor_tensor(msl, msl, gsl, ALU.add).then_inc(s["merged_ok"], 1)

            wait_full(v, "o1")
            merge("C")
            wait_drained(v, "pC0", "pC1", "pC2", "pC3")
            merge("A")
            wait_drained(v, "Y0")
            wait_drained(v, "Y1e")
            wait_drained(v, "Y1o")
            for i in range(2):
                wait_full(v, f"mu{i}")
                ins = v.scalar_tensor_tensor(out=blk(9)[:, i * 512:(i + 1) * 512], in0=bank(f"mu{i}"), scalar=-1.0 / DH,
                                             in1=blk(8)[:, i * 512:(i + 1) * 512], op0=ALU.mult, op1=ALU.add)
                free(ins, f"mu{i}")
            for i in range(2):
                wait_drained(v, f"va{i}")
            link(v.reciprocal(blk(13), blk(13)))
            link(v.tensor_tensor(blk(9), blk(9), blk(13), ALU.mult))
            for ct in range(CT):
                ins = v.tensor_scalar(y_cen[:, ct, :], y_cen[:, ct, :], pcol("lnx_g", ct), pcol("lnx_b", ct), ALU.mult, ALU.add)
            link(ins)
            link(v.tensor_tensor(blk(9), blk(9), flat(bonus), ALU.add))
            for i in range(2):
                wait_full(v, f"gg{i}")
                ins = v.tensor_tensor(flat(kt)[:, i * 512:(i + 1) * 512], blk(9)[:, i * 512:(i + 1) * 512], bank(f"gg{i}"),
                                      ALU.mult)
                free(ins, f"gg{i}")
            need("merged_ok", 4)
            merge("B")
            need("x_again", 16)
            for half in range(2):
                for t in range(TT):
                    name = f"wo{2 * half + t}"
                    wait_full(v, name)
                    xsl = x2[:, t, half * 512:(half + 1) * 512]
                    free(v.tensor_tensor(xsl, bank(name), xsl, ALU.add), name)
            wait_drained(v, "wo0", "wo1", "wo2", "wo3")
            need("x2ssq", 3)
            link(v.reciprocal(small[:, 14:16], small[:, 14:16]))
            need("bcast2_ok", 1)
            for t in range(TT):
                v.scalar_tensor_tensor(out=h2[:, t, :], in0=x2[:, t, :], scalar=small[:, 14 + t:15 + t], in1=norm2_b,
                                       op0=ALU.mult, op1=ALU.mult).then_inc(s["h2_ok"], 1)
            need("rbcast_ok", 1)
            wait_full(v, "rt")
            bias = router_b[:].unsqueeze(1).to_broadcast([P, TT, 36])
            free(v.tensor_tensor(lg, bank("rt")[:, 0:72].rearrange("p (t n) -> p t n", t=TT), bias, ALU.add), "rt")
            wait_drained(v, "rt")
            gl, el = lg[:, :, 0:NG], lg[:, :, NG:]

            def tmp3(o, n):
                return rtmp[:, o:o + TT * n].rearrange("p (t n) -> p t n", t=TT)

            def col2(o):
                return small[:, o:o + 2]

            def wide(ap, n):
                return ap.unsqueeze(2).to_broadcast([P, TT, n])

            asg, one1, one2, el2, cand, gw = tmp3(0, NE), tmp3(64, NE), tmp3(128, NE), tmp3(192, NE), tmp3(256, NE), tmp3(320, NE)
            g4, g4b = tmp3(384, NG), tmp3(392, NG)
            iota4 = iota_e[:, :, 0:NG]

            def first_max(dst, src, n, m, it, c):
                link(v.tensor_reduce(m, src, AX.X, ALU.max))
                link(v.tensor_tensor(c, src, wide(m, n), ALU.is_equal))
                link(v.scalar_tensor_tensor(out=c, in0=c, scalar=-100.0, in1=it, op0=ALU.mult, op1=ALU.add))
                link(v.tensor_reduce(col2(28), c, AX.X, ALU.min))
                link(v.tensor_tensor(dst, c, wide(col2(28), n), ALU.is_equal))

            first_max(g4, gl, NG, col2(26), iota4, g4b)
            v.tensor_tensor(small[:, 32:40].rearrange("p (t n) -> p t n", t=TT), gl, wide(col2(26), NG),
                            ALU.subtract).then_inc(s["eexp_in"], 1)
            link(v.tensor_scalar(g4b, g4, FAR, -FAR, ALU.mult, ALU.add))
            for t in range(TT):
                gsel = g4[:, t, :].unsqueeze(2).to_broadcast([P, NG, EPG])
                gpen = g4b[:, t, :].unsqueeze(2).to_broadcast([P, NG, EPG])
                e3 = el2[:, t, :].rearrange("p (g e) -> p g e", g=NG)
                link(v.tensor_tensor(e3, el[:, t, :].rearrange("p (g e) -> p g e", g=NG), gsel, ALU.mult))
                link(v.tensor_tensor(e3, e3, gpen, ALU.add))
            first_max(one1, el2, NE, col2(30), iota_e[:], cand)
            link(v.scalar_tensor_tensor(out=el2, in0=one1, scalar=-2 * FAR, in1=el2, op0=ALU.mult, op1=ALU.add))
            first_max(one2, el2, NE, col2(24), iota_e[:], cand)
            v.tensor_tensor(asg, one1, one2, ALU.add).then_inc(s["cs_in"], 1)
            v.tensor_tensor(col2(24), col2(24), col2(30), ALU.subtract).then_inc(s["eexp_in"], 1)
            need("eexp_ok", 1)
            link(v.tensor_reduce(col2(50), small[:, 32:40].rearrange("p (t n) -> p t n", t=TT), AX.X, ALU.add))
            need("eexp_ok", 2)
            link(v.tensor_scalar(col2(52), col2(24), 1.0, None, ALU.add))
            link(v.tensor_tensor(col2(50), col2(50), col2(52), ALU.mult))
            link(v.reciprocal(col2(50), col2(50)))
            link(v.tensor_tensor(col2(52), col2(50), col2(24), ALU.mult))
            link(v.tensor_tensor(one1, one1, wide(col2(50), NE), ALU.mult))
            link(v.tensor_tensor(one2, one2, wide(col2(52), NE), ALU.mult))
            link(v.tensor_tensor(gw, one1, one2, ALU.add))
            for r in range(ROUNDS):
                v.tensor_copy(wts[:, :, r * NE:(r + 1) * NE], gw)
            v.memset(wts[:, :, NE * ROUNDS:], 0.0)
            v.memset(pos[:, :, NE * ROUNDS:], -1e4)
            wait_full(v, "cs")
            link(v.tensor_reduce(small[:, 54:55], bank("cs")[:, 64:96], AX.X, ALU.max))
            place = bank("cs")[:, 0:64].rearrange("p (t n) -> p t n", t=TT)
            need("cs_in", 1)
            free(v.tensor_tensor(cand, place, asg, ALU.mult), "cs")
            link(v.tensor_scalar(el2, asg, 1000.0, -1000.0, ALU.mult, ALU.add))
            wait_drained(v, "cs")
            link(v.tensor_tensor(cand, cand, el2, ALU.add))
            for r in range(ROUNDS):
                ins = v.tensor_scalar(pos[:, :, r * NE:(r + 1) * NE], cand, float(-CAP * r), None, ALU.add)
            link(ins)
            link(v.tensor_scalar(small[:, 55:56], small[:, 54:55], CAP + 0.5, 16.0, ALU.is_gt, ALU.mult))
            for r in range(2, ROUNDS):
                link(v.tensor_scalar(small[:, 56:57], small[:, 54:55], CAP * r + 0.5, 16.0, ALU.is_gt, ALU.mult))
                link(v.tensor_tensor(small[:, 55:56], small[:, 55:56], small[:, 56:57], ALU.add))
            v.tensor_scalar(pairs_i[:], small[:, 55:56], 16.0, None, ALU.add).then_inc(s["pairs_ok"], 1)

            def select(b, col, count):
                for t in range(TT):
                    ins = v.tensor_scalar(sel[b][:, t, :], iota_slot[:], pos[:, t, col], None, ALU.is_equal)
                ins.then_inc(s["sel_ok"], 1)

            def weigh(b, col):
                for t in range(TT):
                    ins = v.tensor_scalar(selw[:, t, b, :], iota_slot[:], pos[:, t, col], wts[:, t, col], ALU.is_equal, ALU.mult)
                ins.then_inc(s["sel_table"], 1)

            need("pairs_ok", 1)
            pairs = v.value_load(pairs_i[0:1, 0:1], min_val=16, max_val=16 * ROUNDS)
            select(0, slice(0, 1), 1)
            weigh(0, slice(0, 1))
            with v.Fori(0, pairs) as i:
                for b in range(2):
                    n = i * 2 + b
                    nxt = bass.ds(n + 1, 1)
                    v.wait_ge(s["gathered"], n + 1)
                    select(1 - b, nxt, n + 2)
                    if b == 0:
                        weigh(1, nxt)
                    v.wait_ge(s["silu_ok"], n + 1)
                    v.wait_ge(s["h3_full"], n + 1)
                    v.tensor_tensor(hid[b].rearrange("p k c -> p (k c)"), silu[b], ps[:, 7, 0:256], ALU.mult).then_inc(
                        s["hid_ok"], 1)
                v.wait_ge(s["swT_full"], i + 1)
                v.tensor_copy(selwT, ps[:, 4, 0:256]).then_inc(s["swT_ok"], 1)
                weigh(0, bass.ds(i * 2 + 2, 1))
                v.wait_ge(s["yn_full"], i * 2 + 2)
                v.tensor_copy(yn[:, 512:1024], ps[:, 5, :]).then_inc(s["yn1_ok"], 1)
            need("fssq", 3)
            link(v.reciprocal(small[:, 18:20], small[:, 18:20]))
            need("bcastf_ok", 1)
            for t in range(TT):
                v.scalar_tensor_tensor(out=out_sb[:, t, :], in0=ps[:, 2 * t:2 * t + 2, :].rearrange("p b c -> p (b c)"),
                                       scalar=small[:, 18 + t:19 + t], in1=final_b, op0=ALU.mult, op1=ALU.mult).then_inc(
                    s["out_ok"], 1)


def attn_heads(n):
    return ((0, 2), (1, 3), (4, 6), (5, 7), (0, 2, 4, 6), (1, 3, 5, 7))[n]


NAMES = ("x norm1_g w_in rwkv_mu w0 w_decay_up a0 w_iclr_up w_gate_up k_k k_a r_k lnx_g lnx_b pool_w pool_scale "
         "w_branch w_out norm2_g router_grp_w router_grp_b router_exp_w router_exp_b exp_w1 exp_w3 exp_w2 "
         "final_norm_g").split()


def kernel(**inputs):
    import numpy as _np
    import concourse.bacc as _bacc
    from concourse import mybir as _mybir
    from concourse.bass_utils import run_bass_kernel_spmd as _run

    nc = _bacc.Bacc("TRN2", target_bir_lowering=False, num_devices=1)
    arrays, args = {}, {}
    for name in NAMES:
        a = _np.ascontiguousarray(inputs[name])
        arrays[f"in_{name}_dram"] = a
        args[name] = nc.dram_tensor(f"in_{name}_dram", a.shape, _mybir.dt.from_np(a.dtype), kind="ExternalInput").ap()
    out = nc.dram_tensor("out_0_dram", (1, T, D), _mybir.dt.float32, kind="ExternalOutput").ap()
    trunk_and_experts(nc, out=out, **args)
    r = _run(nc, [arrays], core_ids=[0])
    return r.results[0]["out_0_dram"]
```

```python
from contextlib import ExitStack

import concourse.bass as bass
from concourse import mybir

ALU = mybir.AluOpType
ACT = mybir.ActivationFunctionType
AX = mybir.AxisListType
F32 = mybir.dt.float32
F32R = mybir.dt.float32r
I32 = mybir.dt.int32

P = 128
T = 256
TT = T // P
D = 1024
KD = D // P
BW = 512
CT = BW // P
H = 8
DH = 64
NG, EPG = 4, 8
NE = NG * EPG
HID = 512
HC = HID // P
CAP = 64
ROUNDS = T // CAP
RMS_EPS = 1e-6
LNX_EPS = 64e-5
DECAY_SCALE = 0.6065306597126334
FAR = 1e30
PIECE = 4096

Q_COL, K_COL, V_COL = 0, BW, 2 * BW
GATE_COL = 3 * BW
POOL_COL = GATE_COL + 3 * D
R_COL = POOL_COL + BW
RK_COL, RV_COL, LORA_COL = R_COL + BW, R_COL + 2 * BW, R_COL + 3 * BW

PAR_ROWS = (("norm1_g", 8), ("rwkv_mu", 14), ("w0", 4), ("a0", 4), ("k_k", 4), ("k_a", 4),
            ("r_k", 4), ("lnx_g", 4), ("lnx_b", 4), ("pool_scale", 4))

PIECES = ["lora", "rk", "rr", "rv", "aq", "ak", "av", "pool", "gC0", "gC1", "pC",
          "gA0", "gA1", "pA", "gB0", "gB1", "pB", "wo0", "wo1"]
TRUNK_SLOTS = 4
HALF = PIECE // 2
HALVES = 6
RAW = 6
SPLIT = 4

LEVELS = (2, 4, 8, 16, 32, 64)


def fill_plan():
    plan = [("par", 1)] + [(f"hT{n}", 0) for n in range(4)]
    plan += [("lora", 0), ("rk0", 0), ("rk1", 0)]
    plan += [("u0", 1), ("u1", 1), ("a0", 1), ("a1", 1)]
    plan += [("rr0", 0), ("rr1", 0), ("rv0", 0), ("rv1", 0), ("ss0", 1), ("ss1", 1)]
    plan += [("aq0", 0), ("aq1", 0), ("ak0", 0), ("ak1", 0), ("av0", 0), ("av1", 0), ("pool0", 0), ("pool1", 0)]
    plan += [("vn0", 1), ("vn1", 1), ("bn", 1), ("kn", 1), ("bon0", 1), ("bon1", 1)]
    plan += [(f"sc{n}", 1) for n in range(16)]
    plan += [(f"at{n}", 0) for n in range(6)]
    plan += [(f"L{g}", 1) for g in range(4)] + [(f"G1_{g}", 1) for g in range(4)]
    for b in LEVELS:
        plan += [(f"A{b}_{g}", 1) for g in range(4)]
        plan += [(f"T{b}_{g}", 1) for g in range(4)]
        plan += [(f"G{b}_{g}", 1) for g in range(4)]
    plan += [(f"pt{h}", 0) for h in range(5)] + [("o0", 1)]
    plan += [(f"pt{h}", 0) for h in range(5, 8)] + [("o1", 1)]
    plan += [("pw", 1), ("pw1", 1)]
    plan += [("X0", 1), ("gC0a", 0), ("gC0b", 0), ("SA0", 1), ("gC1a", 0), ("gC1b", 0), ("St", 1)]
    plan += [(f"pC{n}", 0) for n in range(4)]
    plan += [("X1e", 1), ("X1o", 1), ("gA0a", 0), ("gA0b", 0), ("SA1", 1), ("gA1a", 0), ("gA1b", 0)]
    plan += [("Y0", 1), ("Y1e", 1), ("Y1o", 1)]
    plan += [(f"pA{n}", 0) for n in range(4)]
    plan += [("mu0", 1), ("mu1", 1), ("gB0a", 0), ("gB0b", 0), ("va0", 1), ("va1", 1)]
    plan += [("gg0", 1), ("gg1", 1), ("gB1a", 0), ("gB1b", 0)]
    plan += [(f"pB{n}", 0) for n in range(4)]
    plan += [(f"wo{n}", 0) for n in range(4)]
    plan += [(f"h2T{n}", 0) for n in range(4)] + [("rt", 1), ("cs", 1)]
    return [n for n, _ in plan], dict(plan)


FILLS, RING_OF = fill_plan()
BANK, USE, seen = {}, {}, [0, 0]
for _name in FILLS:
    _r = RING_OF[_name]
    BANK[_name] = 4 * _r + seen[_r] % 4
    USE[_name] = seen[_r] // 4
    seen[_r] += 1
FULL = {n: i + 1 for i, n in enumerate(FILLS)}


def trunk_and_experts(nc, x, norm1_g, w_in, rwkv_mu, w0, w_decay_up, a0, w_iclr_up, w_gate_up, k_k, k_a, r_k,
                      lnx_g, lnx_b, pool_w, pool_scale, w_branch, w_out, norm2_g, router_grp_w, router_grp_b,
                      router_exp_w, router_exp_b, exp_w1, exp_w3, exp_w2, final_norm_g, out):
    with ExitStack() as ctx:
        start = (nc.sbuf_base + 63) // 64 * 64
        top = [start]
        where = {}

        def sb(name, shape, dt=F32, over=None, skip=0):
            n = 4
            for d in shape[1:]:
                n *= d
            if over is None:
                at, top[0] = top[0], top[0] + (n + 31) // 32 * 32
                assert top[0] <= nc.sbuf_usable_end, name
            else:
                at = where[over] + 4 * skip
            where[name] = at
            return nc.alloc_sbuf_tensor_at(name, shape, dt, offset=at)

        ring = sb("ring", [P, TRUNK_SLOTS * PIECE])
        arena = sb("arena", [P, 14 * 1024])
        hT = sb("hT", [P, KD, T])
        qk = sb("qk", [P, 2, CT, T])
        va = sb("va", [P, TT, BW])
        pz = sb("pz", [P, CT, T])
        ar = sb("ar", [P, CT, TT, 2, P])
        bt = sb("bt", [P, CT, T])
        kt = sb("kt", [P, CT, T])
        vn = sb("vn", [P, TT, BW])
        bkn = sb("bkn", [P, 2, BW])
        bonus = sb("bonus", [P, CT, T])
        sig_g = sb("sig_g", [P, T])
        gm = sb("gm", [P, 2, KD, T])
        par_rows = bkn[0:64, 1, 0:P]
        par = sb("par", [P, 54])
        ident = sb("ident", [P, P])
        ones = sb("ones", [P, P])
        head_ones = sb("head_ones", [P, P])
        causal = sb("causal", [P, 4, P])
        level_mask = sb("level_mask", [P, 7, P])
        dist = sb("dist", [P, T])
        count_inv = sb("count_inv", [P, CT, 16])
        lora_up = sb("lora_up", [P, BW])
        gate_up = sb("gate_up", [P, BW])
        poolw = sb("poolw", [P, CT, P])
        router_w = sb("router_w", [P, KD, NG + NE])
        router_b = sb("router_b", [P, NG + NE])
        router_b_row = sb("router_b_row", [1, NG + NE])
        small = sb("small", [P, 64])
        slopes = sb("slopes", [P, TT, H])
        amax = sb("amax", [P, TT, H])
        asum = sb("asum", [P, TT, H])
        state = sb("state", [P, CT, DH])
        iota_slot = sb("iota_slot", [P, 2, CAP])
        iota_e = sb("iota_e", [P, TT, NE])
        last_quad_i = sb("last_quad_i", [P, 1], I32)

        ps = ctx.enter_context(nc.psum_tensor("ps", [P, 8, 512], F32))

        def blk(n, m=1):
            return arena[:, n * 1024:(n + m) * 1024]

        def slot(n):
            return ring[:, n * PIECE:(n + 1) * PIECE] if n < TRUNK_SLOTS else arena[:, (n - 4) * PIECE:(n - 3) * PIECE]

        def ch(ap):
            return ap.rearrange("p (c t) -> p c t", c=CT)

        def chunks(ap):
            return ap.rearrange("p (c t) -> p c t", c=CT * TT)

        x_sb = blk(0, 2).rearrange("p (t d) -> p t d", t=TT)
        xn = blk(2, 2).rearrange("p (t d) -> p t d", t=TT)
        k_, r_, v_, dz, kprime = ch(blk(4)), ch(blk(1)), ch(blk(2)), ch(blk(3)), ch(blk(3))
        lora = blk(0)[:, 0:2 * T].rearrange("p (c t) -> p c t", c=2)
        dlora = blk(0)[:, 2 * T:4 * T].rearrange("p (c t) -> p c t", c=2)
        logw, iclr, lp, lpm, ep, en, kk, sq, tmp = (ch(blk(n)) for n in range(5, 14))
        tanh_w = bkn[0:64, 0, 0:T]
        sc = blk(0, 8).rearrange("p (n m t) -> p n m t", n=16, m=4)
        tri = blk(8, 2).rearrange("p (n t) -> p n t", n=16)
        triT = blk(10, 2).rearrange("p (n t) -> p n t", n=16)
        triA = blk(12, 2).rearrange("p (n t) -> p n t", n=16)
        xs = [blk(12)[:, 0:512], blk(13)[:, 0:512]]
        sa = [blk(12)[:, 512:1024], blk(13)[:, 512:1024]]
        y_raw, y_cen, y_sq, y_rstd = ch(blk(8)), ch(blk(9)), ch(blk(12)), ch(blk(13))
        flat_gm = gm[:, :, :, :].rearrange("p a k t -> p (a k t)")
        prob = flat_gm[:, 0:H * 384].rearrange("p (h k) -> p h k", h=H)
        probT = flat_gm[:, 3072:3072 + 2 * 384].rearrange("p (b k) -> p b k", b=2)
        scan_ones = flat_gm[:, 0:1024]
        ptmp = flat_gm[:, 3840:4096]
        pool_a, pool_b = blk(13)[:, 0:T], blk(13)[:, T:2 * T]
        gates, merged = gm[:, 0], gm[:, 1]
        y_attn, y_rwkv, y_pool = bt, kt, pz
        x2 = qk[:, :, :, :].rearrange("p a c t -> p (a c t)").rearrange("p (t d) -> p t d", t=TT)
        h2 = gm[:, 0].rearrange("p k t -> p (k t)").rearrange("p (t d) -> p t d", t=TT)
        h2n = gm[:, 1].rearrange("p k t -> p (k t)").rearrange("p (t d) -> p t d", t=TT)
        flat_ar = ar[:, :, :, :, :].rearrange("p a b c d -> p (a b c d)")
        norm2_b, final_b = flat_ar[:, 0:D], flat_ar[:, D:2 * D]
        out_sb = gm[:, 1].rearrange("p k t -> p (k t)").rearrange("p (t d) -> p t d", t=TT)
        NPOS = NE * ROUNDS
        raw = [ring[:, n * HALF:(n + 1) * HALF].rearrange("p (k c) -> p k c", k=4) for n in range(RAW)]
        whi = sb("whi", [P, SPLIT, 4, 512], F32R, over="ring", skip=3 * PIECE)
        wlo = sb("wlo", [P, SPLIT, 4, 512], F32R, over="arena", skip=4 * 1024)
        h2hi = sb("h2hi", [P, TT, D], F32R, over="bt")
        h2lo = sb("h2lo", [P, TT, D], F32R, over="va")
        xg = [sb("xg0", [P, KD, 2, 2, CAP], F32R, over="hT"), sb("xg1", [P, KD, 2, 2, CAP], F32R, over="gm")]
        yhi = sb("yhi", [P, D], F32R, over="qk")
        ylo = sb("ylo", [P, D], F32R, over="qk", skip=D)
        hidden = sb("hidden", [P, HC, 2, CAP], F32R, over="bonus")
        silu, hid = bonus[:, 2, :], bonus[:, 3, :]
        selp = sb("selp", [P, TT, 2, CAP], F32R, over="bkn")
        selT = [sb(f"selT{b}", [P, T], F32R, over="bkn", skip=256 * (1 + b)) for b in range(2)]
        hs = blk(13)[:, 0:1024].rearrange("p (a c) -> p a c", a=2)
        pos = blk(12)[:, 0:TT * NPOS].rearrange("p (t n) -> p t n", t=TT)
        wts = blk(12)[:, 256:256 + TT * NPOS].rearrange("p (t n) -> p t n", t=TT)
        seldup = [blk(12)[:, 512 + b * 256:768 + b * 256].rearrange("p (t c) -> p t c", t=TT) for b in range(2)]
        fold = sb("fold", [P, CAP], over="bkn", skip=768)
        foldw = [sb(f"foldw{b}", [P, CAP], over="bkn", skip=832 + CAP * b) for b in range(2)]
        wcol = sb("wcol", [P, 2, TT], over="bkn", skip=960)
        pair_cols = sb("pair_cols", [P, TT, 2], over="bkn", skip=968)[:]
        dup_cols = sb("dup_cols", [P, 2, TT], over="bkn", skip=976)
        lg = vn[:, 0, 0:TT * 36].rearrange("p (t n) -> p t n", t=TT)
        rtmp = vn[:, 1, :]

        full = ctx.enter_context(nc.semaphore("full"))
        drained = [ctx.enter_context(nc.semaphore(f"drained{b}")) for b in range(8)]
        loaded = [ctx.enter_context(nc.semaphore(f"loaded{n}")) for n in range(TRUNK_SLOTS)]
        raw_in = [ctx.enter_context(nc.semaphore(f"raw_in{n}")) for n in range(RAW)]
        SEMS = ("column_ok compared x_in par_in x_again lo_ok quads_ok out_ok out_done pool_chain ident_ok lora_in gateup_in "
                "pool_in rw_in rb_in ones_ok masks_ok levels_ok dist_ok misc_ok rbcast_ok n2_in nf_in "
                "bcast2_ok bcastf_ok fold_ok selp_ok dup_ok gathered selT_full xn_ok tanh_ok lora_ok sq_ok "
                "v_ok bonin_ok ar_ok prob_ok pool_ok ysq_ok sigg_ok merged_ok h2_ok cs_in scattered xg_ok "
                "ylo_ok half_done hs_ok selT_ok folded hidlo_ok h2r_ok hi_ok const_ok ssq k_ok norm_ok "
                "logw_ok exps_ok smax_ok exp_ok x2ssq h2hi_ok eexp_in eexp_ok silu_ok hid_ok hidhi_ok "
                "yhi_ok fssq dve kk_ok r_ok bt_ok kt_ok dve0 ").split()
        s = {n: ctx.enter_context(nc.semaphore(n)) for n in SEMS}

        def bank(name):
            return ps[:, BANK[name], :]

        def wait_full(eng, *names):
            for name in names:
                eng.wait_ge(full, FULL[name])

        def wait_drained(eng, *names):
            for name in names:
                eng.wait_ge(drained[BANK[name]], USE[name] + 1)

        pc, at = {}, 0
        for n, rows in PAR_ROWS:
            pc[n] = at
            at += rows

        def pcol(name, i):
            return par[:, pc[name] + i:pc[name] + i + 1]

        block = ctx.enter_context(nc.Block())

        piece_src = {
            "lora": w_in[0, :, LORA_COL:LORA_COL + 256], "rk": w_in[0, :, RK_COL:RK_COL + BW],
            "rr": w_in[0, :, R_COL:R_COL + BW], "rv": w_in[0, :, RV_COL:RV_COL + BW],
            "aq": w_in[0, :, Q_COL:Q_COL + BW], "ak": w_in[0, :, K_COL:K_COL + BW],
            "av": w_in[0, :, V_COL:V_COL + BW], "pool": w_in[0, :, POOL_COL:POOL_COL + BW],
            "wo0": w_out[0, :, 0:BW], "wo1": w_out[0, :, BW:D],
        }
        for br, b in (("A", 0), ("B", 1), ("C", 2)):
            for half in range(2):
                c0 = GATE_COL + b * D + half * BW
                piece_src[f"g{br}{half}"] = w_in[0, :, c0:c0 + BW]
            piece_src[f"p{br}"] = w_branch[0, b]
        last_fill = {"lora": "lora", "rk": "rk1", "rr": "rr1", "rv": "rv1", "aq": "aq1", "ak": "ak1", "av": "av1",
                     "pool": "pool1", "gC0": "gC0b", "gC1": "gC1b", "pC": "pC3", "gA0": "gA0b", "gA1": "gA1b",
                     "pA": "pA3", "gB0": "gB0b", "gB1": "gB1b", "pB": "pB3", "wo0": "wo1", "wo1": "wo3"}

        def piece(name):
            n = PIECES.index(name)
            cols = {"lora": 256}.get(name, D if name[0] == "p" and name != "pool" else BW)
            k = 4 if cols == D else KD
            return slot(n % TRUNK_SLOTS)[:, 0:k * cols].rearrange("p (k c) -> p k c", k=k)

        def trunk_loads(n):
            return 16 * (n // TRUNK_SLOTS + 1)

        SLOT_FREE = [last_fill[[p for n, p in enumerate(PIECES) if n % TRUNK_SLOTS == b][-1]] for b in range(TRUNK_SLOTS)]

        def half_dma(sp, j, e):
            w = (exp_w1, exp_w3, exp_w2)[j // 2][0, bass.ds(e, 1)]
            src = w[:, (j % 2) * 512:(j % 2 + 1) * 512, :] if j < 4 else w[:, :, (j % 2) * 512:(j % 2 + 1) * 512]
            return sp.dma_start(raw[j], src.rearrange("o (k p) c -> p (o k) c", p=P))

        @block.sync
        def _(sp):
            sp.dma_start(x_sb, x[0].rearrange("(t p) d -> p t d", p=P)).then_inc(s["x_in"], 16)
            row = 0
            for name, src in (("norm1_g", norm1_g), ("rwkv_mu", rwkv_mu), ("w0", w0), ("a0", a0), ("k_k", k_k),
                              ("k_a", k_a), ("r_k", r_k), ("lnx_g", lnx_g), ("lnx_b", lnx_b),
                              ("pool_scale", pool_scale)):
                rows = dict(PAR_ROWS)[name]
                flat = src[0].rearrange("h d -> (h d)") if name == "r_k" else src[0]
                sp.dma_start(par_rows[row:row + rows, :], flat.rearrange("(r c) -> r c", c=P)).then_inc(s["par_in"], 16)
                row += rows
            for n, name in enumerate(PIECES):
                if n >= TRUNK_SLOTS:
                    sp.wait_ge(full, FULL[last_fill[PIECES[n - TRUNK_SLOTS]]])
                sp.dma_start(piece(name), piece_src[name].rearrange("(k p) c -> p k c", p=P)).then_inc(
                    loaded[n % TRUNK_SLOTS], 16)
                if name == "gA0":
                    sp.wait_ge(full, FULL["at5"])
                    sp.dma_start(x2, x[0].rearrange("(t p) d -> p t d", p=P)).then_inc(s["x_again"], 16)
            for j in range(RAW):
                sp.wait_ge(full, FULL[SLOT_FREE[j // 2]])
                half_dma(sp, j, 0).then_inc(raw_in[j], 16)
            for j in range(HALVES):
                sp.wait_ge(s["lo_ok"], j + 1)
                half_dma(sp, j, 1).then_inc(raw_in[j], 16)
            sp.wait_ge(s["quads_ok"], 1)
            last_quad = sp.value_load(last_quad_i[0:1, 0:1], min_val=NE // 4 - 1, max_val=NE // 4 * ROUNDS - 1)
            for n in (2, 3):
                for j in range(HALVES):
                    sp.wait_ge(s["lo_ok"], HALVES * (n - 1) + j + 1)
                    half_dma(sp, j, n).then_inc(raw_in[j], 16)
            with sp.Fori(1, last_quad + 1) as i:
                for n in range(4):
                    e = sp.snap((i % (NE // 4)) * 4 + n, min_val=0, max_val=NE - 1)
                    for j in range(HALVES):
                        sp.wait_ge(s["lo_ok"], i * 24 + (HALVES * (n - 1) + j + 1))
                        half_dma(sp, j, e).then_inc(raw_in[j], 16)
            for t in range(TT):
                sp.wait_ge(s["out_ok"], t + 1)
                sp.dma_start(out[0, t * P:(t + 1) * P, :], out_sb[:, t, :]).then_inc(s["out_done"], 16)
            sp.wait_ge(s["out_done"], 16 * TT)

        @block.gpsimd
        def _(g):
            chain = [0]

            def link(ins):
                chain[0] += 1
                ins.then_inc(s["pool_chain"], 1)
                g.wait_ge(s["pool_chain"], chain[0])

            link(nc.gpsimd.memset(ident[:], 0.0))
            nc.gpsimd.affine_select(out=ident[:], in_=ident[:], compare_op=ALU.not_equal, fill=1.0, base=0,
                                    pattern=[[-1, P]], channel_multiplier=1).then_inc(s["ident_ok"], 1)
            g.dma_start(lora_up[0:64, :], w_decay_up[0]).then_inc(s["lora_in"], 16)
            g.dma_start(lora_up[64:P, :], w_iclr_up[0]).then_inc(s["lora_in"], 16)
            g.dma_start(gate_up[:], w_gate_up[0]).then_inc(s["gateup_in"], 16)
            g.dma_start(poolw[:], pool_w[0].rearrange("g c d -> c g d")).then_inc(s["pool_in"], 16)
            g.dma_start(router_w[:, :, 0:NG], router_grp_w[0].rearrange("(k p) n -> p k n", p=P)).then_inc(s["rw_in"], 16)
            g.dma_start(router_w[:, :, NG:], router_exp_w[0].rearrange("(k p) n -> p k n", p=P)).then_inc(s["rw_in"], 16)
            g.dma_start(router_b_row[:, 0:NG], router_grp_b).then_inc(s["rb_in"], 16)
            g.dma_start(router_b_row[:, NG:], router_exp_b).then_inc(s["rb_in"], 16)
            nc.gpsimd.memset(ones[:], 1.0).then_inc(s["ones_ok"], 1)
            link(nc.gpsimd.memset(head_ones[:], 1.0))
            nc.gpsimd.affine_select(out=head_ones[:, 0:DH], in_=head_ones[:, 0:DH], compare_op=ALU.is_ge, fill=0.0,
                                    base=DH - 1, pattern=[[0, DH]], channel_multiplier=-1)
            nc.gpsimd.affine_select(out=head_ones[:, DH:P], in_=head_ones[:, DH:P], compare_op=ALU.is_ge, fill=0.0,
                                    base=-DH, pattern=[[0, DH]], channel_multiplier=1).then_inc(s["ones_ok"], 1)
            nc.gpsimd.memset(scan_ones, 1.0).then_inc(s["ones_ok"], 1)
            g.wait_ge(s["ones_ok"], 3)
            nc.gpsimd.memset(scan_ones.rearrange("p (n t) -> p n t", t=P)[:, :, 0:1], 0.0).then_inc(s["ones_ok"], 1)
            link(nc.gpsimd.memset(causal[:], 1.0))
            for m in range(4):
                nc.gpsimd.affine_select(out=causal[:, m, :], in_=causal[:, m, :], compare_op=ALU.is_ge, fill=0.0,
                                        base=-1 if m % 2 == 0 else 0, pattern=[[1, P]],
                                        channel_multiplier=-1).then_inc(s["masks_ok"], 1)
            link(nc.gpsimd.memset(level_mask[:], 0.0))
            for lev in range(7):
                b = 1 << lev
                view = level_mask[:, lev, :].rearrange("p (n c) -> p n c", c=2 * b)[:, :, 0:b]
                nb = P // (2 * b)
                link(nc.gpsimd.memset(view, 1.0))
                link(nc.gpsimd.affine_select(out=view, in_=view, compare_op=ALU.is_ge, fill=0.0, base=-b,
                                             pattern=[[-2 * b, nb], [0, b]], channel_multiplier=1))
                nc.gpsimd.affine_select(out=view, in_=view, compare_op=ALU.is_ge, fill=0.0, base=2 * b - 1,
                                        pattern=[[2 * b, nb], [0, b]], channel_multiplier=-1).then_inc(s["levels_ok"], 1)
            link(nc.gpsimd.iota(dist[:], [[-1, T]], base=P, channel_multiplier=1, allow_small_or_imprecise_dtypes=True))
            nc.gpsimd.affine_select(out=dist[:], in_=dist[:], compare_op=ALU.is_ge, fill=FAR, base=P,
                                    pattern=[[-1, T]], channel_multiplier=1).then_inc(s["dist_ok"], 1)
            for h in range(H):
                nc.gpsimd.memset(slopes[:, :, h:h + 1], -(2.0 ** -(h + 1))).then_inc(s["misc_ok"], 1)
            nc.gpsimd.iota(iota_slot[:], [[0, 2], [1, CAP]], base=0, channel_multiplier=0,
                           allow_small_or_imprecise_dtypes=True).then_inc(s["misc_ok"], 1)
            nc.gpsimd.iota(iota_e[:], [[0, TT], [1, NE]], base=0, channel_multiplier=0,
                           allow_small_or_imprecise_dtypes=True).then_inc(s["misc_ok"], 1)
            link(nc.gpsimd.iota(count_inv[:], [[0, CT], [1, 16]], base=1, channel_multiplier=0,
                                allow_small_or_imprecise_dtypes=True))
            for i in range(CT):
                nc.gpsimd.tensor_scalar(count_inv[:, i, :], count_inv[:, i, :], float(2 << i), None,
                                        ALU.min).then_inc(s["misc_ok"], 1)
            g.wait_ge(s["rb_in"], 32)
            nc.gpsimd.partition_broadcast(router_b[:], router_b_row[:]).then_inc(s["rbcast_ok"], 1)
            g.wait_ge(full, FULL["Y1o"])
            g.dma_start(norm2_b[0:1, :], norm2_g).then_inc(s["n2_in"], 16)
            g.dma_start(final_b[0:1, :], final_norm_g.rearrange("(o d) -> o d", o=1)).then_inc(s["nf_in"], 16)
            g.wait_ge(s["n2_in"], 16)
            nc.gpsimd.partition_broadcast(norm2_b, norm2_b[0:1, :]).then_inc(s["bcast2_ok"], 1)
            g.wait_ge(s["nf_in"], 16)
            nc.gpsimd.partition_broadcast(final_b, final_b[0:1, :]).then_inc(s["bcastf_ok"], 1)
            link(nc.gpsimd.memset(fold[:], 0.0))
            link(nc.gpsimd.affine_select(out=fold[:], in_=fold[:], compare_op=ALU.not_equal, fill=1.0, base=0,
                                         pattern=[[-1, CAP]], channel_multiplier=1))
            nc.gpsimd.affine_select(out=fold[:], in_=fold[:], compare_op=ALU.not_equal, fill=1.0, base=-CAP,
                                    pattern=[[-1, CAP]], channel_multiplier=1).then_inc(s["fold_ok"], 1)

            g.wait_ge(s["quads_ok"], 1)
            last_quad = g.value_load(last_quad_i[0:1, 0:1], min_val=NE // 4 - 1, max_val=NE // 4 * ROUNDS - 1)

            def select_pair(n0, columns):
                nc.gpsimd.tensor_copy(pair_cols, pos[:, :, bass.ds(n0, 2)]).then_inc(s["column_ok"], 1)
                g.wait_ge(s["column_ok"], columns + 1)
                g.sem_inc(s["compared"], 1)
                for b in range(2):
                    for t in range(TT):
                        ins = nc.gpsimd.tensor_scalar(selp[:, t, b, :], iota_slot[:, 0, :], pair_cols[:, t, b:b + 1], None,
                                                      ALU.is_equal)
                ins.then_inc(s["selp_ok"], 1)

            def select_dup(b, n, columns):
                nc.gpsimd.tensor_copy(wcol[:, b, :].unsqueeze(2), wts[:, :, bass.ds(n, 1)])
                nc.gpsimd.tensor_copy(dup_cols[:, b, :].unsqueeze(2), pos[:, :, bass.ds(n, 1)]).then_inc(s["column_ok"], 1)
                g.wait_ge(s["column_ok"], columns + 2 + b)
                g.sem_inc(s["compared"], 1)
                for t in range(TT):
                    ins = nc.gpsimd.tensor_scalar(seldup[b][:, t, :], iota_slot[:].rearrange("p a c -> p (a c)"),
                                                  dup_cols[:, b, t:t + 1], None, ALU.is_equal)
                ins.then_inc(s["dup_ok"], 1)

            select_pair(0, 0)
            select_dup(0, 0, 0)
            select_dup(1, 1, 0)

            def next_pair(i, p):
                n0 = i * 4 + 2 * p
                columns = i * 6 + 3 * (p + 1)
                g.wait_ge(s["gathered"], i * 8 + 4 * (p + 1))
                select_pair(n0 + 2, columns)
                for b in range(2):
                    g.wait_ge(s["selT_full"], n0 + b + 1)
                    select_dup(b, n0 + b + 2, columns)

            with g.Fori(0, last_quad) as i:
                next_pair(i, 0)
                next_pair(i, 1)
            next_pair(last_quad, 0)

        @block.tensor
        def _(pe):
            order = iter(FILLS)

            def open_fill(name):
                if USE[name]:
                    pe.wait_ge(drained[BANK[name]], USE[name])
                return bank(name)

            def close_fill(name, ins):
                assert next(order) == name, name
                ins.then_inc(full, 1)

            def need_piece(name):
                n = PIECES.index(name)
                pe.wait_ge(loaded[n % TRUNK_SLOTS], trunk_loads(n))
                return piece(name)

            def need(sem, n):
                pe.wait_ge(s[sem], n)

            def project(fill, w, tiles, c0, rhs, nk):
                b = open_fill(fill)
                for i in range(tiles):
                    for k in range(nk):
                        mm = pe.matmul(b[:, i * T:(i + 1) * T], w[:, k, (c0 + i) * P:(c0 + i + 1) * P], rhs[:, k, :],
                                       start=(k == 0), stop=(k == nk - 1))
                close_fill(fill, mm)

            need("ident_ok", 1)
            need("par_in", 160)
            b = open_fill("par")
            close_fill("par", pe.transpose(b[:, 0:54], par_rows[0:54, :], ident[0:54, 0:54]))
            for n in range(4):
                b = open_fill(f"hT{n}")
                for i in range(2):
                    for t in range(TT):
                        need("xn_ok", t + 1)
                        k = 2 * n + i
                        mm = pe.transpose(b[:, i * T + t * P:i * T + (t + 1) * P], xn[:, t, k * P:(k + 1) * P], ident[:])
                close_fill(f"hT{n}", mm)
            wait_drained(pe, "hT0", "hT1", "hT2", "hT3")
            project("lora", need_piece("lora"), 2, 0, hT, KD)
            w = need_piece("rk")
            for i in range(2):
                project(f"rk{i}", w, 2, 2 * i, hT, KD)
            need("lora_in", 32)
            need("tanh_ok", 1)
            for i in range(2):
                b = open_fill(f"u{i}")
                for c in range(2):
                    mm = pe.matmul(b[:, c * T:(c + 1) * T], lora_up[0:64, (2 * i + c) * P:(2 * i + c + 1) * P], tanh_w,
                                   start=True, stop=True)
                close_fill(f"u{i}", mm)
            need("lora_ok", 2)
            for i in range(2):
                b = open_fill(f"a{i}")
                for c in range(2):
                    mm = pe.matmul(b[:, c * T:(c + 1) * T], lora_up[64:P, (2 * i + c) * P:(2 * i + c + 1) * P],
                                   lora[64:P, 0, :], start=True, stop=True)
                close_fill(f"a{i}", mm)
            for name in ("rr", "rv"):
                w = need_piece(name)
                for i in range(2):
                    project(f"{name}{i}", w, 2, 2 * i, hT, KD)
            need("ones_ok", 2)
            need("sq_ok", 4)
            for i in range(2):
                b = open_fill(f"ss{i}")
                close_fill(f"ss{i}", pe.matmul(b, head_ones[:], blk(12)[:, i * 512:(i + 1) * 512], start=True, stop=True))
            for name in ("aq", "ak"):
                w = need_piece(name)
                for i in range(2):
                    project(f"{name}{i}", w, 2, 2 * i, hT, KD)
            w = need_piece("av")
            for t in range(TT):
                b = open_fill(f"av{t}")
                for k in range(KD):
                    mm = pe.matmul(b, hT[:, k, t * P:(t + 1) * P], w[:, k, :], start=(k == 0), stop=(k == KD - 1))
                close_fill(f"av{t}", mm)
            w = need_piece("pool")
            for i in range(2):
                project(f"pool{i}", w, 2, 2 * i, hT, KD)
            need("v_ok", 4)
            for c in range(TT):
                b = open_fill(f"vn{c}")
                for t in range(CT):
                    mm = pe.transpose(b[:, t * P:(t + 1) * P], v_[:, t, c * P:(c + 1) * P], ident[:])
                close_fill(f"vn{c}", mm)
            for name, src, sem in (("bn", bt, "bt_ok"), ("kn", kt, "kt_ok")):
                need(sem, 1)
                b = open_fill(name)
                for t in range(CT):
                    mm = pe.transpose(b[:, t * P:(t + 1) * P], src[:, t, 0:P], ident[:])
                close_fill(name, mm)
            need("bonin_ok", 4)
            for i in range(2):
                b = open_fill(f"bon{i}")
                close_fill(f"bon{i}", pe.matmul(b, head_ones[:], blk(13)[:, i * 512:(i + 1) * 512], start=True, stop=True))
            need("ar_ok", 2)
            for n in range(16):
                c, h = divmod(n, H)
                rows = slice(64 * (h % 2), 64 * (h % 2) + 64)
                b = open_fill(f"sc{n}")
                both = ar[rows, h // 2, c, :, :].rearrange("p m t -> p (m t)")
                for m, left in enumerate((bt, kt)):
                    mm = pe.matmul(b[:, m * T:(m + 1) * T], left[rows, h // 2, c * P:(c + 1) * P], both,
                                   start=True, stop=True)
                close_fill(f"sc{n}", mm)
            wait_drained(pe, "aq0", "aq1", "ak0", "ak1")
            for n in range(6):
                b = open_fill(f"at{n}")
                for i, h in enumerate(attn_heads(n)):
                    rows = slice(64 * (h % 2), 64 * (h % 2) + 64)
                    if n < 4:
                        mm = pe.matmul(b[:, i * T:(i + 1) * T], qk[rows, 0, h // 2, P:T], qk[rows, 1, h // 2, :],
                                       start=True, stop=True)
                    else:
                        mm = pe.matmul(b[:, i * P:(i + 1) * P], qk[rows, 0, h // 2, 0:P], qk[rows, 1, h // 2, 0:P],
                                       start=True, stop=True)
                close_fill(f"at{n}", mm)
            for g in range(4):
                b = open_fill(f"L{g}")
                for i in range(4):
                    n = 4 * g + i
                    wait_drained(pe, f"sc{n}")
                    mm = pe.transpose(b[:, i * P:(i + 1) * P], sc[:, n, 0, :], ident[:])
                close_fill(f"L{g}", mm)

            def transpose_tri(name, g, source):
                b = open_fill(name)
                wait_drained(pe, source)
                for i in range(4):
                    mm = pe.transpose(b[:, i * P:(i + 1) * P], tri[:, 4 * g + i, :], ident[:])
                close_fill(name, mm)

            for g in range(4):
                transpose_tri(f"G1_{g}", g, f"L{g}")
            for size in LEVELS:
                for g in range(4):
                    b = open_fill(f"A{size}_{g}")
                    for i in range(4):
                        n = 4 * g + i
                        mm = pe.matmul(b[:, i * P:(i + 1) * P], sc[:, n, 0, :], tri[:, n, :], start=True, stop=True)
                    close_fill(f"A{size}_{g}", mm)
                for g in range(4):
                    b = open_fill(f"T{size}_{g}")
                    wait_drained(pe, f"G{size // 2}_{g}", f"A{size}_{g}")
                    for i in range(4):
                        n = 4 * g + i
                        mm = pe.matmul(b[:, i * P:(i + 1) * P], triT[:, n, :], triA[:, n, :], start=True, stop=True)
                    close_fill(f"T{size}_{g}", mm)
                for g in range(4):
                    transpose_tri(f"G{size}_{g}", g, f"T{size}_{g}")

            def pT(h):
                b = open_fill(f"pt{h}")
                need("prob_ok", 2)
                for j in range(3):
                    mm = pe.transpose(b[:, j * P:(j + 1) * P], prob[:, h, j * P:(j + 1) * P], ident[:])
                close_fill(f"pt{h}", mm)

            def pv(h):
                b = bank(f"o{h // 4}")
                if h % 4 == 0:
                    open_fill(f"o{h // 4}")
                wait_drained(pe, f"pt{h}")
                orow = slice(64 * (h % 2), 64 * (h % 2) + 64)
                c0 = (h // 2 % 2) * T
                head = slice(h * DH, (h + 1) * DH)
                if h == 0:
                    wait_drained(pe, "av0", "av1")
                pe.matmul(b[orow, c0:c0 + P], va[:, 0, head], probT[:, h % 2, 0:P], start=True, stop=True)
                for j in range(2):
                    mm = pe.matmul(b[orow, c0 + P:c0 + T], va[:, j, head], probT[:, h % 2, (1 + j) * P:(2 + j) * P],
                                   start=(j == 0), stop=(j == 1))
                return mm

            pT(0)
            pT(1)
            for h in range(H):
                mm = pv(h)
                if h % 4 == 3:
                    close_fill(f"o{h // 4}", mm)
                if h + 2 < H:
                    pT(h + 2)
            need("pool_in", 16)
            need("pool_ok", 4)
            for i, name in enumerate(("pw", "pw1")):
                b = open_fill(name)
                for c in range(2):
                    mm = pe.matmul(b[:, c * T:(c + 1) * T], poolw[:, 2 * i + c, :], pz[:, 2 * i + c, :],
                                   start=True, stop=True)
                close_fill(name, mm)

            def heads_out(b, h):
                return b[:, h * DH:(h + 1) * DH]

            wait_drained(pe, "vn0", "vn1")
            b = open_fill("X0")
            for h in range(H):
                mm = pe.matmul(heads_out(b, h), sc[:, h, 2, :], vn[:, 0, h * DH:(h + 1) * DH], start=True, stop=True)
            close_fill("X0", mm)

            def gate_half(br, half):
                w = need_piece(f"g{br}{half}")
                for i, part in enumerate("ab"):
                    project(f"g{br}{half}{part}", w, 2, 2 * i, hT, KD)

            def branch(br, y):
                w = need_piece(f"p{br}")
                for n in range(4):
                    project(f"p{br}{n}", w, 2, 2 * n, y, CT)

            gate_half("C", 0)
            wait_drained(pe, "X0", "G64_0", "G64_1", "G64_2", "G64_3")
            b = open_fill("SA0")
            for h in range(H):
                mm = pe.matmul(heads_out(b, h), triT[:, h, :], xs[0][:, h * DH:(h + 1) * DH], start=True, stop=True)
            close_fill("SA0", mm)
            gate_half("C", 1)
            wait_drained(pe, "SA0", "bn", "kn")
            b = open_fill("St")
            for h in range(H):
                o = b[64 * (h % 2):64 * (h % 2) + 64, (h // 2) * DH:(h // 2 + 1) * DH]
                head = slice(h * DH, (h + 1) * DH)
                pe.matmul(o, bkn[:, 0, head], sa[0][:, head], start=True, stop=False)
                mm = pe.matmul(o, bkn[:, 1, head], vn[:, 0, head], start=False, stop=True)
            close_fill("St", mm)
            wait_drained(pe, "pw", "pw1")
            branch("C", y_pool)
            wait_drained(pe, "St")
            for parity, name in enumerate(("X1e", "X1o")):
                b = open_fill(name)
                rows = slice(64 * parity, 64 * parity + 64)
                for i in range(4):
                    h = 2 * i + parity
                    pe.matmul(b[:, i * DH:(i + 1) * DH], sc[:, H + h, 2, :], vn[:, 1, h * DH:(h + 1) * DH],
                              start=True, stop=False)
                    mm = pe.matmul(b[:, i * DH:(i + 1) * DH], ar[rows, i, 1, 0, :], state[rows, i, :],
                                   start=False, stop=True)
                close_fill(name, mm)
            gate_half("A", 0)
            wait_drained(pe, "X1e", "X1o")
            b = open_fill("SA1")
            for h in range(H):
                mm = pe.matmul(heads_out(b, h), triT[:, H + h, :], xs[1][:, h * DH:(h + 1) * DH], start=True, stop=True)
            close_fill("SA1", mm)
            gate_half("A", 1)
            wait_drained(pe, "SA1")
            b = open_fill("Y0")
            for h in range(H):
                o = b[64 * (h % 2):64 * (h % 2) + 64, (h // 2) * P:(h // 2 + 1) * P]
                head = slice(h * DH, (h + 1) * DH)
                pe.matmul(o, sa[0][:, head], sc[:, h, 1, :], start=True, stop=False)
                mm = pe.matmul(o, vn[:, 0, head], sc[:, h, 3, :], start=False, stop=True)
            close_fill("Y0", mm)
            for parity, name in enumerate(("Y1e", "Y1o")):
                b = open_fill(name)
                rows = slice(64 * parity, 64 * parity + 64)
                for i in range(4):
                    h = 2 * i + parity
                    o = b[rows, i * P:(i + 1) * P]
                    head = slice(h * DH, (h + 1) * DH)
                    pe.matmul(o, sa[1][:, head], sc[:, H + h, 1, :], start=True, stop=False)
                    pe.matmul(o, vn[:, 1, head], sc[:, H + h, 3, :], start=False, stop=False)
                    mm = pe.matmul(o, state[rows, i, :], ar[rows, i, 1, 1, :], start=False, stop=True)
                close_fill(name, mm)
            wait_drained(pe, "o0", "o1")
            branch("A", y_attn)
            wait_drained(pe, "Y0", "Y1e", "Y1o")
            for i in range(2):
                b = open_fill(f"mu{i}")
                close_fill(f"mu{i}", pe.matmul(b, head_ones[:], blk(8)[:, i * 512:(i + 1) * 512], start=True, stop=True))
            gate_half("B", 0)
            need("ysq_ok", 1)
            for i in range(2):
                b = open_fill(f"va{i}")
                close_fill(f"va{i}", pe.matmul(b, head_ones[:], blk(12)[:, i * 512:(i + 1) * 512], start=True, stop=True))
            need("gateup_in", 16)
            need("sigg_ok", 1)
            for i in range(2):
                b = open_fill(f"gg{i}")
                for c in range(2):
                    mm = pe.matmul(b[:, c * T:(c + 1) * T], gate_up[:, (2 * i + c) * P:(2 * i + c + 1) * P], sig_g[:],
                                   start=True, stop=True)
                close_fill(f"gg{i}", mm)
            gate_half("B", 1)
            wait_drained(pe, "gg0", "gg1")
            branch("B", y_rwkv)
            need("merged_ok", 8)
            for half in range(2):
                w = need_piece(f"wo{half}")
                for t in range(TT):
                    name = f"wo{2 * half + t}"
                    b = open_fill(name)
                    for k in range(KD):
                        mm = pe.matmul(b, merged[:, k, t * P:(t + 1) * P], w[:, k, :], start=(k == 0), stop=(k == KD - 1))
                    close_fill(name, mm)
            for n in range(4):
                b = open_fill(f"h2T{n}")
                for i in range(2):
                    for t in range(TT):
                        need("h2_ok", t + 1)
                        k = 2 * n + i
                        mm = pe.transpose(b[:, i * T + t * P:i * T + (t + 1) * P], h2[:, t, k * P:(k + 1) * P], ident[:])
                close_fill(f"h2T{n}", mm)
            wait_drained(pe, "h2T0", "h2T1", "h2T2", "h2T3")
            need("rw_in", 32)
            b = open_fill("rt")
            for t in range(TT):
                for k in range(KD):
                    mm = pe.matmul(b[:, t * 36:(t + 1) * 36], hT[:, k, t * P:(t + 1) * P], router_w[:, k, :],
                                   start=(k == 0), stop=(k == KD - 1))
            close_fill("rt", mm)
            for t in range(TT):
                for half in range(2):
                    mm = pe.matmul(ps[:, 2 * t + half, :], ident[:], x2[:, t, half * 512:(half + 1) * 512],
                                   start=True, stop=False, skip_group_check=True)
            need("cs_in", 1)
            b = open_fill("cs")
            assigned = rtmp[:, 0:TT * NE].rearrange("p (t n) -> p t n", t=TT)
            pe.matmul(b[:, 0:32], causal[:, 0, :], assigned[:, 0, :], start=True, stop=True)
            pe.matmul(b[:, 32:64], causal[:, 0, :], assigned[:, 1, :], start=True, stop=False)
            pe.matmul(b[:, 32:64], ones[:], assigned[:, 0, :], start=False, stop=True)
            pe.matmul(b[:, 64:96], ones[:], assigned[:, 0, :], start=True, stop=False)
            mm = pe.matmul(b[:, 64:96], ones[:], assigned[:, 1, :], start=False, stop=True)
            close_fill("cs", mm)
            assert next(order, None) is None

            BA, BB, BC, BD = 4, 5, 6, 7

            pe.wait_ge(s["quads_ok"], 1)
            last_quad = pe.value_load(last_quad_i[0:1, 0:1], min_val=NE // 4 - 1, max_val=NE // 4 * ROUNDS - 1)

            def gather(c):
                d = ps[:, BD, :].rearrange("p (k b r c) -> p k b r c", k=2, b=2, r=2)
                for kk in range(2):
                    k = 2 * c + kk
                    for r, src in enumerate((h2hi, h2lo)):
                        for t in range(TT):
                            mm = pe.matmul(d[:, kk, :, r, :], src[:, t, k * P:(k + 1) * P], selp[:, t, :, :],
                                           start=(t == 0), stop=(t == TT - 1))
                mm.then_inc(s["gathered"], 1)

            def scatter(b):
                for part in (yhi, ylo):
                    for t in range(TT):
                        for half in range(2):
                            mm = pe.matmul(ps[:, 2 * t + half, :], selT[b][:, t * P:(t + 1) * P],
                                           part[:, half * 512:(half + 1) * 512], start=False, stop=False,
                                           skip_group_check=True)
                mm.then_inc(s["scattered"], 1)

            def expert(i, p, b, last):
                n = i * 4 + (2 * p + b)
                more = not (last and p == 1)
                m = i * 24 + (12 * p + 6 * b)
                chunks_in = i * 8 + (4 * (p + 1) + (2 * b if more else 0))

                def split_slot(j):
                    return (12 * p + 6 * b + j) % SPLIT

                if b == 0:
                    pe.wait_ge(s["xg_ok"], i * 8 + 4 * (p + 1))
                for w, dst in ((0, BA), (1, BB)):
                    pe.wait_ge(s["ylo_ok"], n * 2 + (w + 1))
                    for j in (2 * w, 2 * w + 1):
                        pe.wait_ge(s["lo_ok"], m + (j + 1))
                        for kk in range(4):
                            k = 4 * (j % 2) + kk
                            for part in (whi, wlo):
                                mm = pe.matmul(ps[:, dst, :], xg[p][:, k, b, :, :].rearrange("p r c -> p (r c)"),
                                               part[:, split_slot(j), kk, :], start=(k == 0 and part is whi),
                                               stop=(k == KD - 1 and part is wlo))
                        mm.then_inc(s["half_done"], 1)
                    if w == 0:
                        pe.wait_ge(s["dup_ok"], n + 1)
                        pe.wait_ge(s["xg_ok"], chunks_in)
                        for t in range(TT):
                            pe.transpose(ps[:, BD, t * P:(t + 1) * P], seldup[b][:, t, :], ident[:])
                        for t in range(TT):
                            mm = pe.matmul(ps[:, BD, T:T + 1], seldup[b][:, t, :], wcol[:, b, t:t + 1],
                                           start=(t == 0), stop=(t == TT - 1))
                        mm.then_inc(s["selT_full"], 1)
                pe.wait_ge(s["hs_ok"], n * 2 + 1)
                for c in range(HC):
                    pe.matmul(ps[:, BC, c * CAP:(c + 1) * CAP], hs[:, 0, c * P:(c + 1) * P], fold[:], start=True, stop=True)
                pe.wait_ge(s["selT_ok"], n + 1)
                if more:
                    pe.wait_ge(s["selp_ok"], i * 2 + (p + 2))
                    gather(2 * b)
                pe.wait_ge(s["hs_ok"], n * 2 + 2)
                for c in range(HC):
                    mm = pe.matmul(ps[:, BC, (HC + c) * CAP:(HC + c + 1) * CAP], hs[:, 1, c * P:(c + 1) * P], foldw[b][:],
                                   start=True, stop=True)
                mm.then_inc(s["folded"], 1)
                pe.wait_ge(s["ylo_ok"], n * 2 + 2)
                scatter(1 - b)
                pe.wait_ge(s["hidlo_ok"], n + 1)
                for j, dst in ((4, BA), (5, BB)):
                    pe.wait_ge(s["lo_ok"], m + (j + 1))
                    for k in range(HC):
                        for part in (whi, wlo):
                            mm = pe.matmul(ps[:, dst, :], hidden[:, k, :, :].rearrange("p r c -> p (r c)"),
                                           part[:, split_slot(j), k, :], start=(k == 0 and part is whi),
                                           stop=(k == HC - 1 and part is wlo))
                    mm.then_inc(s["half_done"], 1)
                if more:
                    pe.wait_ge(s["xg_ok"], chunks_in + 1)
                    gather(2 * b + 1)

            pe.wait_ge(s["selp_ok"], 1)
            pe.wait_ge(s["h2r_ok"], 2)
            for c in range(4):
                if c:
                    pe.wait_ge(s["xg_ok"], c)
                gather(c)
            with pe.Fori(0, last_quad) as i:
                for p in range(2):
                    for b in range(2):
                        expert(i, p, b, False)
            for p in range(2):
                for b in range(2):
                    expert(last_quad, p, b, True)
            pe.wait_ge(s["ylo_ok"], last_quad * 8 + 10)
            scatter(1)

        @block.scalar
        def _(a):
            def free(ins, name):
                ins.then_inc(drained[BANK[name]], 1)

            def need(sem, n):
                a.wait_ge(s[sem], n)

            def move(dst, name, cols=512):
                wait_full(a, name)
                free(a.activation(dst, bank(name)[:, 0:cols], ACT.Copy), name)

            def high_part(m, q, i=None):
                nxt = q + SPLIT
                j = nxt % HALVES
                a.wait_ge(raw_in[j], i * 64 + 16 * (nxt // HALVES + 1))
                a.activation(whi[:, q % SPLIT, :, :].rearrange("p k c -> p (k c)"),
                             ring[:, j * HALF:(j + 1) * HALF], ACT.Copy).then_inc(s["hi_ok"], 1)

            def first_high(j):
                a.wait_ge(raw_in[j], 16)
                a.activation(whi[:, j, :, :].rearrange("p k c -> p (k c)"),
                             ring[:, j * HALF:(j + 1) * HALF], ACT.Copy).then_inc(s["hi_ok"], 1)

            need("x_in", 16)
            need("const_ok", 1)
            for t in range(TT):
                a.activation(blk(4 + t), x_sb[:, t, :], ACT.Square, accum_out=small[:, t:t + 1]).then_inc(s["ssq"], 1)
            need("ssq", 2)
            a.activation(small[:, 2:4], small[:, 0:2], ACT.Sqrt, scale=1.0 / D, bias=small[:, 4:5]).then_inc(s["ssq"], 1)
            wait_drained(a, "par")
            for n in (0, 2):
                wait_full(a, f"hT{n}")
                for i in range(2):
                    k = 2 * n + i
                    ins = a.activation(hT[:, k, :], bank(f"hT{n}")[:, i * T:(i + 1) * T], ACT.Copy, scale=pcol("norm1_g", k))
                free(ins, f"hT{n}")
            for n in range(4):
                wait_full(a, f"hT{n}")
            move(blk(0)[:, 0:512], "lora")
            for i in range(2):
                move(blk(4)[:, i * 512:(i + 1) * 512], f"rk{i}")
            need("lora_ok", 2)
            a.activation(tanh_w, lora[0:64, 0, :], ACT.Tanh).then_inc(s["tanh_ok"], 1)
            a.activation(sig_g[:], lora[:, 1, :], ACT.Sigmoid).then_inc(s["sigg_ok"], 1)
            for i in range(2):
                wait_full(a, f"u{i}")
                for c in range(2):
                    ct = 2 * i + c
                    ins = a.activation(logw[:, ct, :], bank(f"u{i}")[:, c * T:(c + 1) * T], ACT.Sigmoid, bias=pcol("w0", ct))
                free(ins, f"u{i}")
            for i in range(2):
                wait_full(a, f"a{i}")
                for c in range(2):
                    ct = 2 * i + c
                    ins = a.activation(iclr[:, ct, :], bank(f"a{i}")[:, c * T:(c + 1) * T], ACT.Sigmoid, bias=pcol("a0", ct))
                free(ins, f"a{i}")
            need("k_ok", 4)
            for ct in range(CT):
                a.activation(sq[:, ct, :], k_[:, ct, :], ACT.Square, scale=pcol("k_k", ct)).then_inc(s["sq_ok"], 1)
            for i in range(2):
                move(blk(1)[:, i * 512:(i + 1) * 512], f"rr{i}")
            for i in range(2):
                move(blk(2)[:, i * 512:(i + 1) * 512], f"rv{i}")
            wait_drained(a, "ss0", "ss1")
            a.activation(blk(12), blk(12), ACT.Sqrt).then_inc(s["norm_ok"], 1)
            need("logw_ok", 2)
            a.activation(blk(9), blk(8), ACT.Exp).then_inc(s["exps_ok"], 1)
            a.activation(blk(10), blk(8), ACT.Exp, scale=-1.0).then_inc(s["exps_ok"], 1)
            a.activation(blk(7), blk(7), ACT.Exp).then_inc(s["exps_ok"], 1)
            a.activation(small[:, 8:12], small[:, 8:12], ACT.Exp).then_inc(s["exps_ok"], 1)
            for i in range(2):
                move(qk[:, 0, 2 * i:2 * i + 2, :].rearrange("p c t -> p (c t)"), f"aq{i}")
            for i in range(2):
                move(qk[:, 1, 2 * i:2 * i + 2, :].rearrange("p c t -> p (c t)"), f"ak{i}")
            for t in range(TT):
                move(va[:, t, :], f"av{t}")
            for i in range(2):
                move(pz[:, 2 * i:2 * i + 2, :].rearrange("p c t -> p (c t)"), f"pool{i}")
            for c in range(2):
                move(vn[:, c, :], f"vn{c}")
            move(bkn[:, 0, :], "bn")
            move(bkn[:, 1, :], "kn")
            need("smax_ok", 3)
            for c in range(TT):
                for h in range(H):
                    p = prob[:, h, 0:P] if c == 0 else prob[:, h, P:3 * P]
                    ins = a.activation(p, p, ACT.Exp, scale=2.0 ** -(h + 1), bias=amax[:, c, h:h + 1],
                                       accum_out=asum[:, c, h:h + 1])
            ins.then_inc(s["exp_ok"], 1)

            for g in range(4):
                wait_full(a, f"G1_{g}")
                free(a.activation(blk(10 + g // 2)[:, (g % 2) * 512:(g % 2 + 1) * 512], bank(f"G1_{g}"), ACT.Copy),
                     f"G1_{g}")
            for size in LEVELS:
                for g in range(4):
                    wait_full(a, f"A{size}_{g}")
                    free(a.activation(blk(12 + g // 2)[:, (g % 2) * 512:(g % 2 + 1) * 512], bank(f"A{size}_{g}"), ACT.Copy),
                         f"A{size}_{g}")
                for g in range(4):
                    wait_full(a, f"G{size}_{g}")
                    free(a.activation(blk(10 + g // 2)[:, (g % 2) * 512:(g % 2 + 1) * 512], bank(f"G{size}_{g}"), ACT.Copy),
                         f"G{size}_{g}")
            need("prob_ok", 2)
            for h in range(H):
                wait_full(a, f"pt{h}")
                free(a.activation(probT[:, h % 2, :], bank(f"pt{h}")[:, 0:384], ACT.Copy), f"pt{h}")
            for i in range(2):
                move(bt[:, 2 * i:2 * i + 2, :].rearrange("p c t -> p (c t)"), f"o{i}")
            for i, name in enumerate(("pw", "pw1")):
                wait_full(a, "pw1")
                for c in range(2):
                    ct = 2 * i + c
                    ins = a.activation(pz[:, ct, :], bank(name)[:, c * T:(c + 1) * T], ACT.Copy, scale=pcol("pool_scale", ct))
                free(ins, name)
            move(xs[0], "X0")

            def gate(br, half):
                for i, part in enumerate("ab"):
                    name = f"g{br}{half}{part}"
                    wait_full(a, name)
                    k = 4 * half + 2 * i
                    free(a.activation(gates[:, k:k + 2, :].rearrange("p k t -> p (k t)"), bank(name), ACT.Sigmoid), name)

            gate("C", 0)
            move(sa[0], "SA0")
            gate("C", 1)
            for parity, name in enumerate(("X1e", "X1o")):
                wait_full(a, name)
                free(a.activation(xs[1].rearrange("p (i q d) -> p i q d", q=2, d=DH)[:, :, parity, :],
                                  bank(name)[:, 0:256].rearrange("p (i d) -> p i d", d=DH), ACT.Copy), name)
            wait_drained(a, "pC0", "pC1", "pC2", "pC3")
            gate("A", 0)
            move(sa[1], "SA1")
            gate("A", 1)
            wait_full(a, "Y0")
            free(a.activation(y_raw[:, :, 0:P], bank("Y0").rearrange("p (c t) -> p c t", c=CT), ACT.Copy), "Y0")
            for parity, name in enumerate(("Y1e", "Y1o")):
                rows = slice(64 * parity, 64 * parity + 64)
                wait_full(a, name)
                free(a.activation(y_raw[rows, :, P:T], ps[rows, BANK[name], :].rearrange("p (c t) -> p c t", c=CT), ACT.Copy),
                     name)
            need("merged_ok", 4)
            gate("B", 0)
            wait_drained(a, "mu0", "mu1")
            a.activation(blk(12), blk(9), ACT.Square).then_inc(s["ysq_ok"], 1)
            for i in range(2):
                wait_full(a, f"va{i}")
                free(a.activation(blk(13)[:, i * 512:(i + 1) * 512], bank(f"va{i}"), ACT.Sqrt, scale=1.0 / DH,
                                  bias=small[:, 5:6]), f"va{i}")
            gate("B", 1)
            wait_full(a, "gB1b")
            wait_drained(a, "gg0", "gg1")
            first_high(0)
            first_high(1)
            wait_drained(a, "wo0", "wo1", "wo2", "wo3")
            for t in range(TT):
                a.activation(h2n[:, t, :], x2[:, t, :], ACT.Square, accum_out=small[:, 12 + t:13 + t]).then_inc(s["x2ssq"], 1)
            need("x2ssq", 2)
            a.activation(small[:, 14:16], small[:, 12:14], ACT.Sqrt, scale=1.0 / D, bias=small[:, 4:5]).then_inc(s["x2ssq"], 1)
            first_high(2)
            first_high(3)
            need("h2_ok", 2)
            for t in range(TT):
                a.activation(h2hi[:, t, :], h2[:, t, :], ACT.Copy).then_inc(s["h2hi_ok"], 1)
            for n in range(4):
                wait_full(a, f"h2T{n}")
                free(a.activation(hT[:, 2 * n:2 * n + 2, :].rearrange("p k t -> p (k t)"), bank(f"h2T{n}"), ACT.Copy),
                     f"h2T{n}")
            need("eexp_in", 1)
            a.activation(small[:, 32:40], small[:, 32:40], ACT.Exp).then_inc(s["eexp_ok"], 1)
            need("eexp_in", 2)
            a.activation(small[:, 24:26], small[:, 24:26], ACT.Exp).then_inc(s["eexp_ok"], 1)
            need("quads_ok", 1)
            last_quad = a.value_load(last_quad_i[0:1, 0:1], min_val=NE // 4 - 1, max_val=NE // 4 * ROUNDS - 1)

            def move_gathered(p, c, count):
                a.wait_ge(s["gathered"], count)
                a.activation(xg[p][:, 2 * c:2 * c + 2, :, :, :].rearrange("p k b r c -> p (k b r c)"), ps[:, 7, :],
                             ACT.Copy).then_inc(s["xg_ok"], 1)

            def expert(i, p, b, last):
                n = i * 4 + (2 * p + b)
                more = not (last and p == 1)
                h0 = 12 * p + 6 * b
                count = i * 8 + (4 * (p + 1) + 2 * b + 1)

                def split_ahead(j):
                    if last and h0 + j + SPLIT >= 24:
                        return
                    high_part(i * 24 + (h0 + j), h0 + j, i)

                def done(j):
                    a.wait_ge(s["half_done"], i * 24 + (h0 + j + 1))

                done(0)
                split_ahead(0)
                done(1)
                a.activation(hs[:, 0, :], ps[:, 4, :], ACT.Copy).then_inc(s["hs_ok"], 1)
                split_ahead(1)
                done(2)
                split_ahead(2)
                done(3)
                a.activation(hs[:, 1, :], ps[:, 5, :], ACT.Copy).then_inc(s["hs_ok"], 1)
                split_ahead(3)
                if more:
                    move_gathered(1 - p, 2 * b, count)
                a.wait_ge(s["folded"], n + 1)
                a.activation(silu, ps[:, 6, 0:T], ACT.Silu).then_inc(s["silu_ok"], 1)
                a.wait_ge(s["hid_ok"], n + 1)
                a.activation(hidden[:, :, 0, :], hid.rearrange("p (k c) -> p k c", k=HC), ACT.Copy).then_inc(
                    s["hidhi_ok"], 1)
                done(4)
                a.activation(yhi[:, 0:512], ps[:, 4, :], ACT.Copy).then_inc(s["yhi_ok"], 1)
                split_ahead(4)
                done(5)
                a.activation(yhi[:, 512:1024], ps[:, 5, :], ACT.Copy).then_inc(s["yhi_ok"], 1)
                if more:
                    move_gathered(1 - p, 2 * b + 1, count + 1)
                split_ahead(5)

            for c in range(4):
                move_gathered(0, c, c + 1)
            with a.Fori(0, last_quad) as i:
                for p in range(2):
                    for b in range(2):
                        expert(i, p, b, False)
            for p in range(2):
                for b in range(2):
                    expert(last_quad, p, b, True)
            a.wait_ge(s["scattered"], last_quad * 4 + 5)
            for t in range(TT):
                a.activation(h2[:, t, :], ps[:, 2 * t:2 * t + 2, :].rearrange("p b c -> p (b c)"), ACT.Square,
                             accum_out=small[:, 16 + t:17 + t]).then_inc(s["fssq"], 1)
            need("fssq", 2)
            a.activation(small[:, 18:20], small[:, 16:18], ACT.Sqrt, scale=1.0 / D, bias=small[:, 4:5]).then_inc(s["fssq"], 1)

        @block.vector
        def _(v):
            chain = [0]

            def link(ins):
                chain[0] += 1
                ins.then_inc(s["dve"], 1)
                v.wait_ge(s["dve"], chain[0])

            def free(ins, name):
                ins.then_inc(drained[BANK[name]], 1)

            def need(sem, n):
                v.wait_ge(s[sem], n)

            v.memset(small[:, 4:5], RMS_EPS)
            v.memset(small[:, 5:6], LNX_EPS).then_inc(s["const_ok"], 1)
            wait_full(v, "par")
            free(v.tensor_copy(par[:], bank("par")[:, 0:54]), "par")
            wait_drained(v, "par")
            link(v.tensor_scalar(small[:, 20:24], par[:, pc["k_a"]:pc["k_a"] + 4], -1.0, 1.0, ALU.mult, ALU.add))
            need("x_in", 16)
            need("ssq", 3)
            link(v.reciprocal(small[:, 6:8], small[:, 2:4]))
            for t in range(TT):
                v.tensor_scalar(xn[:, t, :], x_sb[:, t, :], small[:, 6 + t:7 + t], None, ALU.mult).then_inc(s["xn_ok"], 1)
            for n in (1, 3):
                wait_full(v, f"hT{n}")
                for i in range(2):
                    k = 2 * n + i
                    ins = v.tensor_scalar(hT[:, k, :], bank(f"hT{n}")[:, i * T:(i + 1) * T], pcol("norm1_g", k), None, ALU.mult)
                free(ins, f"hT{n}")

            def token_shift(z, d, tiles, mu0, sem):
                v.tensor_tensor(d[:, :, 1:T], z[:, :, 0:T - 1], z[:, :, 1:T], ALU.subtract)
                link(v.tensor_scalar(d[:, :, 0:1], z[:, :, 0:1], -1.0, None, ALU.mult))
                for c in range(tiles):
                    v.scalar_tensor_tensor(out=z[:, c, :], in0=d[:, c, :], scalar=pcol("rwkv_mu", mu0 + c),
                                           in1=z[:, c, :], op0=ALU.mult, op1=ALU.add).then_inc(s[sem], 1)

            wait_drained(v, "lora")
            token_shift(lora, dlora, 2, 12, "lora_ok")
            wait_drained(v, "rk0")
            wait_drained(v, "rk1")
            token_shift(k_, dz, CT, 4, "k_ok")
            wait_drained(v, "u0")
            wait_drained(v, "u1")
            need("ones_ok", 4)
            link(v.tensor_scalar(blk(5), blk(5), -DECAY_SCALE, None, ALU.mult))
            link(v.tensor_tensor_scan(blk(7), scan_ones, blk(5), 0.0, ALU.mult, ALU.add))
            lp8 = chunks(blk(7))
            v.tensor_tensor(chunks(blk(8)), lp8, lp8[:, :, 63:64].to_broadcast([P, 8, P]), ALU.subtract).then_inc(
                s["logw_ok"], 1)
            need("logw_ok", 1)
            v4 = lambda ap: ap.rearrange("p (c k t) -> p c k t", c=CT, k=TT)
            link(v.tensor_tensor(small[:, 8:12], v4(blk(8))[:, :, 0, P - 1], v4(blk(7))[:, :, 1, 63], ALU.add))
            v.tensor_tensor(blk(7), blk(8), blk(5), ALU.subtract).then_inc(s["logw_ok"], 1)
            need("k_ok", 4)
            for ct in range(CT):
                v.tensor_scalar(kk[:, ct, :], k_[:, ct, :], pcol("k_k", ct), None, ALU.mult).then_inc(s["kk_ok"], 1)
            wait_drained(v, "rr0")
            wait_drained(v, "rr1")
            token_shift(r_, dz, CT, 0, "r_ok")
            wait_drained(v, "rv0")
            wait_drained(v, "rv1")
            need("r_ok", 4)
            token_shift(v_, dz, CT, 8, "v_ok")
            for i in range(2):
                wait_full(v, f"ss{i}")
                if i == 0:
                    wait_full(v, "ss1")
                ins = v.tensor_scalar(blk(12)[:, i * 512:(i + 1) * 512], bank(f"ss{i}"), 1e-24, None, ALU.max)
                free(ins, f"ss{i}")
            need("norm_ok", 1)
            link(v.reciprocal(blk(12), blk(12)))
            need("kk_ok", 4)
            link(v.tensor_tensor(blk(11), blk(11), blk(12), ALU.mult))
            need("exps_ok", 4)
            ar8 = ar[:, :, :, :, :].rearrange("p c k m t -> p (c k) m t")
            v.scalar_tensor_tensor(out=ar8[:, :, 0, :], in0=chunks(blk(11)), scalar=-1.0, in1=chunks(blk(7)),
                                   op0=ALU.mult, op1=ALU.mult).then_inc(s["ar_ok"], 1)
            v.tensor_tensor(ar8[:, :, 1, :], chunks(blk(1)), chunks(blk(9)), ALU.mult).then_inc(s["ar_ok"], 1)
            wait_drained(v, "a0")
            wait_drained(v, "a1")
            link(v.tensor_tensor(blk(13), blk(11), blk(6), ALU.mult))
            flat = lambda t3: t3[:, :, :].rearrange("p c t -> p (c t)")
            v.tensor_tensor(flat(bt), blk(13), blk(10), ALU.mult).then_inc(s["bt_ok"], 1)
            need("v_ok", 4)
            for ct in range(CT):
                ins = v.tensor_scalar(kprime[:, ct, :], iclr[:, ct, :], pcol("k_a", ct), small[:, 20 + ct:21 + ct],
                                      ALU.mult, ALU.add)
            link(ins)
            link(v.tensor_tensor(blk(3), blk(3), blk(4), ALU.mult))
            v.tensor_tensor(flat(kt), blk(3), blk(10), ALU.mult).then_inc(s["kt_ok"], 1)
            for ct in range(CT):
                v.scalar_tensor_tensor(out=tmp[:, ct, :], in0=r_[:, ct, :], scalar=pcol("r_k", ct), in1=kprime[:, ct, :],
                                       op0=ALU.mult, op1=ALU.mult).then_inc(s["bonin_ok"], 1)
            for i in range(2):
                wait_full(v, f"bon{i}")
                ins = v.tensor_tensor(flat(bonus)[:, i * 512:(i + 1) * 512], bank(f"bon{i}"),
                                      blk(2)[:, i * 512:(i + 1) * 512], ALU.mult)
                free(ins, f"bon{i}")
            wait_drained(v, "pool0")
            wait_drained(v, "pool1")
            need("misc_ok", 14)
            link(v.reciprocal(count_inv[:], count_inv[:]))
            for gi in range(CT):
                src, bufs, step = pz[:, gi, :], (pool_a, pool_b), 1
                for j in range(gi + 1):
                    dst = bufs[j % 2]
                    v.tensor_tensor(dst[:, step:T], src[:, step:T], src[:, 0:T - step], ALU.add)
                    link(v.tensor_copy(dst[:, 0:step], src[:, 0:step]))
                    src, step = dst, 2 * step
                win = step
                other = bufs[(gi + 1) % 2]
                link(v.tensor_tensor(other[:, 0:win], src[:, 0:win], count_inv[:, gi, 0:win], ALU.mult))
                v.tensor_tensor(pz[:, gi, 0:win], other[:, 0:win], pz[:, gi, 0:win], ALU.subtract)
                v.scalar_tensor_tensor(out=pz[:, gi, win:T], in0=src[:, win:T], scalar=1.0 / win,
                                       in1=pz[:, gi, win:T], op0=ALU.mult, op1=ALU.subtract).then_inc(s["pool_ok"], 1)
                need("pool_ok", gi + 1)
            need("masks_ok", 4)
            flat_mask = causal[:, :, :].rearrange("p m t -> p (m t)")
            wait_full(v, "bon1")
            need("tanh_ok", 1)
            need("sigg_ok", 1)
            need("sq_ok", 4)
            for n in range(16):
                wait_full(v, f"sc{n}")
                ins = v.tensor_tensor(sc[:, n, :, :].rearrange("p m t -> p (m t)"), bank(f"sc{n}"), flat_mask, ALU.mult)
                free(ins, f"sc{n}")
            need("dist_ok", 1)
            for n in range(6):
                wait_full(v, f"at{n}")
                for i, h in enumerate(attn_heads(n)):
                    slope = 2.0 ** -(h + 1)
                    if n < 4:
                        ins = v.scalar_tensor_tensor(out=prob[:, h, P:3 * P], in0=bank(f"at{n}")[:, i * T:(i + 1) * T],
                                                     scalar=DH ** -0.5 / slope, in1=dist[:], op0=ALU.mult, op1=ALU.subtract)
                    else:
                        ins = v.scalar_tensor_tensor(out=prob[:, h, 0:P], in0=bank(f"at{n}")[:, i * P:(i + 1) * P],
                                                     scalar=DH ** -0.5 / slope, in1=dist[:, P:T], op0=ALU.mult,
                                                     op1=ALU.subtract)
                free(ins, f"at{n}")
            wait_drained(v, *(f"at{n}" for n in range(2, 6)))
            v.tensor_reduce(amax[:, 0, :], prob[:, :, 0:P], AX.X, ALU.max).then_inc(s["smax_ok"], 1)
            v.tensor_reduce(amax[:, 1, :], prob[:, :, P:3 * P], AX.X, ALU.max).then_inc(s["smax_ok"], 1)
            need("smax_ok", 2)
            v.tensor_tensor(amax[:], amax[:], slopes[:], ALU.mult).then_inc(s["smax_ok"], 1)
            need("levels_ok", 7)

            def fill_blocks(name, g, lev):
                wait_full(v, name)
                mask = level_mask[:, lev, :].bitcast(I32).unsqueeze(1).to_broadcast([P, 4, P])
                return v.copy_predicated(tri[:, 4 * g:4 * g + 4, :], mask, bank(name).rearrange("p (n t) -> p n t", n=4))

            for g in range(4):
                link(v.tensor_copy(tri[:, 4 * g:4 * g + 4, :], ident[:, :].unsqueeze(1).to_broadcast([P, 4, P])))
            for g in range(4):
                free(fill_blocks(f"L{g}", g, 0), f"L{g}")
            need("exp_ok", 1)
            link(v.reciprocal(asum[:], asum[:]))
            rs = asum[:, :, :]
            v.tensor_tensor(prob[:, :, 0:P], prob[:, :, 0:P], rs[:, 0, :].unsqueeze(2).to_broadcast([P, H, P]),
                            ALU.mult).then_inc(s["prob_ok"], 1)
            v.tensor_tensor(prob[:, :, P:3 * P], prob[:, :, P:3 * P], rs[:, 1, :].unsqueeze(2).to_broadcast([P, H, 2 * P]),
                            ALU.mult).then_inc(s["prob_ok"], 1)
            for lev, size in enumerate(LEVELS):
                for g in range(4):
                    free(fill_blocks(f"T{size}_{g}", g, lev + 1), f"T{size}_{g}")
            wait_full(v, "St")
            for ct in range(CT):
                ins = v.tensor_scalar(state[:, ct, :], bank("St")[:, ct * DH:(ct + 1) * DH], small[:, 8 + ct:9 + ct], None,
                                      ALU.mult)
            free(ins, "St")

            def merge(br):
                for n in range(4):
                    name = f"p{br}{n}"
                    wait_full(v, name)
                    gsl = gates[:, 2 * n:2 * n + 2, :].rearrange("p k t -> p (k t)")
                    msl = merged[:, 2 * n:2 * n + 2, :].rearrange("p k t -> p (k t)")
                    wait_drained(v, f"g{br}{n // 2}{'ab'[n % 2]}")
                    if br == "C":
                        free(v.tensor_tensor(msl, gsl, bank(name), ALU.mult), name)
                        continue
                    free(v.tensor_tensor(gsl, gsl, bank(name), ALU.mult), name)
                    wait_drained(v, name)
                    v.tensor_tensor(msl, msl, gsl, ALU.add).then_inc(s["merged_ok"], 1)

            wait_full(v, "o1")
            merge("C")
            wait_drained(v, "pC0", "pC1", "pC2", "pC3")
            merge("A")
            wait_drained(v, "Y0")
            wait_drained(v, "Y1e")
            wait_drained(v, "Y1o")
            for i in range(2):
                wait_full(v, f"mu{i}")
                ins = v.scalar_tensor_tensor(out=blk(9)[:, i * 512:(i + 1) * 512], in0=bank(f"mu{i}"), scalar=-1.0 / DH,
                                             in1=blk(8)[:, i * 512:(i + 1) * 512], op0=ALU.mult, op1=ALU.add)
                free(ins, f"mu{i}")
            for i in range(2):
                wait_drained(v, f"va{i}")
            link(v.reciprocal(blk(13), blk(13)))
            link(v.tensor_tensor(blk(9), blk(9), blk(13), ALU.mult))
            for ct in range(CT):
                ins = v.tensor_scalar(y_cen[:, ct, :], y_cen[:, ct, :], pcol("lnx_g", ct), pcol("lnx_b", ct), ALU.mult, ALU.add)
            link(ins)
            link(v.tensor_tensor(blk(9), blk(9), flat(bonus), ALU.add))
            for i in range(2):
                wait_full(v, f"gg{i}")
                ins = v.tensor_tensor(flat(kt)[:, i * 512:(i + 1) * 512], blk(9)[:, i * 512:(i + 1) * 512], bank(f"gg{i}"),
                                      ALU.mult)
                free(ins, f"gg{i}")
            need("merged_ok", 4)
            merge("B")

            def low_part(place, j, count):
                v.wait_ge(s["hi_ok"], count)
                v.tensor_tensor(wlo[:, place, :, :].rearrange("p k c -> p (k c)"), ring[:, j * HALF:(j + 1) * HALF],
                                whi[:, place, :, :].rearrange("p k c -> p (k c)").bitcast(F32),
                                ALU.subtract).then_inc(s["lo_ok"], 1)

            low_part(0, 0, 1)
            low_part(1, 1, 2)
            need("x_again", 16)
            for half in range(2):
                for t in range(TT):
                    name = f"wo{2 * half + t}"
                    wait_full(v, name)
                    xsl = x2[:, t, half * 512:(half + 1) * 512]
                    free(v.tensor_tensor(xsl, bank(name), xsl, ALU.add), name)
            wait_drained(v, "wo0", "wo1", "wo2", "wo3")
            need("x2ssq", 3)
            link(v.reciprocal(small[:, 14:16], small[:, 14:16]))
            need("bcast2_ok", 1)
            for t in range(TT):
                v.scalar_tensor_tensor(out=h2[:, t, :], in0=x2[:, t, :], scalar=small[:, 14 + t:15 + t], in1=norm2_b,
                                       op0=ALU.mult, op1=ALU.mult).then_inc(s["h2_ok"], 1)
            low_part(2, 2, 3)
            low_part(3, 3, 4)
            for t in range(TT):
                need("h2hi_ok", t + 1)
                v.tensor_tensor(h2lo[:, t, :], h2[:, t, :], h2hi[:, t, :].bitcast(F32), ALU.subtract).then_inc(
                    s["h2r_ok"], 1)
            need("rbcast_ok", 1)
            wait_full(v, "rt")
            bias = router_b[:].unsqueeze(1).to_broadcast([P, TT, 36])
            free(v.tensor_tensor(lg, bank("rt")[:, 0:72].rearrange("p (t n) -> p t n", t=TT), bias, ALU.add), "rt")
            wait_drained(v, "rt")
            gl, el = lg[:, :, 0:NG], lg[:, :, NG:]

            def tmp3(o, n):
                return rtmp[:, o:o + TT * n].rearrange("p (t n) -> p t n", t=TT)

            def col2(o):
                return small[:, o:o + 2]

            def wide(ap, n):
                return ap.unsqueeze(2).to_broadcast([P, TT, n])

            asg, one1, one2, el2, cand, gw = tmp3(0, NE), tmp3(64, NE), tmp3(128, NE), tmp3(192, NE), tmp3(256, NE), tmp3(320, NE)
            g4, g4b = tmp3(384, NG), tmp3(392, NG)
            iota4 = iota_e[:, :, 0:NG]

            def first_max(dst, src, n, m, it, c):
                link(v.tensor_reduce(m, src, AX.X, ALU.max))
                link(v.tensor_tensor(c, src, wide(m, n), ALU.is_equal))
                link(v.scalar_tensor_tensor(out=c, in0=c, scalar=-100.0, in1=it, op0=ALU.mult, op1=ALU.add))
                link(v.tensor_reduce(col2(28), c, AX.X, ALU.min))
                link(v.tensor_tensor(dst, c, wide(col2(28), n), ALU.is_equal))

            first_max(g4, gl, NG, col2(26), iota4, g4b)
            v.tensor_tensor(small[:, 32:40].rearrange("p (t n) -> p t n", t=TT), gl, wide(col2(26), NG),
                            ALU.subtract).then_inc(s["eexp_in"], 1)
            link(v.tensor_scalar(g4b, g4, FAR, -FAR, ALU.mult, ALU.add))
            for t in range(TT):
                gsel = g4[:, t, :].unsqueeze(2).to_broadcast([P, NG, EPG])
                gpen = g4b[:, t, :].unsqueeze(2).to_broadcast([P, NG, EPG])
                e3 = el2[:, t, :].rearrange("p (g e) -> p g e", g=NG)
                link(v.tensor_tensor(e3, el[:, t, :].rearrange("p (g e) -> p g e", g=NG), gsel, ALU.mult))
                link(v.tensor_tensor(e3, e3, gpen, ALU.add))
            first_max(one1, el2, NE, col2(30), iota_e[:], cand)
            link(v.scalar_tensor_tensor(out=el2, in0=one1, scalar=-2 * FAR, in1=el2, op0=ALU.mult, op1=ALU.add))
            first_max(one2, el2, NE, col2(24), iota_e[:], cand)
            v.tensor_tensor(asg, one1, one2, ALU.add).then_inc(s["cs_in"], 1)
            v.tensor_tensor(col2(24), col2(24), col2(30), ALU.subtract).then_inc(s["eexp_in"], 1)
            need("eexp_ok", 1)
            link(v.tensor_reduce(col2(50), small[:, 32:40].rearrange("p (t n) -> p t n", t=TT), AX.X, ALU.add))
            need("eexp_ok", 2)
            link(v.tensor_scalar(col2(52), col2(24), 1.0, None, ALU.add))
            link(v.tensor_tensor(col2(50), col2(50), col2(52), ALU.mult))
            link(v.reciprocal(col2(50), col2(50)))
            link(v.tensor_tensor(col2(52), col2(50), col2(24), ALU.mult))
            link(v.tensor_tensor(one1, one1, wide(col2(50), NE), ALU.mult))
            link(v.tensor_tensor(one2, one2, wide(col2(52), NE), ALU.mult))
            link(v.tensor_tensor(gw, one1, one2, ALU.add))
            for r in range(ROUNDS):
                v.tensor_copy(wts[:, :, r * NE:(r + 1) * NE], gw)
            wait_full(v, "cs")
            link(v.tensor_reduce(small[:, 54:55], bank("cs")[:, 64:96], AX.X, ALU.max))
            place = bank("cs")[:, 0:64].rearrange("p (t n) -> p t n", t=TT)
            need("cs_in", 1)
            free(v.tensor_tensor(cand, place, asg, ALU.mult), "cs")
            link(v.tensor_scalar(el2, asg, 1000.0, -1000.0, ALU.mult, ALU.add))
            wait_drained(v, "cs")
            link(v.tensor_tensor(cand, cand, el2, ALU.add))
            for r in range(ROUNDS):
                ins = v.tensor_scalar(pos[:, :, r * NE:(r + 1) * NE], cand, float(-CAP * r), None, ALU.add)
            link(ins)
            link(v.tensor_scalar(small[:, 55:56], small[:, 54:55], CAP + 0.5, float(NE // 4), ALU.is_gt, ALU.mult))
            for r in range(2, ROUNDS):
                link(v.tensor_scalar(small[:, 56:57], small[:, 54:55], CAP * r + 0.5, float(NE // 4), ALU.is_gt, ALU.mult))
                link(v.tensor_tensor(small[:, 55:56], small[:, 55:56], small[:, 56:57], ALU.add))
            v.tensor_scalar(last_quad_i[:], small[:, 55:56], float(NE // 4 - 1), None, ALU.add).then_inc(s["quads_ok"], 1)

            v.memset(yhi[:].bitcast(F32), 0.0).then_inc(s["dve0"], 1)
            v.memset(selT[1][:].bitcast(F32), 0.0).then_inc(s["dve0"], 1)
            v.memset(ylo[:].bitcast(F32), 0.0).then_inc(s["ylo_ok"], 2)
            need("fold_ok", 1)
            need("quads_ok", 1)
            last_quad = v.value_load(last_quad_i[0:1, 0:1], min_val=NE // 4 - 1, max_val=NE // 4 * ROUNDS - 1)

            def expert(i, p, b, last):
                n = i * 4 + (2 * p + b)
                h0 = 12 * p + 6 * b

                def split_ahead(j):
                    if last and h0 + j + SPLIT >= 24:
                        return
                    low_part((h0 + j) % SPLIT, (h0 + j + SPLIT) % HALVES, i * 24 + (h0 + j + SPLIT + 1))

                split_ahead(0)
                v.wait_ge(s["selT_full"], n + 1)
                v.tensor_scalar(foldw[b][:], fold[:], ps[:, 7, T:T + 1], None, ALU.mult)
                v.tensor_copy(selT[b][:], ps[:, 7, 0:T]).then_inc(s["selT_ok"], 1)
                split_ahead(1)
                split_ahead(2)
                split_ahead(3)
                v.wait_ge(s["silu_ok"], n + 1)
                v.tensor_tensor(hid, silu, ps[:, 6, T:2 * T], ALU.mult).then_inc(s["hid_ok"], 1)
                v.wait_ge(s["hidhi_ok"], n + 1)
                v.tensor_tensor(hidden[:, :, 1, :], hid.rearrange("p (k c) -> p k c", k=HC),
                                hidden[:, :, 0, :].bitcast(F32), ALU.subtract).then_inc(s["hidlo_ok"], 1)
                for half in range(2):
                    v.wait_ge(s["yhi_ok"], n * 2 + (half + 1))
                    v.tensor_tensor(ylo[:, half * 512:(half + 1) * 512], ps[:, 4 + half, :],
                                    yhi[:, half * 512:(half + 1) * 512].bitcast(F32), ALU.subtract).then_inc(
                        s["ylo_ok"], 1)
                    split_ahead(4 + half)

            with v.Fori(0, last_quad) as i:
                for p in range(2):
                    for b in range(2):
                        expert(i, p, b, False)
            for p in range(2):
                for b in range(2):
                    expert(last_quad, p, b, True)
            need("fssq", 3)
            link(v.reciprocal(small[:, 18:20], small[:, 18:20]))
            need("bcastf_ok", 1)
            for t in range(TT):
                v.scalar_tensor_tensor(out=out_sb[:, t, :], in0=ps[:, 2 * t:2 * t + 2, :].rearrange("p b c -> p (b c)"),
                                       scalar=small[:, 18 + t:19 + t], in1=final_b, op0=ALU.mult, op1=ALU.mult).then_inc(
                    s["out_ok"], 1)


def attn_heads(n):
    return ((0, 2), (1, 3), (4, 6), (5, 7), (0, 2, 4, 6), (1, 3, 5, 7))[n]


NAMES = ("x norm1_g w_in rwkv_mu w0 w_decay_up a0 w_iclr_up w_gate_up k_k k_a r_k lnx_g lnx_b pool_w pool_scale "
         "w_branch w_out norm2_g router_grp_w router_grp_b router_exp_w router_exp_b exp_w1 exp_w3 exp_w2 "
         "final_norm_g").split()


def kernel(**inputs):
    import numpy as _np
    import concourse.bacc as _bacc
    from concourse import mybir as _mybir
    from concourse.bass_utils import run_bass_kernel_spmd as _run

    nc = _bacc.Bacc("TRN2", target_bir_lowering=False, num_devices=1)
    arrays, args = {}, {}
    for name in NAMES:
        a = _np.ascontiguousarray(inputs[name])
        arrays[f"in_{name}_dram"] = a
        args[name] = nc.dram_tensor(f"in_{name}_dram", a.shape, _mybir.dt.from_np(a.dtype), kind="ExternalInput").ap()
    out = nc.dram_tensor("out_0_dram", (1, T, D), _mybir.dt.float32, kind="ExternalOutput").ap()
    trunk_and_experts(nc, out=out, **args)
    r = _run(nc, [arrays], core_ids=[0])
    return r.results[0]["out_0_dram"]
```

```python
from contextlib import ExitStack

import concourse.bass as bass
from concourse import mybir

ALU = mybir.AluOpType
ACT = mybir.ActivationFunctionType
AX = mybir.AxisListType
F32 = mybir.dt.float32
F32R = mybir.dt.float32r
I32 = mybir.dt.int32

P = 128
T = 256
TT = T // P
D = 1024
KD = D // P
BW = 512
CT = BW // P
H = 8
DH = 64
NG, EPG = 4, 8
NE = NG * EPG
HID = 512
HC = HID // P
CAP = 64
ROUNDS = T // CAP
RMS_EPS = 1e-6
LNX_EPS = 64e-5
DECAY_SCALE = 0.6065306597126334
FAR = 1e30
PIECE = 4096

Q_COL, K_COL, V_COL = 0, BW, 2 * BW
GATE_COL = 3 * BW
POOL_COL = GATE_COL + 3 * D
R_COL = POOL_COL + BW
RK_COL, RV_COL, LORA_COL = R_COL + BW, R_COL + 2 * BW, R_COL + 3 * BW

PAR_ROWS = (("norm1_g", 8), ("rwkv_mu", 14), ("w0", 4), ("a0", 4), ("k_k", 4), ("k_a", 4),
            ("r_k", 4), ("lnx_g", 4), ("lnx_b", 4), ("pool_scale", 4))

PIECES = ["lora", "rk", "rr", "rv", "aq", "ak", "pool", "av", "gC0", "gC1", "pC",
          "gA0", "gA1", "pA", "gB0", "gB1", "pB", "wo0", "wo1"]
TRUNK_SLOTS = 4
HALF = PIECE // 2
HALVES = 6
RAW = 4
SPLIT = 4
FIRST_BANKS = (4, 6, 5, 7)

LEVELS = (2, 4, 8, 16, 32, 64)


def fill_plan():
    plan = [("par", 1)] + [(f"hT{n}", 0) for n in range(4)]
    plan += [("lora", 0), ("rk0", 0), ("rk1", 0), ("rr0", 0)]
    plan += [("u0", 1), ("u1", 1), ("a0", 1), ("a1", 1)]
    plan += [("rr1", 0), ("rv0", 0), ("rv1", 0), ("ss0", 1), ("ss1", 1)]
    plan += [("aq0", 0), ("aq1", 0), ("ak0", 0), ("ak1", 0), ("pool0", 0), ("pool1", 0)]
    plan += [("vn0", 1), ("vn1", 1), ("bn", 1), ("kn", 1), ("bon0", 1), ("bon1", 1)]
    plan += [(f"sc{n}", 1) for n in range(16)]
    plan += [(f"at{n}", 0) for n in range(6)]
    plan += [(f"L{g}", 1) for g in range(4)] + [("av0", 0), ("av1", 0)] + [(f"G1_{g}", 1) for g in range(4)]
    for b in LEVELS:
        plan += [(f"A{b}_{g}", 1) for g in range(4)]
        plan += [(f"T{b}_{g}", 1) for g in range(4)]
        plan += [(f"G{b}_{g}", 1) for g in range(4)]
    plan += [(f"pt{h}", 0) for h in range(5)] + [("o0", 1)]
    plan += [(f"pt{h}", 0) for h in range(5, 8)] + [("o1", 1)]
    plan += [("pw", 1), ("pw1", 1)]
    plan += [("X0", 1), ("gC0a", 0), ("gC0b", 0), ("SA0", 1), ("gC1a", 0), ("gC1b", 0), ("St", 1)]
    plan += [(f"pC{n}", 0) for n in range(4)]
    plan += [("X1e", 1), ("X1o", 1), ("gA0a", 0), ("gA0b", 0), ("SA1", 1), ("gA1a", 0), ("gA1b", 0)]
    plan += [("Y0", 1), ("Y1e", 1), ("Y1o", 1)]
    plan += [(f"pA{n}", 0) for n in range(4)]
    plan += [("mu0", 1), ("mu1", 1), ("gB0a", 0), ("gB0b", 0), ("va0", 1), ("va1", 1)]
    plan += [("gg0", 1), ("gg1", 1), ("gB1a", 0), ("gB1b", 0)]
    plan += [(f"pB{n}", 0) for n in range(4)]
    plan += [("wo0", 0), ("wo1", 0), ("wo2", 0), ("h2T0", 1), ("h2T1", 1), ("wo3", 0)]
    plan += [("rt0", 1), ("h2T2", 1), ("h2T3", 1), ("rt1", 1), ("cs", 1)]
    return [n for n, _ in plan], dict(plan)


FILLS, RING_OF = fill_plan()
BANK, USE, seen = {}, {}, [0, 0]
for _name in FILLS:
    _r = RING_OF[_name]
    BANK[_name] = 4 * _r + seen[_r] % 4
    USE[_name] = seen[_r] // 4
    seen[_r] += 1
FULL = {n: i + 1 for i, n in enumerate(FILLS)}


def trunk_and_experts(nc, x, norm1_g, w_in, rwkv_mu, w0, w_decay_up, a0, w_iclr_up, w_gate_up, k_k, k_a, r_k,
                      lnx_g, lnx_b, pool_w, pool_scale, w_branch, w_out, norm2_g, router_grp_w, router_grp_b,
                      router_exp_w, router_exp_b, exp_w1, exp_w3, exp_w2, final_norm_g, out):
    with ExitStack() as ctx:
        start = (nc.sbuf_base + 63) // 64 * 64
        top = [start]
        where = {}

        def sb(name, shape, dt=F32, over=None, skip=0):
            n = 4
            for d in shape[1:]:
                n *= d
            if over is None:
                at, top[0] = top[0], top[0] + (n + 31) // 32 * 32
                assert top[0] <= nc.sbuf_usable_end, name
            else:
                at = where[over] + 4 * skip
            where[name] = at
            return nc.alloc_sbuf_tensor_at(name, shape, dt, offset=at)

        ring = sb("ring", [P, TRUNK_SLOTS * PIECE])
        arena = sb("arena", [P, 14 * 1024])
        hT = sb("hT", [P, KD, T])
        qk = sb("qk", [P, 2, CT, T])
        va = sb("va", [P, TT, BW])
        pz = sb("pz", [P, CT, T])
        bt = sb("bt", [P, CT, T])
        kt = sb("kt", [P, CT, T])
        bkn = sb("bkn", [P, 2, BW])
        bonus = sb("bonus", [P, CT, T])
        sig_g = sb("sig_g", [P, T])
        gm = sb("gm", [P, 2, KD, T])
        vn = sb("vn", [P, TT, BW])
        ar = sb("ar", [P, CT, TT, 2, P])
        par_rows = bkn[0:64, 1, 0:P]
        par = sb("par", [P, 54])
        ident = sb("ident", [P, P])
        ones = sb("ones", [P, P])
        head_ones = sb("head_ones", [P, P])
        causal = sb("causal", [P, 4, P])
        level_mask = sb("level_mask", [P, 7, P])
        dist = sb("dist", [P, T])
        count_inv = sb("count_inv", [P, CT, 16])
        lora_up = sb("lora_up", [P, BW])
        gate_up = sb("gate_up", [P, BW])
        poolw = sb("poolw", [P, CT, P])
        router_w = sb("router_w", [P, KD, NG + NE])
        router_b = sb("router_b", [P, NG + NE])
        router_b_row = sb("router_b_row", [1, NG + NE])
        small = sb("small", [P, 64])
        slopes = sb("slopes", [P, TT, H])
        amax = sb("amax", [P, TT, H])
        asum = sb("asum", [P, TT, H])
        state = sb("state", [P, CT, DH])
        iota_slot = sb("iota_slot", [P, 2, CAP])
        iota_e = sb("iota_e", [P, TT, NE])
        last_quad_i = sb("last_quad_i", [P, 1], I32)

        ps = ctx.enter_context(nc.psum_tensor("ps", [P, 8, 512], F32))

        def blk(n, m=1):
            return arena[:, n * 1024:(n + m) * 1024]

        def slot(n):
            return ring[:, n * PIECE:(n + 1) * PIECE]

        def ch(ap):
            return ap.rearrange("p (c t) -> p c t", c=CT)

        def chunks(ap):
            return ap.rearrange("p (c t) -> p c t", c=CT * TT)

        x_sb = blk(0, 2).rearrange("p (t d) -> p t d", t=TT)
        xn = blk(2, 2).rearrange("p (t d) -> p t d", t=TT)
        k_, r_, v_, dz, kprime = ch(blk(4)), ch(blk(1)), ch(blk(2)), ch(blk(3)), ch(blk(3))
        lora = blk(0)[:, 0:2 * T].rearrange("p (c t) -> p c t", c=2)
        dlora = blk(0)[:, 2 * T:4 * T].rearrange("p (c t) -> p c t", c=2)
        logw, iclr, kk, sq, tmp = (ch(blk(n)) for n in (5, 6, 11, 12, 13))
        tanh_w = bkn[0:64, 0, 0:T]
        sc = blk(0, 8).rearrange("p (n m t) -> p n m t", n=16, m=4)
        tri = blk(8, 2).rearrange("p (n t) -> p n t", n=16)
        triT = blk(10, 2).rearrange("p (n t) -> p n t", n=16)
        triA = blk(12, 2).rearrange("p (n t) -> p n t", n=16)
        xs = [blk(12)[:, 0:512], blk(13)[:, 0:512]]
        sa = [blk(12)[:, 512:1024], blk(13)[:, 512:1024]]
        y_raw, y_cen = ch(blk(8)), ch(blk(9))
        flat_gm = gm[:, :, :, :].rearrange("p a k t -> p (a k t)")
        prob = flat_gm[:, 0:H * 384].rearrange("p (h k) -> p h k", h=H)
        probT = flat_gm[:, 3072:3072 + 2 * 384].rearrange("p (b k) -> p b k", b=2)
        scan_ones = flat_gm[:, 0:1024]
        pool_a, pool_b = blk(13)[:, 0:T], blk(13)[:, T:2 * T]
        gates, merged = gm[:, 0], gm[:, 1]
        y_attn, y_rwkv, y_pool = bt, kt, pz
        x2 = qk[:, :, :, :].rearrange("p a c t -> p (a c t)").rearrange("p (t d) -> p t d", t=TT)
        h2 = gm[:, 0].rearrange("p k t -> p (k t)").rearrange("p (t d) -> p t d", t=TT)
        flat_ar = ar[:, :, :, :, :].rearrange("p a b c d -> p (a b c d)")
        norm2_b, final_b = flat_ar[:, 0:D], flat_ar[:, D:2 * D]
        out_sb = gm[:, 1].rearrange("p k t -> p (k t)").rearrange("p (t d) -> p t d", t=TT)
        NPOS = NE * ROUNDS
        whi = sb("whi", [P, SPLIT, 4, 512], F32R, over="ring", skip=3 * PIECE)
        wlo = sb("wlo", [P, SPLIT, 4, 512], F32R, over="arena", skip=4 * 1024)
        h2hi = sb("h2hi", [P, TT, D], F32R, over="bt")
        h2lo = sb("h2lo", [P, TT, D], F32R, over="va")
        xg = [sb("xg0", [P, KD, 2, 2, CAP], F32R, over="hT"), sb("xg1", [P, KD, 2, 2, CAP], F32R, over="gm")]
        yhi = sb("yhi", [P, D], F32R, over="qk")
        ylo = sb("ylo", [P, D], F32R, over="qk", skip=D)
        hidden = sb("hidden", [P, HC, 2, CAP], F32R, over="bonus")
        silu, hid = bonus[:, 2, :], bonus[:, 3, :]
        selp = sb("selp", [P, TT, 2, CAP], F32R, over="bkn")
        selT = [sb(f"selT{b}", [P, T], F32R, over="bkn", skip=256 * (1 + b)) for b in range(2)]
        hs = blk(13)[:, 0:1024].rearrange("p (a c) -> p a c", a=2)
        pos = blk(12)[:, 0:TT * NPOS].rearrange("p (t n) -> p t n", t=TT)
        wts = blk(12)[:, 256:256 + TT * NPOS].rearrange("p (t n) -> p t n", t=TT)
        seldup = [blk(12)[:, 512 + b * 256:768 + b * 256].rearrange("p (t c) -> p t c", t=TT) for b in range(2)]
        fold = sb("fold", [P, CAP], over="bkn", skip=768)
        foldw = [sb(f"foldw{b}", [P, CAP], over="bkn", skip=832 + CAP * b) for b in range(2)]
        wcol = sb("wcol", [P, 2, TT], over="bkn", skip=960)
        pair_cols = sb("pair_cols", [P, TT, 2], over="bkn", skip=968)[:]
        dup_cols = sb("dup_cols", [P, 2, TT], over="bkn", skip=976)
        lg = gate_up[:, 0:TT * 36].rearrange("p (t n) -> p t n", t=TT)
        rtmp = gate_up[:, TT * 36:]
        tri_ones = sb("tri_ones", [P, 2, P], F32R, over="lora_up")
        assigned = sb("assigned", [P, TT, NE], F32R, over="lora_up", skip=2 * P)
        raw = [slot(n) for n in range(3)] + [sb("raw3", [P, PIECE], over="gm", skip=KD * T)[:]]
        raw_first = sb("raw_first", [P, PIECE], over="arena", skip=8 * 1024)[:]

        full = ctx.enter_context(nc.semaphore("full"))
        drained = [ctx.enter_context(nc.semaphore(f"drained{b}")) for b in range(8)]
        loaded = [ctx.enter_context(nc.semaphore(f"loaded{n}")) for n in range(TRUNK_SLOTS)]
        raw_in = [ctx.enter_context(nc.semaphore(f"raw_in{n}")) for n in range(RAW)]
        SEMS = ("first_in tri_ones_ok column_ok wts_ok x_in0 x_in1 compared par_in x_again lo_ok quads_ok "
                "table_ok out_ok out_done pool_chain ident_ok lora_in gateup_in "
                "pool_in rw_in rb_in ones_ok masks_ok levels_ok dist_ok misc_ok rbcast_ok n2_in nf_in "
                "bcast2_ok bcastf_ok fold_ok selp_ok dup_ok gathered selT_full xn_ok tanh_ok lora_ok sq_ok "
                "v_ok bonin_ok ar_ok prob_ok pool_ok ysq_ok sigg_ok merged_ok h2_ok cs_in scattered xg_ok "
                "ylo_ok half_done hs_ok selT_ok folded hidlo_ok h2r_ok hi_ok const_ok ssq k_ok norm_ok "
                "logw_ok exps_ok smax_ok exp_ok x2ssq h2hi_ok eexp_in eexp_ok silu_ok hid_ok hidhi_ok "
                "yhi_ok fssq dve kk_ok r_ok bt_ok kt_ok ").split()
        s = {n: ctx.enter_context(nc.semaphore(n)) for n in SEMS}

        def bank(name):
            return ps[:, BANK[name], :]

        def wait_full(eng, *names):
            for name in names:
                eng.wait_ge(full, FULL[name])

        def wait_drained(eng, *names):
            for name in names:
                eng.wait_ge(drained[BANK[name]], USE[name] + 1)

        pc, at = {}, 0
        for n, rows in PAR_ROWS:
            pc[n] = at
            at += rows

        def pcol(name, i):
            return par[:, pc[name] + i:pc[name] + i + 1]

        block = ctx.enter_context(nc.Block())

        piece_src = {
            "lora": w_in[0, :, LORA_COL:LORA_COL + 256], "rk": w_in[0, :, RK_COL:RK_COL + BW],
            "rr": w_in[0, :, R_COL:R_COL + BW], "rv": w_in[0, :, RV_COL:RV_COL + BW],
            "aq": w_in[0, :, Q_COL:Q_COL + BW], "ak": w_in[0, :, K_COL:K_COL + BW],
            "av": w_in[0, :, V_COL:V_COL + BW], "pool": w_in[0, :, POOL_COL:POOL_COL + BW],
            "wo0": w_out[0, :, 0:BW], "wo1": w_out[0, :, BW:D],
        }
        for br, b in (("A", 0), ("B", 1), ("C", 2)):
            for half in range(2):
                c0 = GATE_COL + b * D + half * BW
                piece_src[f"g{br}{half}"] = w_in[0, :, c0:c0 + BW]
            piece_src[f"p{br}"] = w_branch[0, b]
        last_fill = {"lora": "lora", "rk": "rk1", "rr": "rr1", "rv": "rv1", "aq": "aq1", "ak": "ak1", "av": "av1",
                     "pool": "pool1", "gC0": "gC0b", "gC1": "gC1b", "pC": "pC3", "gA0": "gA0b", "gA1": "gA1b",
                     "pA": "pA3", "gB0": "gB0b", "gB1": "gB1b", "pB": "pB3", "wo0": "wo2", "wo1": "wo3"}

        def piece(name):
            n = PIECES.index(name)
            cols = {"lora": 256}.get(name, D if name[0] == "p" and name != "pool" else BW)
            k = 4 if cols == D else KD
            return slot(n % TRUNK_SLOTS)[:, 0:k * cols].rearrange("p (k c) -> p k c", k=k)

        def trunk_loads(n):
            return 16 * (n // TRUNK_SLOTS + 1)

        SLOT_FREE = [last_fill[[p for n, p in enumerate(PIECES) if n % TRUNK_SLOTS == b][-1]] for b in range(TRUNK_SLOTS)]

        def raw_place(m):
            return (raw_first, s["first_in"]) if m == 0 else (raw[(m - 1) % RAW], raw_in[(m - 1) % RAW])

        def matrix_dma(sp, w, e, m):
            place, arrived = raw_place(m)
            sp.dma_start(place.rearrange("p (k c) -> p k c", c=w.shape[-1]),
                         w[0, bass.ds(e, 1)].rearrange("o (k p) c -> p (o k) c", p=P)).then_inc(arrived, 16)

        def raw_half(q, tail):
            m, half = q // 2, q % 2
            place = raw_place(m)[0]
            if (m > 0 and m % 3 == 0) or (tail and m == 11):
                return place.rearrange("p (k c) -> p k c", k=HC)[:, :, half * 512:(half + 1) * 512]
            return place[:, half * HALF:(half + 1) * HALF].rearrange("p (k c) -> p k c", k=4)

        @block.sync
        def _(sp):
            for t in range(TT):
                sp.dma_start(x_sb[:, t, :], x[0, t * P:(t + 1) * P, :]).then_inc(s[f"x_in{t}"], 16)
            row = 0
            for name, src in (("norm1_g", norm1_g), ("rwkv_mu", rwkv_mu), ("w0", w0), ("a0", a0), ("k_k", k_k),
                              ("k_a", k_a), ("r_k", r_k), ("lnx_g", lnx_g), ("lnx_b", lnx_b),
                              ("pool_scale", pool_scale)):
                rows = dict(PAR_ROWS)[name]
                flat = src[0].rearrange("h d -> (h d)") if name == "r_k" else src[0]
                sp.dma_start(par_rows[row:row + rows, :], flat.rearrange("(r c) -> r c", c=P)).then_inc(s["par_in"], 16)
                row += rows
            for n, name in enumerate(PIECES):
                if n >= TRUNK_SLOTS:
                    sp.wait_ge(full, FULL[last_fill[PIECES[n - TRUNK_SLOTS]]])
                sp.dma_start(piece(name), piece_src[name].rearrange("(k p) c -> p k c", p=P)).then_inc(
                    loaded[n % TRUNK_SLOTS], 16)
                if name == "gA0":
                    sp.wait_ge(full, FULL["at5"])
                    sp.dma_start(x2, x[0].rearrange("(t p) d -> p t d", p=P)).then_inc(s["x_again"], 16)
            wait_drained(sp, "gg0", "gg1")
            matrix_dma(sp, exp_w1, 0, 0)
            for m, w, e in ((1, exp_w3, 0), (2, exp_w1, 1), (3, exp_w2, 0)):
                sp.wait_ge(full, FULL[SLOT_FREE[m - 1]])
                matrix_dma(sp, w, e, m)
            sp.wait_ge(full, FULL["wo3"])
            sp.wait_ge(s["h2_ok"], TT)

            def step_loads(i, c, this, then, last=False):
                matrices = ((exp_w3, this), (exp_w2, this)) if last else ((exp_w3, this), (exp_w1, then), (exp_w2, this))
                for j, (w, e) in enumerate(matrices):
                    m = 3 * c + 4 + j
                    sp.wait_ge(s["lo_ok"], i * 24 + 2 * (m - RAW + 1))
                    matrix_dma(sp, w, e, m)

            step_loads(0, 0, 1, 2)
            sp.wait_ge(s["quads_ok"], 1)
            last_quad = sp.value_load(last_quad_i[0:1, 0:1], min_val=NE // 4 - 1, max_val=NE // 4 * ROUNDS - 1)
            for c in range(1, 4):
                step_loads(0, c, c + 1, c + 2)
            with sp.Fori(1, last_quad) as i:
                for c in range(4):
                    this, then = (sp.snap(((i + (c + d) // 4) % (NE // 4)) * 4 + (c + d) % 4, min_val=0, max_val=NE - 1)
                                  for d in (1, 2))
                    step_loads(i, c, this, then)
            step_loads(last_quad, 0, NE - 3, NE - 2)
            step_loads(last_quad, 1, NE - 2, NE - 1)
            step_loads(last_quad, 2, NE - 1, None, last=True)
            for t in range(TT):
                sp.wait_ge(s["out_ok"], t + 1)
                sp.dma_start(out[0, t * P:(t + 1) * P, :], out_sb[:, t, :]).then_inc(s["out_done"], 16)
            sp.wait_ge(s["out_done"], 16 * TT)

        @block.gpsimd
        def _(g):
            chain = [0]

            def link(ins):
                chain[0] += 1
                ins.then_inc(s["pool_chain"], 1)
                g.wait_ge(s["pool_chain"], chain[0])

            link(nc.gpsimd.memset(ident[:], 0.0))
            nc.gpsimd.affine_select(out=ident[:], in_=ident[:], compare_op=ALU.not_equal, fill=1.0, base=0,
                                    pattern=[[-1, P]], channel_multiplier=1).then_inc(s["ident_ok"], 1)
            g.dma_start(lora_up[0:64, :], w_decay_up[0]).then_inc(s["lora_in"], 16)
            g.dma_start(lora_up[64:P, :], w_iclr_up[0]).then_inc(s["lora_in"], 16)
            g.dma_start(gate_up[:], w_gate_up[0]).then_inc(s["gateup_in"], 16)
            g.dma_start(poolw[:], pool_w[0].rearrange("g c d -> c g d")).then_inc(s["pool_in"], 16)
            g.dma_start(router_w[:, :, 0:NG], router_grp_w[0].rearrange("(k p) n -> p k n", p=P)).then_inc(s["rw_in"], 16)
            g.dma_start(router_w[:, :, NG:], router_exp_w[0].rearrange("(k p) n -> p k n", p=P)).then_inc(s["rw_in"], 16)
            g.dma_start(router_b_row[:, 0:NG], router_grp_b).then_inc(s["rb_in"], 16)
            g.dma_start(router_b_row[:, NG:], router_exp_b).then_inc(s["rb_in"], 16)
            nc.gpsimd.memset(ones[:], 1.0).then_inc(s["ones_ok"], 1)
            link(nc.gpsimd.memset(head_ones[:], 1.0))
            nc.gpsimd.affine_select(out=head_ones[:, 0:DH], in_=head_ones[:, 0:DH], compare_op=ALU.is_ge, fill=0.0,
                                    base=DH - 1, pattern=[[0, DH]], channel_multiplier=-1)
            nc.gpsimd.affine_select(out=head_ones[:, DH:P], in_=head_ones[:, DH:P], compare_op=ALU.is_ge, fill=0.0,
                                    base=-DH, pattern=[[0, DH]], channel_multiplier=1).then_inc(s["ones_ok"], 1)
            nc.gpsimd.memset(scan_ones, 1.0).then_inc(s["ones_ok"], 1)
            g.wait_ge(s["ones_ok"], 3)
            nc.gpsimd.memset(scan_ones.rearrange("p (n t) -> p n t", t=P)[:, :, 0:1], 0.0).then_inc(s["ones_ok"], 1)
            link(nc.gpsimd.memset(causal[:], 1.0))
            for m in range(4):
                nc.gpsimd.affine_select(out=causal[:, m, :], in_=causal[:, m, :], compare_op=ALU.is_ge, fill=0.0,
                                        base=-1 if m % 2 == 0 else 0, pattern=[[1, P]],
                                        channel_multiplier=-1).then_inc(s["masks_ok"], 1)
            link(nc.gpsimd.memset(level_mask[:], 0.0))
            for lev in range(7):
                b = 1 << lev
                view = level_mask[:, lev, :].rearrange("p (n c) -> p n c", c=2 * b)[:, :, 0:b]
                nb = P // (2 * b)
                link(nc.gpsimd.memset(view, 1.0))
                link(nc.gpsimd.affine_select(out=view, in_=view, compare_op=ALU.is_ge, fill=0.0, base=-b,
                                             pattern=[[-2 * b, nb], [0, b]], channel_multiplier=1))
                nc.gpsimd.affine_select(out=view, in_=view, compare_op=ALU.is_ge, fill=0.0, base=2 * b - 1,
                                        pattern=[[2 * b, nb], [0, b]], channel_multiplier=-1).then_inc(s["levels_ok"], 1)
            link(nc.gpsimd.iota(dist[:], [[-1, T]], base=P, channel_multiplier=1, allow_small_or_imprecise_dtypes=True))
            nc.gpsimd.affine_select(out=dist[:], in_=dist[:], compare_op=ALU.is_ge, fill=FAR, base=P,
                                    pattern=[[-1, T]], channel_multiplier=1).then_inc(s["dist_ok"], 1)
            for h in range(H):
                nc.gpsimd.memset(slopes[:, :, h:h + 1], -(2.0 ** -(h + 1))).then_inc(s["misc_ok"], 1)
            nc.gpsimd.iota(iota_slot[:], [[0, 2], [1, CAP]], base=0, channel_multiplier=0,
                           allow_small_or_imprecise_dtypes=True).then_inc(s["misc_ok"], 1)
            nc.gpsimd.iota(iota_e[:], [[0, TT], [1, NE]], base=0, channel_multiplier=0,
                           allow_small_or_imprecise_dtypes=True).then_inc(s["misc_ok"], 1)
            link(nc.gpsimd.iota(count_inv[:], [[0, CT], [1, 16]], base=1, channel_multiplier=0,
                                allow_small_or_imprecise_dtypes=True))
            for i in range(CT):
                nc.gpsimd.tensor_scalar(count_inv[:, i, :], count_inv[:, i, :], float(2 << i), None,
                                        ALU.min).then_inc(s["misc_ok"], 1)
            g.wait_ge(s["rb_in"], 32)
            nc.gpsimd.partition_broadcast(router_b[:], router_b_row[:]).then_inc(s["rbcast_ok"], 1)
            g.wait_ge(full, FULL["Y1o"])
            g.dma_start(norm2_b[0:1, :], norm2_g).then_inc(s["n2_in"], 16)
            g.dma_start(final_b[0:1, :], final_norm_g.rearrange("(o d) -> o d", o=1)).then_inc(s["nf_in"], 16)
            g.wait_ge(s["n2_in"], 16)
            nc.gpsimd.partition_broadcast(norm2_b, norm2_b[0:1, :]).then_inc(s["bcast2_ok"], 1)
            g.wait_ge(s["nf_in"], 16)
            nc.gpsimd.partition_broadcast(final_b, final_b[0:1, :]).then_inc(s["bcastf_ok"], 1)
            link(nc.gpsimd.memset(fold[:], 0.0))
            link(nc.gpsimd.affine_select(out=fold[:], in_=fold[:], compare_op=ALU.not_equal, fill=1.0, base=0,
                                         pattern=[[-1, CAP]], channel_multiplier=1))
            nc.gpsimd.affine_select(out=fold[:], in_=fold[:], compare_op=ALU.not_equal, fill=1.0, base=-CAP,
                                    pattern=[[-1, CAP]], channel_multiplier=1).then_inc(s["fold_ok"], 1)

            g.wait_ge(s["quads_ok"], 1)
            last_quad = g.value_load(last_quad_i[0:1, 0:1], min_val=NE // 4 - 1, max_val=NE // 4 * ROUNDS - 1)

            def select_pair(n0, columns):
                nc.gpsimd.tensor_copy(pair_cols, pos[:, :, bass.ds(n0, 2)]).then_inc(s["column_ok"], 1)
                g.wait_ge(s["column_ok"], columns + 1)
                g.sem_inc(s["compared"], 1)
                for b in range(2):
                    for t in range(TT):
                        ins = nc.gpsimd.tensor_scalar(selp[:, t, b, :], iota_slot[:, 0, :], pair_cols[:, t, b:b + 1], None,
                                                      ALU.is_equal)
                ins.then_inc(s["selp_ok"], 1)

            def select_dup(b, n, columns):
                nc.gpsimd.tensor_copy(wcol[:, b, :].unsqueeze(2), wts[:, :, bass.ds(n, 1)])
                nc.gpsimd.tensor_copy(dup_cols[:, b, :].unsqueeze(2), pos[:, :, bass.ds(n, 1)]).then_inc(s["column_ok"], 1)
                g.wait_ge(s["column_ok"], columns + 2 + b)
                g.sem_inc(s["compared"], 1)
                for t in range(TT):
                    ins = nc.gpsimd.tensor_scalar(seldup[b][:, t, :], iota_slot[:].rearrange("p a c -> p (a c)"),
                                                  dup_cols[:, b, t:t + 1], None, ALU.is_equal)
                ins.then_inc(s["dup_ok"], 1)

            g.wait_ge(s["wts_ok"], 1)
            select_dup(0, 0, -1)
            select_dup(1, 1, -1)

            def next_pair(i, p):
                n0 = i * 4 + 2 * p
                columns = i * 6 + (3 * p + 2)
                g.wait_ge(s["gathered"], i * 8 + 4 * (p + 1))
                select_pair(n0 + 2, columns)
                for b in range(2):
                    g.wait_ge(s["selT_full"], n0 + b + 1)
                    select_dup(b, n0 + b + 2, columns)

            with g.Fori(0, last_quad) as i:
                next_pair(i, 0)
                next_pair(i, 1)
            next_pair(last_quad, 0)

        @block.tensor
        def _(pe):
            order = iter(FILLS)

            def open_fill(name):
                if USE[name]:
                    pe.wait_ge(drained[BANK[name]], USE[name])
                return bank(name)

            def close_fill(name, ins):
                assert next(order) == name, name
                ins.then_inc(full, 1)

            def need_piece(name):
                n = PIECES.index(name)
                pe.wait_ge(loaded[n % TRUNK_SLOTS], trunk_loads(n))
                return piece(name)

            def need(sem, n):
                pe.wait_ge(s[sem], n)

            def project(fill, w, tiles, c0, rhs, nk, source=None):
                b = open_fill(fill)
                for i in range(tiles):
                    for k in range(nk):
                        if source and i == 0 and k % 2 == 0:
                            wait_drained(pe, f"{source}{k // 2}")
                        mm = pe.matmul(b[:, i * T:(i + 1) * T], w[:, k, (c0 + i) * P:(c0 + i + 1) * P], rhs[:, k, :],
                                       start=(k == 0), stop=(k == nk - 1))
                close_fill(fill, mm)

            need("ident_ok", 1)
            need("par_in", 160)
            b = open_fill("par")
            close_fill("par", pe.transpose(b[:, 0:54], par_rows[0:54, :], ident[0:54, 0:54]))
            for n in range(4):
                b = open_fill(f"hT{n}")
                for i in range(2):
                    for t in range(TT):
                        need("xn_ok", t + 1)
                        k = 2 * n + i
                        mm = pe.transpose(b[:, i * T + t * P:i * T + (t + 1) * P], xn[:, t, k * P:(k + 1) * P], ident[:])
                close_fill(f"hT{n}", mm)
            project("lora", need_piece("lora"), 2, 0, hT, KD, source="hT")
            w = need_piece("rk")
            for i in range(2):
                project(f"rk{i}", w, 2, 2 * i, hT, KD)
            w = need_piece("rr")
            project("rr0", w, 2, 0, hT, KD)
            need("lora_in", 32)
            need("tanh_ok", 1)
            for i in range(2):
                b = open_fill(f"u{i}")
                for c in range(2):
                    mm = pe.matmul(b[:, c * T:(c + 1) * T], lora_up[0:64, (2 * i + c) * P:(2 * i + c + 1) * P], tanh_w,
                                   start=True, stop=True)
                close_fill(f"u{i}", mm)
            need("lora_ok", 2)
            for i in range(2):
                b = open_fill(f"a{i}")
                for c in range(2):
                    mm = pe.matmul(b[:, c * T:(c + 1) * T], lora_up[64:P, (2 * i + c) * P:(2 * i + c + 1) * P],
                                   lora[64:P, 0, :], start=True, stop=True)
                close_fill(f"a{i}", mm)
            project("rr1", w, 2, 2, hT, KD)
            w = need_piece("rv")
            for i in range(2):
                project(f"rv{i}", w, 2, 2 * i, hT, KD)
            need("ones_ok", 2)
            need("sq_ok", 4)
            for i in range(2):
                b = open_fill(f"ss{i}")
                close_fill(f"ss{i}", pe.matmul(b, head_ones[:], blk(12)[:, i * 512:(i + 1) * 512], start=True, stop=True))
            for name in ("aq", "ak"):
                w = need_piece(name)
                for i in range(2):
                    project(f"{name}{i}", w, 2, 2 * i, hT, KD)
            w = need_piece("pool")
            for i in range(2):
                project(f"pool{i}", w, 2, 2 * i, hT, KD)
            need("v_ok", 4)
            for c in range(TT):
                b = open_fill(f"vn{c}")
                for t in range(CT):
                    mm = pe.transpose(b[:, t * P:(t + 1) * P], v_[:, t, c * P:(c + 1) * P], ident[:])
                close_fill(f"vn{c}", mm)
            for name, src, sem in (("bn", bt, "bt_ok"), ("kn", kt, "kt_ok")):
                need(sem, 1)
                b = open_fill(name)
                for t in range(CT):
                    mm = pe.transpose(b[:, t * P:(t + 1) * P], src[:, t, 0:P], ident[:])
                close_fill(name, mm)
            need("bonin_ok", 4)
            for i in range(2):
                b = open_fill(f"bon{i}")
                close_fill(f"bon{i}", pe.matmul(b, head_ones[:], blk(13)[:, i * 512:(i + 1) * 512], start=True, stop=True))
            need("ar_ok", 2)
            def score(n, m):
                c, h = divmod(n, H)
                rows = slice(64 * (h % 2), 64 * (h % 2) + 64)
                return pe.matmul(bank(f"sc{n}")[:, m * T:(m + 1) * T], (bt, kt)[m][rows, h // 2, c * P:(c + 1) * P],
                                 ar[rows, h // 2, c, :, :].rearrange("p m t -> p (m t)"), start=True, stop=True)

            for n in range(0, 16, 2):
                open_fill(f"sc{n}")
                open_fill(f"sc{n + 1}")
                score(n, 0)
                score(n + 1, 0)
                close_fill(f"sc{n}", score(n, 1))
                close_fill(f"sc{n + 1}", score(n + 1, 1))
            wait_drained(pe, "aq0", "aq1", "ak0", "ak1")

            def attention_score(n, i):
                h = attn_heads(n)[i]
                rows = slice(64 * (h % 2), 64 * (h % 2) + 64)
                if n < 4:
                    return pe.matmul(bank(f"at{n}")[:, i * T:(i + 1) * T], qk[rows, 0, h // 2, P:T], qk[rows, 1, h // 2, :],
                                     start=True, stop=True)
                return pe.matmul(bank(f"at{n}")[:, i * P:(i + 1) * P], qk[rows, 0, h // 2, 0:P], qk[rows, 1, h // 2, 0:P],
                                 start=True, stop=True)

            for n in (0, 2, 4):
                open_fill(f"at{n}")
                open_fill(f"at{n + 1}")
                for i in range(len(attn_heads(n)) - 1):
                    attention_score(n, i)
                    attention_score(n + 1, i)
                close_fill(f"at{n}", attention_score(n, i + 1))
                close_fill(f"at{n + 1}", attention_score(n + 1, i + 1))
            for g in range(4):
                b = open_fill(f"L{g}")
                for i in range(4):
                    n = 4 * g + i
                    wait_drained(pe, f"sc{n}")
                    mm = pe.transpose(b[:, i * P:(i + 1) * P], sc[:, n, 0, :], ident[:])
                close_fill(f"L{g}", mm)

            w = need_piece("av")
            for t in range(TT):
                b = open_fill(f"av{t}")
                for k in range(KD):
                    mm = pe.matmul(b, hT[:, k, t * P:(t + 1) * P], w[:, k, :], start=(k == 0), stop=(k == KD - 1))
                close_fill(f"av{t}", mm)

            def transpose_tri(name, g, source):
                b = open_fill(name)
                wait_drained(pe, source)
                for i in range(4):
                    mm = pe.transpose(b[:, i * P:(i + 1) * P], tri[:, 4 * g + i, :], ident[:])
                close_fill(name, mm)

            for g in range(4):
                transpose_tri(f"G1_{g}", g, f"L{g}")
            low = slice(64, P)
            for size in LEVELS:
                for g in range(4):
                    b = open_fill(f"A{size}_{g}")
                    for i in range(4):
                        n = 4 * g + i
                        if size == 64:
                            mm = pe.matmul(b[low, i * 64:(i + 1) * 64], sc[0:64, n, 0, 64:P], tri[0:64, n, 0:64],
                                           start=True, stop=True)
                        else:
                            mm = pe.matmul(b[:, i * P:(i + 1) * P], sc[:, n, 0, :], tri[:, n, :], start=True, stop=True)
                    close_fill(f"A{size}_{g}", mm)
                for g in range(4):
                    b = open_fill(f"T{size}_{g}")
                    wait_drained(pe, f"G{size // 2}_{g}", f"A{size}_{g}")
                    for i in range(4):
                        n = 4 * g + i
                        if size == 64:
                            mm = pe.matmul(b[low, i * 64:(i + 1) * 64], triT[low, n, 64:P], triA[low, n, 0:64],
                                           start=True, stop=True)
                        else:
                            mm = pe.matmul(b[:, i * P:(i + 1) * P], triT[:, n, :], triA[:, n, :], start=True, stop=True)
                    close_fill(f"T{size}_{g}", mm)
                for g in range(4):
                    transpose_tri(f"G{size}_{g}", g, f"T{size}_{g}")

            def pT(h):
                b = open_fill(f"pt{h}")
                need("prob_ok", 2)
                for j in range(3):
                    mm = pe.transpose(b[:, j * P:(j + 1) * P], prob[:, h, j * P:(j + 1) * P], ident[:])
                close_fill(f"pt{h}", mm)

            def pv(h):
                b = bank(f"o{h // 4}")
                if h % 4 == 0:
                    open_fill(f"o{h // 4}")
                wait_drained(pe, f"pt{h}")
                orow = slice(64 * (h % 2), 64 * (h % 2) + 64)
                c0 = (h // 2 % 2) * T
                head = slice(h * DH, (h + 1) * DH)
                if h == 0:
                    wait_drained(pe, "av0", "av1")
                pe.matmul(b[orow, c0:c0 + P], va[:, 0, head], probT[:, h % 2, 0:P], start=True, stop=True)
                for j in range(2):
                    mm = pe.matmul(b[orow, c0 + P:c0 + T], va[:, j, head], probT[:, h % 2, (1 + j) * P:(2 + j) * P],
                                   start=(j == 0), stop=(j == 1))
                return mm

            pT(0)
            pT(1)
            for h in range(H):
                mm = pv(h)
                if h % 4 == 3:
                    close_fill(f"o{h // 4}", mm)
                if h + 2 < H:
                    pT(h + 2)
            need("pool_in", 16)
            need("pool_ok", 4)
            for i, name in enumerate(("pw", "pw1")):
                b = open_fill(name)
                for c in range(2):
                    mm = pe.matmul(b[:, c * T:(c + 1) * T], poolw[:, 2 * i + c, :], pz[:, 2 * i + c, :],
                                   start=True, stop=True)
                close_fill(name, mm)

            def heads_out(b, h):
                return b[:, h * DH:(h + 1) * DH]

            wait_drained(pe, "vn0", "vn1")
            b = open_fill("X0")
            for h in range(H):
                mm = pe.matmul(heads_out(b, h), sc[:, h, 2, :], vn[:, 0, h * DH:(h + 1) * DH], start=True, stop=True)
            close_fill("X0", mm)

            def gate_half(br, half):
                w = need_piece(f"g{br}{half}")
                for i, part in enumerate("ab"):
                    project(f"g{br}{half}{part}", w, 2, 2 * i, hT, KD)

            def branch(br, y):
                w = need_piece(f"p{br}")
                for n in range(4):
                    project(f"p{br}{n}", w, 2, 2 * n, y, CT)

            gate_half("C", 0)
            wait_drained(pe, "X0", "G64_0", "G64_1", "G64_2", "G64_3")
            b = open_fill("SA0")
            for h in range(H):
                mm = pe.matmul(heads_out(b, h), triT[:, h, :], xs[0][:, h * DH:(h + 1) * DH], start=True, stop=True)
            close_fill("SA0", mm)
            gate_half("C", 1)
            wait_drained(pe, "SA0", "bn", "kn")
            b = open_fill("St")
            for h in range(H):
                o = b[64 * (h % 2):64 * (h % 2) + 64, (h // 2) * DH:(h // 2 + 1) * DH]
                head = slice(h * DH, (h + 1) * DH)
                pe.matmul(o, bkn[:, 0, head], sa[0][:, head], start=True, stop=False)
                mm = pe.matmul(o, bkn[:, 1, head], vn[:, 0, head], start=False, stop=True)
            close_fill("St", mm)
            wait_drained(pe, "pw", "pw1")
            branch("C", y_pool)
            wait_drained(pe, "St")
            for parity, name in enumerate(("X1e", "X1o")):
                b = open_fill(name)
                rows = slice(64 * parity, 64 * parity + 64)
                for i in range(4):
                    h = 2 * i + parity
                    pe.matmul(b[:, i * DH:(i + 1) * DH], sc[:, H + h, 2, :], vn[:, 1, h * DH:(h + 1) * DH],
                              start=True, stop=False)
                    mm = pe.matmul(b[:, i * DH:(i + 1) * DH], ar[rows, i, 1, 0, :], state[rows, i, :],
                                   start=False, stop=True)
                close_fill(name, mm)
            gate_half("A", 0)
            wait_drained(pe, "X1e", "X1o")
            b = open_fill("SA1")
            for h in range(H):
                mm = pe.matmul(heads_out(b, h), triT[:, H + h, :], xs[1][:, h * DH:(h + 1) * DH], start=True, stop=True)
            close_fill("SA1", mm)
            gate_half("A", 1)
            wait_drained(pe, "SA1")
            b = open_fill("Y0")
            for h in range(H):
                o = b[64 * (h % 2):64 * (h % 2) + 64, (h // 2) * P:(h // 2 + 1) * P]
                head = slice(h * DH, (h + 1) * DH)
                pe.matmul(o, sa[0][:, head], sc[:, h, 1, :], start=True, stop=False)
                mm = pe.matmul(o, vn[:, 0, head], sc[:, h, 3, :], start=False, stop=True)
            close_fill("Y0", mm)
            for parity, name in enumerate(("Y1e", "Y1o")):
                b = open_fill(name)
                rows = slice(64 * parity, 64 * parity + 64)
                for i in range(4):
                    h = 2 * i + parity
                    o = b[rows, i * P:(i + 1) * P]
                    head = slice(h * DH, (h + 1) * DH)
                    pe.matmul(o, sa[1][:, head], sc[:, H + h, 1, :], start=True, stop=False)
                    pe.matmul(o, vn[:, 1, head], sc[:, H + h, 3, :], start=False, stop=False)
                    mm = pe.matmul(o, state[rows, i, :], ar[rows, i, 1, 1, :], start=False, stop=True)
                close_fill(name, mm)
            wait_drained(pe, "o0", "o1")
            branch("A", y_attn)
            wait_drained(pe, "Y0", "Y1e", "Y1o")
            for i in range(2):
                b = open_fill(f"mu{i}")
                close_fill(f"mu{i}", pe.matmul(b, head_ones[:], blk(8)[:, i * 512:(i + 1) * 512], start=True, stop=True))
            gate_half("B", 0)
            need("ysq_ok", 1)
            for i in range(2):
                b = open_fill(f"va{i}")
                close_fill(f"va{i}", pe.matmul(b, head_ones[:], blk(12)[:, i * 512:(i + 1) * 512], start=True, stop=True))
            need("gateup_in", 16)
            need("sigg_ok", 1)
            for i in range(2):
                b = open_fill(f"gg{i}")
                for c in range(2):
                    mm = pe.matmul(b[:, c * T:(c + 1) * T], gate_up[:, (2 * i + c) * P:(2 * i + c + 1) * P], sig_g[:],
                                   start=True, stop=True)
                close_fill(f"gg{i}", mm)
            gate_half("B", 1)
            wait_drained(pe, "gg0", "gg1")
            branch("B", y_rwkv)
            def output(t, half):
                name = f"wo{2 * t + half}"
                b = open_fill(name)
                w = need_piece(f"wo{half}")
                for k in range(KD):
                    if t == half == 0:
                        need("merged_ok", 4 + k // 2 + 1)
                    mm = pe.matmul(b, merged[:, k, t * P:(t + 1) * P], w[:, k, :], start=(k == 0), stop=(k == KD - 1))
                close_fill(name, mm)

            def h2_transposes(t):
                for half in range(2):
                    name = f"h2T{2 * t + half}"
                    b = open_fill(name)
                    for i in range(4):
                        need("h2_ok", t + 1)
                        k = 4 * half + i
                        mm = pe.transpose(b[:, i * P:(i + 1) * P], h2[:, t, k * P:(k + 1) * P], ident[:])
                    close_fill(name, mm)

            def router(t):
                b = open_fill(f"rt{t}")
                for k in range(KD):
                    if k % 4 == 0:
                        wait_drained(pe, f"h2T{2 * t + k // 4}")
                    mm = pe.matmul(b[:, 0:NG + NE], hT[:, k, t * P:(t + 1) * P], router_w[:, k, :],
                                   start=(k == 0), stop=(k == KD - 1))
                close_fill(f"rt{t}", mm)

            def start_sum(t, half):
                pe.matmul(ps[:, 2 * t + half, :], ident[:], x2[:, t, half * 512:(half + 1) * 512],
                          start=True, stop=False, skip_group_check=True)

            output(0, 0)
            output(0, 1)
            output(1, 0)
            h2_transposes(0)
            output(1, 1)
            need("rw_in", 32)
            router(0)
            wait_drained(pe, "wo0", "wo1", "wo2", "wo3")
            h2_transposes(1)
            router(1)
            start_sum(0, 0)
            start_sum(0, 1)
            need("eexp_in", 1)
            start_sum(1, 0)
            need("tri_ones_ok", 2)
            need("cs_in", 1)
            b = open_fill("cs")
            before, every = tri_ones[:, 0, :], tri_ones[:, 1, :]
            pe.matmul(b[:, 0:32], before, assigned[:, 0, :], start=True, stop=True)
            pe.matmul(b[:, 32:64], before, assigned[:, 1, :], start=True, stop=False)
            pe.matmul(b[:, 32:64], every, assigned[:, 0, :], start=False, stop=True)
            pe.matmul(b[:, 64:96], every, assigned[:, 0, :], start=True, stop=False)
            mm = pe.matmul(b[:, 64:96], every, assigned[:, 1, :], start=False, stop=True)
            close_fill("cs", mm)
            start_sum(1, 1)
            assert next(order, None) is None

            BA, BB, BC, BD = 4, 5, 6, 7

            def gather(c, to=BD):
                d = ps[:, to, :].rearrange("p (k b r c) -> p k b r c", k=2, b=2, r=2)
                for kk in range(2):
                    k = 2 * c + kk
                    for r, src in enumerate((h2hi, h2lo)):
                        for t in range(TT):
                            mm = pe.matmul(d[:, kk, :, r, :], src[:, t, k * P:(k + 1) * P], selp[:, t, :, :],
                                           start=(t == 0), stop=(t == TT - 1))
                mm.then_inc(s["gathered"], 1)

            def scatter(b):
                for t in range(TT):
                    for part in (yhi, ylo):
                        for half in range(2):
                            mm = pe.matmul(ps[:, 2 * t + half, :], selT[b][:, t * P:(t + 1) * P],
                                           part[:, half * 512:(half + 1) * 512], start=False, stop=False,
                                           skip_group_check=True)
                    mm.then_inc(s["scattered"], 1)

            def products(q0, i, dst, lhsT, k_tiles):
                halves = k_tiles // 4
                for h in range(halves):
                    pe.wait_ge(s["lo_ok"], i * 24 + (q0 + h + 1))
                    for kk in range(4):
                        k = 4 * h + kk
                        for part in (whi, wlo):
                            mm = pe.matmul(ps[:, dst, :], lhsT(k), part[:, (q0 + h) % SPLIT, kk, :],
                                           start=(k == 0 and part is whi), stop=(k == k_tiles - 1 and part is wlo))
                    mm.then_inc(s["half_done"], 1)

            def step(i, c, tail=False):
                n, e = i * 4 + c, i * 4 + (c + 1)
                first, final = c < 0, tail and c == 3
                p, b = (c + 1) // 2, (c + 1) % 2
                more = not (tail and c >= 1)
                q = 4 + HALVES * c
                chunks = i * 8 + (4 * (p + 1) + (2 * b if more else 0))
                tokens = xg[p % 2]

                def x_rows(k):
                    if first and k % 2 == 0:
                        pe.wait_ge(s["xg_ok"], k // 2 + 1)
                    return tokens[:, k, b, :, :].rearrange("p r c -> p (r c)")

                def hidden_rows(k):
                    return hidden[:, k, :, :].rearrange("p r c -> p (r c)")

                if not first:
                    pe.wait_ge(s["hs_ok"], n * 2 + 2)
                    pe.wait_ge(s["silu_ok"], n + 1)
                    for t in range(HC):
                        mm = pe.matmul(ps[:, BC, (HC + t) * CAP:(HC + t + 1) * CAP], hs[:, 1, t * P:(t + 1) * P],
                                       foldw[1 - b][:], start=True, stop=True)
                    mm.then_inc(s["folded"], 1)
                if not final:
                    if b == 0 and not first:
                        pe.wait_ge(s["xg_ok"], i * 8 + 4 * (p + 1))
                    products(q + 2 if first else q, i, BA, x_rows, KD)
                    pe.wait_ge(s["dup_ok"], e + 1)
                    pe.wait_ge(s["xg_ok"], chunks)
                    for t in range(TT):
                        pe.transpose(ps[:, BD, t * P:(t + 1) * P], seldup[b][:, t, :], ident[:])
                    for t in range(TT):
                        mm = pe.matmul(ps[:, BD, T:T + 1], seldup[b][:, t, :], wcol[:, b, t:t + 1],
                                       start=(t == 0), stop=(t == TT - 1))
                    mm.then_inc(s["selT_full"], 1)
                if not first:
                    pe.wait_ge(s["hidlo_ok"], n + 1)
                    products(q if final else q + 2, i, BB, hidden_rows, HC)
                if not final:
                    pe.wait_ge(s["hs_ok"], e * 2 + 1)
                    for t in range(HC):
                        mm = pe.matmul(ps[:, BC, t * CAP:(t + 1) * CAP], hs[:, 0, t * P:(t + 1) * P], fold[:],
                                       start=True, stop=True)
                    mm.then_inc(s["folded"], 1)
                if not first:
                    products(q + 1 if final else q + 3, i, BA, hidden_rows, HC)
                if final:
                    pe.wait_ge(s["ylo_ok"], n * 2 + 2)
                    scatter(1 - b)
                    return
                pe.wait_ge(s["selT_ok"], e + 1)
                if more:
                    pe.wait_ge(s["selp_ok"], i * 2 + (p + 2))
                    gather(2 * b)
                if not first:
                    pe.wait_ge(s["ylo_ok"], n * 2 + 1)
                products(q + 4, i, BB, x_rows, KD)
                if not first:
                    pe.wait_ge(s["ylo_ok"], n * 2 + 2)
                    scatter(1 - b)
                if more:
                    pe.wait_ge(s["xg_ok"], chunks + 1)
                    gather(2 * b + 1)

            pe.wait_ge(s["selp_ok"], 1)
            pe.wait_ge(s["h2r_ok"], 2)
            for c in range(4):
                gather(c, FIRST_BANKS[c])
            pe.wait_ge(s["fold_ok"], 1)
            step(0, -1)
            pe.wait_ge(s["quads_ok"], 1)
            last_quad = pe.value_load(last_quad_i[0:1, 0:1], min_val=NE // 4 - 1, max_val=NE // 4 * ROUNDS - 1)
            with pe.Fori(0, last_quad) as i:
                for c in range(4):
                    step(i, c)
            for c in range(4):
                step(last_quad, c, tail=True)

        @block.scalar
        def _(a):
            def free(ins, name):
                ins.then_inc(drained[BANK[name]], 1)

            def need(sem, n):
                a.wait_ge(s[sem], n)

            def move(dst, name, cols=512):
                wait_full(a, name)
                free(a.activation(dst, bank(name)[:, 0:cols], ACT.Copy), name)

            def high_part(q, i=0, tail=False):
                m = q // 2
                a.wait_ge(raw_place(m)[1], i * (12 // RAW * 16) + 16 * (max(m - 1, 0) // RAW + 1))
                a.activation(whi[:, q % SPLIT, :, :], raw_half(q, tail), ACT.Copy).then_inc(s["hi_ok"], 1)

            need("const_ok", 1)
            a.activation(small[:, 57:58], small[:, 4:5], ACT.Sqrt)
            for t in range(TT):
                need(f"x_in{t}", 16)
                a.activation(blk(4 + t), x_sb[:, t, :], ACT.Square, accum_out=small[:, t:t + 1]).then_inc(s["ssq"], 1)
            need("ssq", 2)
            a.activation(small[:, 2:4], small[:, 0:2], ACT.Sqrt, scale=1.0 / D, bias=small[:, 4:5]).then_inc(s["ssq"], 1)
            wait_drained(a, "par")
            for n in (0, 2):
                wait_full(a, f"hT{n}")
                for i in range(2):
                    k = 2 * n + i
                    ins = a.activation(hT[:, k, :], bank(f"hT{n}")[:, i * T:(i + 1) * T], ACT.Copy, scale=pcol("norm1_g", k))
                free(ins, f"hT{n}")
            for n in range(4):
                wait_full(a, f"hT{n}")
            move(blk(0)[:, 0:512], "lora")
            for i in range(2):
                move(blk(4)[:, i * 512:(i + 1) * 512], f"rk{i}")
            need("lora_ok", 2)
            a.activation(tanh_w, lora[0:64, 0, :], ACT.Tanh).then_inc(s["tanh_ok"], 1)
            a.activation(sig_g[:], lora[:, 1, :], ACT.Sigmoid).then_inc(s["sigg_ok"], 1)
            for i in range(2):
                wait_full(a, f"u{i}")
                for c in range(2):
                    ct = 2 * i + c
                    ins = a.activation(logw[:, ct, :], bank(f"u{i}")[:, c * T:(c + 1) * T], ACT.Sigmoid, bias=pcol("w0", ct))
                free(ins, f"u{i}")
            for i in range(2):
                wait_full(a, f"a{i}")
                for c in range(2):
                    ct = 2 * i + c
                    ins = a.activation(iclr[:, ct, :], bank(f"a{i}")[:, c * T:(c + 1) * T], ACT.Sigmoid, bias=pcol("a0", ct))
                free(ins, f"a{i}")
            need("k_ok", 4)
            for ct in range(CT):
                a.activation(sq[:, ct, :], k_[:, ct, :], ACT.Square, scale=pcol("k_k", ct)).then_inc(s["sq_ok"], 1)
            for i in range(2):
                move(blk(1)[:, i * 512:(i + 1) * 512], f"rr{i}")
            for i in range(2):
                move(blk(2)[:, i * 512:(i + 1) * 512], f"rv{i}")
            wait_drained(a, "ss0", "ss1")
            a.activation(blk(12), blk(12), ACT.Sqrt).then_inc(s["norm_ok"], 1)
            need("logw_ok", 2)
            a.activation(blk(9), blk(8), ACT.Exp).then_inc(s["exps_ok"], 1)
            a.activation(blk(10), blk(8), ACT.Exp, scale=-1.0).then_inc(s["exps_ok"], 1)
            a.activation(blk(7), blk(7), ACT.Exp).then_inc(s["exps_ok"], 1)
            a.activation(small[:, 8:12], small[:, 8:12], ACT.Exp).then_inc(s["exps_ok"], 1)
            for i in range(2):
                move(qk[:, 0, 2 * i:2 * i + 2, :].rearrange("p c t -> p (c t)"), f"aq{i}")
            for i in range(2):
                move(qk[:, 1, 2 * i:2 * i + 2, :].rearrange("p c t -> p (c t)"), f"ak{i}")
            for i in range(2):
                move(pz[:, 2 * i:2 * i + 2, :].rearrange("p c t -> p (c t)"), f"pool{i}")
            for c in range(2):
                move(vn[:, c, :], f"vn{c}")
            move(bkn[:, 0, :], "bn")
            move(bkn[:, 1, :], "kn")
            need("masks_ok", 4)
            a.activation(tri_ones[:, 0, :], causal[:, 0, :], ACT.Copy).then_inc(s["tri_ones_ok"], 1)
            a.activation(tri_ones[:, 1, :], ones[:], ACT.Copy).then_inc(s["tri_ones_ok"], 1)
            need("smax_ok", 3)
            for c in range(TT):
                for h in range(H):
                    p = prob[:, h, 0:P] if c == 0 else prob[:, h, P:3 * P]
                    ins = a.activation(p, p, ACT.Exp, scale=2.0 ** -(h + 1), bias=amax[:, c, h:h + 1],
                                       accum_out=asum[:, c, h:h + 1])
            ins.then_inc(s["exp_ok"], 1)
            for t in range(TT):
                move(va[:, t, :], f"av{t}")

            for g in range(4):
                wait_full(a, f"G1_{g}")
                free(a.activation(blk(10 + g // 2)[:, (g % 2) * 512:(g % 2 + 1) * 512], bank(f"G1_{g}"), ACT.Copy),
                     f"G1_{g}")
            for size in LEVELS:
                for g in range(4):
                    wait_full(a, f"A{size}_{g}")
                    dst, src = triA[:, 4 * g:4 * g + 4, :], bank(f"A{size}_{g}").rearrange("p (n t) -> p n t", n=4)
                    if size == 64:
                        dst = triA[64:P, 4 * g:4 * g + 4, 0:64]
                        src = bank(f"A{size}_{g}")[64:P, 0:256].rearrange("p (n t) -> p n t", n=4)
                    free(a.activation(dst, src, ACT.Copy), f"A{size}_{g}")
                for g in range(4):
                    wait_full(a, f"G{size}_{g}")
                    free(a.activation(blk(10 + g // 2)[:, (g % 2) * 512:(g % 2 + 1) * 512], bank(f"G{size}_{g}"), ACT.Copy),
                         f"G{size}_{g}")
            need("prob_ok", 2)
            for h in range(H):
                wait_full(a, f"pt{h}")
                free(a.activation(probT[:, h % 2, :], bank(f"pt{h}")[:, 0:384], ACT.Copy), f"pt{h}")
            for i in range(2):
                move(bt[:, 2 * i:2 * i + 2, :].rearrange("p c t -> p (c t)"), f"o{i}")
            for i, name in enumerate(("pw", "pw1")):
                wait_full(a, "pw1")
                for c in range(2):
                    ct = 2 * i + c
                    ins = a.activation(pz[:, ct, :], bank(name)[:, c * T:(c + 1) * T], ACT.Copy, scale=pcol("pool_scale", ct))
                free(ins, name)
            move(xs[0], "X0")

            def gate(br, half):
                for i, part in enumerate("ab"):
                    name = f"g{br}{half}{part}"
                    wait_full(a, name)
                    k = 4 * half + 2 * i
                    free(a.activation(gates[:, k:k + 2, :].rearrange("p k t -> p (k t)"), bank(name), ACT.Sigmoid), name)

            gate("C", 0)
            move(sa[0], "SA0")
            gate("C", 1)
            for parity, name in enumerate(("X1e", "X1o")):
                wait_full(a, name)
                free(a.activation(xs[1].rearrange("p (i q d) -> p i q d", q=2, d=DH)[:, :, parity, :],
                                  bank(name)[:, 0:256].rearrange("p (i d) -> p i d", d=DH), ACT.Copy), name)
            wait_drained(a, "pC0", "pC1", "pC2", "pC3")
            gate("A", 0)
            move(sa[1], "SA1")
            gate("A", 1)
            wait_full(a, "Y0")
            free(a.activation(y_raw[:, :, 0:P], bank("Y0").rearrange("p (c t) -> p c t", c=CT), ACT.Copy), "Y0")
            for parity, name in enumerate(("Y1e", "Y1o")):
                rows = slice(64 * parity, 64 * parity + 64)
                wait_full(a, name)
                free(a.activation(y_raw[rows, :, P:T], ps[rows, BANK[name], :].rearrange("p (c t) -> p c t", c=CT), ACT.Copy),
                     name)
            need("merged_ok", 4)
            wait_drained(a, "mu0", "mu1")
            a.activation(blk(12), blk(9), ACT.Square).then_inc(s["ysq_ok"], 1)
            gate("B", 0)
            for i in range(2):
                wait_full(a, f"va{i}")
                free(a.activation(blk(13)[:, i * 512:(i + 1) * 512], bank(f"va{i}"), ACT.Sqrt, scale=1.0 / DH,
                                  bias=small[:, 5:6]), f"va{i}")
            gate("B", 1)
            wait_full(a, "gB1b")
            wait_drained(a, "gg0", "gg1")
            for q in range(SPLIT):
                high_part(q)
            for t in range(TT):
                wait_drained(a, f"wo{2 * t}", f"wo{2 * t + 1}")
                a.activation(h2[:, t, :], x2[:, t, :], ACT.Square, accum_out=small[:, 12 + t:13 + t]).then_inc(s["x2ssq"], 1)
                need("x2ssq", 2 * t + 1)
                a.activation(small[:, 14 + t:15 + t], small[:, 12 + t:13 + t], ACT.Sqrt, scale=1.0 / D,
                             bias=small[:, 4:5]).then_inc(s["x2ssq"], 1)
                for half in range(2):
                    name = f"h2T{2 * t + half}"
                    wait_full(a, name)
                    free(a.activation(hT[:, 4 * half:4 * half + 4, t * P:(t + 1) * P],
                                      bank(name).rearrange("p (k c) -> p k c", k=4), ACT.Copy), name)
                need("h2_ok", t + 1)
                a.activation(h2hi[:, t, :], h2[:, t, :], ACT.Copy).then_inc(s["h2hi_ok"], 1)
            need("eexp_in", 1)
            a.activation(small[:, 32:40], small[:, 32:40], ACT.Exp).then_inc(s["eexp_ok"], 1)
            need("eexp_in", 2)
            a.activation(small[:, 24:26], small[:, 24:26], ACT.Exp).then_inc(s["eexp_ok"], 1)
            def move_gathered(p, c, count, source=7):
                a.wait_ge(s["gathered"], count)
                a.activation(xg[p][:, 2 * c:2 * c + 2, :, :, :].rearrange("p k b r c -> p (k b r c)"), ps[:, source, :],
                             ACT.Copy).then_inc(s["xg_ok"], 1)

            def done_then_split(q, i, tail):
                a.wait_ge(s["half_done"], i * 24 + (q + 1))
                if not (tail and q + SPLIT >= 24):
                    high_part(q + SPLIT, i, tail)

            def hidden_high(i, c):
                a.wait_ge(s["hid_ok"], i * 4 + (c + 1))
                a.activation(hidden[:, :, 0, :], hid.rearrange("p (k c) -> p k c", k=HC), ACT.Copy).then_inc(
                    s["hidhi_ok"], 1)

            def load_silu_table(count):
                a.wait_ge(s["table_ok"], count)
                a.activation(small[:, 59:60], small[:, 4:5], ACT.Silu).then_inc(s["table_ok"], 1)

            def step_start(i, c, tail=False):
                final = tail and c == 3
                q = 4 + HALVES * c
                if not final:
                    done_then_split(q, i, tail)
                    a.wait_ge(s["half_done"], i * 24 + (q + 2))
                    a.activation(hs[:, 0, :], ps[:, 4, :], ACT.Copy).then_inc(s["hs_ok"], 1)
                    done_then_split(q + 1, i, tail)
                    q += 2
                a.wait_ge(s["half_done"], i * 24 + (q + 1))
                a.activation(yhi[:, 0:512], ps[:, 5, :], ACT.Copy).then_inc(s["yhi_ok"], 1)
                done_then_split(q, i, tail)

            def step_rest(i, c, tail=False):
                n, e = i * 4 + c, i * 4 + (c + 1)
                first, final = c < 0, tail and c == 3
                p, b = (c + 1) // 2, (c + 1) % 2
                more = not (tail and c >= 1)
                q = 4 + HALVES * c
                chunks = i * 8 + (4 * (p + 1) + 2 * b)
                if not final:
                    a.wait_ge(s["folded"], e * 2 + 1)
                    a.activation(silu, ps[:, 6, 0:T], ACT.Silu).then_inc(s["silu_ok"], 1)
                if not first:
                    a.wait_ge(s["half_done"], i * 24 + ((q + 1 if final else q + 3) + 1))
                    a.activation(yhi[:, 512:1024], ps[:, 4, :], ACT.Copy).then_inc(s["yhi_ok"], 1)
                if final:
                    return
                if not first:
                    done_then_split(q + 3, i, tail)
                if more:
                    move_gathered((p + 1) % 2, 2 * b, chunks + 1)
                done_then_split(q + 4, i, tail)
                a.wait_ge(s["half_done"], i * 24 + (q + 6))
                a.activation(hs[:, 1, :], ps[:, 5, :], ACT.Copy).then_inc(s["hs_ok"], 1)
                if more and b == 1:
                    move_gathered((p + 1) % 2, 2 * b + 1, chunks + 2)
                done_then_split(q + 5, i, tail)
                if more and b == 0:
                    move_gathered((p + 1) % 2, 2 * b + 1, chunks + 2)

            need("const_ok", 1)
            a.activation(small[:, 59:60], small[:, 4:5], ACT.Silu).then_inc(s["table_ok"], 1)
            for c in range(4):
                move_gathered(0, c, c + 1, FIRST_BANKS[c])
            done_then_split(0, 0, False)
            a.wait_ge(s["half_done"], 2)
            a.activation(hs[:, 0, :], ps[:, 4, :], ACT.Copy).then_inc(s["hs_ok"], 1)
            done_then_split(1, 0, False)
            step_rest(0, -1)
            hidden_high(0, 0)
            need("quads_ok", 1)
            last_quad = a.value_load(last_quad_i[0:1, 0:1], min_val=NE // 4 - 1, max_val=NE // 4 * ROUNDS - 1)
            with a.Fori(0, last_quad) as i:
                load_silu_table(i + 1)
                for c in range(4):
                    step_start(i, c)
                    step_rest(i, c)
                    hidden_high(i + (c + 1) // 4, (c + 1) % 4)
            for c in range(4):
                step_start(last_quad, c, tail=True)
                step_rest(last_quad, c, tail=True)
                if c < 3:
                    hidden_high(last_quad, c + 1)
            a.activation(small[:, 58:59], small[:, 4:5], ACT.Sqrt)
            for t in range(TT):
                a.wait_ge(s["scattered"], last_quad * 8 + (7 + t))
                a.activation(h2[:, t, :], ps[:, 2 * t:2 * t + 2, :].rearrange("p b c -> p (b c)"), ACT.Square,
                             accum_out=small[:, 16 + t:17 + t]).then_inc(s["fssq"], 1)
                need("fssq", 2 * t + 1)
                a.activation(small[:, 18 + t:19 + t], small[:, 16 + t:17 + t], ACT.Sqrt, scale=1.0 / D,
                             bias=small[:, 4:5]).then_inc(s["fssq"], 1)

        @block.vector
        def _(v):
            chain = [0]

            def link(ins):
                chain[0] += 1
                ins.then_inc(s["dve"], 1)
                v.wait_ge(s["dve"], chain[0])

            def free(ins, name):
                ins.then_inc(drained[BANK[name]], 1)

            def need(sem, n):
                v.wait_ge(s[sem], n)

            v.memset(small[:, 4:5], RMS_EPS)
            v.memset(small[:, 5:6], LNX_EPS).then_inc(s["const_ok"], 1)
            need("x_in0", 16)
            need("x_in1", 16)
            need("ssq", 3)
            link(v.reciprocal(small[:, 6:8], small[:, 2:4]))
            for t in range(TT):
                v.tensor_scalar(xn[:, t, :], x_sb[:, t, :], small[:, 6 + t:7 + t], None, ALU.mult).then_inc(s["xn_ok"], 1)
            wait_full(v, "par")
            free(v.tensor_copy(par[:], bank("par")[:, 0:54]), "par")
            wait_drained(v, "par")
            link(v.tensor_scalar(small[:, 20:24], par[:, pc["k_a"]:pc["k_a"] + 4], -1.0, 1.0, ALU.mult, ALU.add))
            for n in (1, 3):
                wait_full(v, f"hT{n}")
                for i in range(2):
                    k = 2 * n + i
                    ins = v.tensor_scalar(hT[:, k, :], bank(f"hT{n}")[:, i * T:(i + 1) * T], pcol("norm1_g", k), None, ALU.mult)
                free(ins, f"hT{n}")

            def token_shift(z, d, tiles, mu0, sem):
                v.tensor_tensor(d[:, :, 1:T], z[:, :, 0:T - 1], z[:, :, 1:T], ALU.subtract)
                link(v.tensor_scalar(d[:, :, 0:1], z[:, :, 0:1], -1.0, None, ALU.mult))
                for c in range(tiles):
                    v.scalar_tensor_tensor(out=z[:, c, :], in0=d[:, c, :], scalar=pcol("rwkv_mu", mu0 + c),
                                           in1=z[:, c, :], op0=ALU.mult, op1=ALU.add).then_inc(s[sem], 1)

            wait_drained(v, "lora")
            token_shift(lora, dlora, 2, 12, "lora_ok")
            wait_drained(v, "rk0")
            wait_drained(v, "rk1")
            token_shift(k_, dz, CT, 4, "k_ok")
            wait_drained(v, "u0")
            wait_drained(v, "u1")
            need("ones_ok", 4)
            link(v.tensor_scalar(blk(5), blk(5), -DECAY_SCALE, None, ALU.mult))
            link(v.tensor_tensor_scan(blk(7), scan_ones, blk(5), 0.0, ALU.mult, ALU.add))
            lp8 = chunks(blk(7))
            v.tensor_tensor(chunks(blk(8)), lp8, lp8[:, :, 63:64].to_broadcast([P, 8, P]), ALU.subtract).then_inc(
                s["logw_ok"], 1)
            need("logw_ok", 1)
            v4 = lambda ap: ap.rearrange("p (c k t) -> p c k t", c=CT, k=TT)
            link(v.tensor_tensor(small[:, 8:12], v4(blk(8))[:, :, 0, P - 1], v4(blk(7))[:, :, 1, 63], ALU.add))
            v.tensor_tensor(blk(7), blk(8), blk(5), ALU.subtract).then_inc(s["logw_ok"], 1)
            need("k_ok", 4)
            for ct in range(CT):
                v.tensor_scalar(kk[:, ct, :], k_[:, ct, :], pcol("k_k", ct), None, ALU.mult).then_inc(s["kk_ok"], 1)
            wait_drained(v, "rr0")
            wait_drained(v, "rr1")
            token_shift(r_, dz, CT, 0, "r_ok")
            wait_drained(v, "rv0")
            wait_drained(v, "rv1")
            need("r_ok", 4)
            token_shift(v_, dz, CT, 8, "v_ok")
            for i in range(2):
                wait_full(v, f"ss{i}")
                if i == 0:
                    wait_full(v, "ss1")
                ins = v.tensor_scalar(blk(12)[:, i * 512:(i + 1) * 512], bank(f"ss{i}"), 1e-24, None, ALU.max)
                free(ins, f"ss{i}")
            need("norm_ok", 1)
            link(v.reciprocal(blk(12), blk(12)))
            need("kk_ok", 4)
            link(v.tensor_tensor(blk(11), blk(11), blk(12), ALU.mult))
            need("exps_ok", 4)
            ar8 = ar[:, :, :, :, :].rearrange("p c k m t -> p (c k) m t")
            v.scalar_tensor_tensor(out=ar8[:, :, 0, :], in0=chunks(blk(11)), scalar=-1.0, in1=chunks(blk(7)),
                                   op0=ALU.mult, op1=ALU.mult).then_inc(s["ar_ok"], 1)
            v.tensor_tensor(ar8[:, :, 1, :], chunks(blk(1)), chunks(blk(9)), ALU.mult).then_inc(s["ar_ok"], 1)
            wait_drained(v, "a0")
            wait_drained(v, "a1")
            link(v.tensor_tensor(blk(13), blk(11), blk(6), ALU.mult))
            flat = lambda t3: t3[:, :, :].rearrange("p c t -> p (c t)")
            v.tensor_tensor(flat(bt), blk(13), blk(10), ALU.mult).then_inc(s["bt_ok"], 1)
            need("v_ok", 4)
            for ct in range(CT):
                ins = v.tensor_scalar(kprime[:, ct, :], iclr[:, ct, :], pcol("k_a", ct), small[:, 20 + ct:21 + ct],
                                      ALU.mult, ALU.add)
            link(ins)
            link(v.tensor_tensor(blk(3), blk(3), blk(4), ALU.mult))
            v.tensor_tensor(flat(kt), blk(3), blk(10), ALU.mult).then_inc(s["kt_ok"], 1)
            for ct in range(CT):
                v.scalar_tensor_tensor(out=tmp[:, ct, :], in0=r_[:, ct, :], scalar=pcol("r_k", ct), in1=kprime[:, ct, :],
                                       op0=ALU.mult, op1=ALU.mult).then_inc(s["bonin_ok"], 1)
            for i in range(2):
                wait_full(v, f"bon{i}")
                ins = v.tensor_tensor(flat(bonus)[:, i * 512:(i + 1) * 512], bank(f"bon{i}"),
                                      blk(2)[:, i * 512:(i + 1) * 512], ALU.mult)
                free(ins, f"bon{i}")
            def pool_group(gi):
                if gi == 0:
                    wait_drained(v, "pool0", "pool1")
                    need("misc_ok", 14)
                    link(v.reciprocal(count_inv[:], count_inv[:]))
                src, bufs, step = pz[:, gi, :], (pool_a, pool_b), 1
                for j in range(gi + 1):
                    dst = bufs[j % 2]
                    v.tensor_tensor(dst[:, step:T], src[:, step:T], src[:, 0:T - step], ALU.add)
                    link(v.tensor_copy(dst[:, 0:step], src[:, 0:step]))
                    src, step = dst, 2 * step
                win = step
                other = bufs[(gi + 1) % 2]
                link(v.tensor_tensor(other[:, 0:win], src[:, 0:win], count_inv[:, gi, 0:win], ALU.mult))
                v.tensor_tensor(pz[:, gi, 0:win], other[:, 0:win], pz[:, gi, 0:win], ALU.subtract)
                v.scalar_tensor_tensor(out=pz[:, gi, win:T], in0=src[:, win:T], scalar=1.0 / win,
                                       in1=pz[:, gi, win:T], op0=ALU.mult, op1=ALU.subtract).then_inc(s["pool_ok"], 1)
                need("pool_ok", gi + 1)

            need("masks_ok", 4)
            flat_mask = causal[:, :, :].rearrange("p m t -> p (m t)")
            wait_full(v, "bon1")
            need("tanh_ok", 1)
            need("sigg_ok", 1)
            need("sq_ok", 4)
            for n in range(16):
                wait_full(v, f"sc{n}")
                ins = v.tensor_tensor(sc[:, n, :, :].rearrange("p m t -> p (m t)"), bank(f"sc{n}"), flat_mask, ALU.mult)
                free(ins, f"sc{n}")
                if n % 4 == 3:
                    pool_group(n // 4)
            need("dist_ok", 1)
            for n in range(6):
                wait_full(v, f"at{n}")
                for i, h in enumerate(attn_heads(n)):
                    slope = 2.0 ** -(h + 1)
                    if n < 4:
                        ins = v.scalar_tensor_tensor(out=prob[:, h, P:3 * P], in0=bank(f"at{n}")[:, i * T:(i + 1) * T],
                                                     scalar=DH ** -0.5 / slope, in1=dist[:], op0=ALU.mult, op1=ALU.subtract)
                    else:
                        ins = v.scalar_tensor_tensor(out=prob[:, h, 0:P], in0=bank(f"at{n}")[:, i * P:(i + 1) * P],
                                                     scalar=DH ** -0.5 / slope, in1=dist[:, P:T], op0=ALU.mult,
                                                     op1=ALU.subtract)
                free(ins, f"at{n}")
            wait_drained(v, *(f"at{n}" for n in range(2, 6)))
            v.tensor_reduce(amax[:, 0, :], prob[:, :, 0:P], AX.X, ALU.max).then_inc(s["smax_ok"], 1)
            v.tensor_reduce(amax[:, 1, :], prob[:, :, P:3 * P], AX.X, ALU.max).then_inc(s["smax_ok"], 1)
            need("smax_ok", 2)
            v.tensor_tensor(amax[:], amax[:], slopes[:], ALU.mult).then_inc(s["smax_ok"], 1)
            need("levels_ok", 7)

            def fill_blocks(name, g, lev):
                wait_full(v, name)
                mask = level_mask[:, lev, :].bitcast(I32).unsqueeze(1).to_broadcast([P, 4, P])
                return v.copy_predicated(tri[:, 4 * g:4 * g + 4, :], mask, bank(name).rearrange("p (n t) -> p n t", n=4))

            for g in range(4):
                link(v.tensor_copy(tri[:, 4 * g:4 * g + 4, :], ident[:, :].unsqueeze(1).to_broadcast([P, 4, P])))
            for g in range(4):
                free(fill_blocks(f"L{g}", g, 0), f"L{g}")
            need("exp_ok", 1)
            link(v.reciprocal(asum[:], asum[:]))
            rs = asum[:, :, :]
            v.tensor_tensor(prob[:, :, 0:P], prob[:, :, 0:P], rs[:, 0, :].unsqueeze(2).to_broadcast([P, H, P]),
                            ALU.mult).then_inc(s["prob_ok"], 1)
            v.tensor_tensor(prob[:, :, P:3 * P], prob[:, :, P:3 * P], rs[:, 1, :].unsqueeze(2).to_broadcast([P, H, 2 * P]),
                            ALU.mult).then_inc(s["prob_ok"], 1)
            for lev, size in enumerate(LEVELS):
                for g in range(4):
                    if size == 64:
                        wait_full(v, f"T{size}_{g}")
                        ins = v.tensor_copy(tri[64:P, 4 * g:4 * g + 4, 0:64],
                                            bank(f"T{size}_{g}")[64:P, 0:256].rearrange("p (n t) -> p n t", n=4))
                    else:
                        ins = fill_blocks(f"T{size}_{g}", g, lev + 1)
                    free(ins, f"T{size}_{g}")
            wait_full(v, "St")
            for ct in range(CT):
                ins = v.tensor_scalar(state[:, ct, :], bank("St")[:, ct * DH:(ct + 1) * DH], small[:, 8 + ct:9 + ct], None,
                                      ALU.mult)
            free(ins, "St")

            def merge(br):
                for n in range(4):
                    name = f"p{br}{n}"
                    wait_full(v, name)
                    gsl = gates[:, 2 * n:2 * n + 2, :].rearrange("p k t -> p (k t)")
                    msl = merged[:, 2 * n:2 * n + 2, :].rearrange("p k t -> p (k t)")
                    wait_drained(v, f"g{br}{n // 2}{'ab'[n % 2]}")
                    if br == "C":
                        free(v.tensor_tensor(msl, gsl, bank(name), ALU.mult), name)
                        continue
                    free(v.tensor_tensor(gsl, gsl, bank(name), ALU.mult), name)
                    wait_drained(v, name)
                    v.tensor_tensor(msl, msl, gsl, ALU.add).then_inc(s["merged_ok"], 1)

            wait_full(v, "o1")
            merge("C")
            wait_drained(v, "pC0", "pC1", "pC2", "pC3")
            merge("A")
            wait_drained(v, "Y0")
            wait_drained(v, "Y1e")
            wait_drained(v, "Y1o")
            for i in range(2):
                wait_full(v, f"mu{i}")
                ins = v.scalar_tensor_tensor(out=blk(9)[:, i * 512:(i + 1) * 512], in0=bank(f"mu{i}"), scalar=-1.0 / DH,
                                             in1=blk(8)[:, i * 512:(i + 1) * 512], op0=ALU.mult, op1=ALU.add)
                free(ins, f"mu{i}")
            for i in range(2):
                wait_drained(v, f"va{i}")
            link(v.reciprocal(blk(13), blk(13)))
            link(v.tensor_tensor(blk(9), blk(9), blk(13), ALU.mult))
            for ct in range(CT):
                ins = v.tensor_scalar(y_cen[:, ct, :], y_cen[:, ct, :], pcol("lnx_g", ct), pcol("lnx_b", ct), ALU.mult, ALU.add)
            link(ins)
            link(v.tensor_tensor(blk(9), blk(9), flat(bonus), ALU.add))
            for i in range(2):
                wait_full(v, f"gg{i}")
                ins = v.tensor_tensor(flat(kt)[:, i * 512:(i + 1) * 512], blk(9)[:, i * 512:(i + 1) * 512], bank(f"gg{i}"),
                                      ALU.mult)
                free(ins, f"gg{i}")
            need("merged_ok", 4)
            merge("B")

            def low_part(q, i=0, tail=False):
                v.wait_ge(s["hi_ok"], i * 24 + (q + 1))
                v.tensor_tensor(wlo[:, q % SPLIT, :, :], raw_half(q, tail), whi[:, q % SPLIT, :, :].bitcast(F32),
                                ALU.subtract).then_inc(s["lo_ok"], 1)

            for q in range(SPLIT):
                if q == 2:
                    need("lo_ok", 2)
                low_part(q)
            need("x_again", 16)
            need("bcast2_ok", 1)
            for t in range(TT):
                for half in range(2):
                    name = f"wo{2 * t + half}"
                    wait_full(v, name)
                    xsl = x2[:, t, half * 512:(half + 1) * 512]
                    free(v.tensor_tensor(xsl, bank(name), xsl, ALU.add), name)
                wait_drained(v, f"wo{2 * t}", f"wo{2 * t + 1}")
                need("x2ssq", 2 * t + 2)
                link(v.reciprocal(small[:, 14 + t:15 + t], small[:, 14 + t:15 + t]))
                v.scalar_tensor_tensor(out=h2[:, t, :], in0=x2[:, t, :], scalar=small[:, 14 + t:15 + t], in1=norm2_b,
                                       op0=ALU.mult, op1=ALU.mult).then_inc(s["h2_ok"], 1)
                need("h2hi_ok", t + 1)
                v.tensor_tensor(h2lo[:, t, :], h2[:, t, :], h2hi[:, t, :].bitcast(F32), ALU.subtract).then_inc(
                    s["h2r_ok"], 1)
            need("rbcast_ok", 1)
            for t in range(TT):
                wait_full(v, f"rt{t}")
                free(v.tensor_tensor(lg[:, t, :], bank(f"rt{t}")[:, 0:NG + NE], router_b[:], ALU.add), f"rt{t}")
            wait_drained(v, "rt0", "rt1")
            gl, el = lg[:, :, 0:NG], lg[:, :, NG:]

            def tmp3(o, n):
                return rtmp[:, o:o + TT * n].rearrange("p (t n) -> p t n", t=TT)

            def col2(o):
                return small[:, o:o + 2]

            def wide(ap, n):
                return ap.unsqueeze(2).to_broadcast([P, TT, n])

            one1, one2, el2, cand, gw = tmp3(64, NE), tmp3(128, NE), tmp3(192, NE), tmp3(256, NE), tmp3(320, NE)
            g4, g4b = tmp3(384, NG), tmp3(392, NG)
            iota4 = iota_e[:, :, 0:NG]

            def first_max(dst, src, n, m, it, c):
                link(v.tensor_reduce(m, src, AX.X, ALU.max))
                link(v.tensor_tensor(c, src, wide(m, n), ALU.is_equal))
                link(v.scalar_tensor_tensor(out=c, in0=c, scalar=-100.0, in1=it, op0=ALU.mult, op1=ALU.add))
                link(v.tensor_reduce(col2(28), c, AX.X, ALU.min))
                link(v.tensor_tensor(dst, c, wide(col2(28), n), ALU.is_equal))

            first_max(g4, gl, NG, col2(26), iota4, g4b)
            v.tensor_tensor(small[:, 32:40].rearrange("p (t n) -> p t n", t=TT), gl, wide(col2(26), NG),
                            ALU.subtract).then_inc(s["eexp_in"], 1)
            link(v.tensor_scalar(g4b, g4, FAR, -FAR, ALU.mult, ALU.add))
            for t in range(TT):
                gsel = g4[:, t, :].unsqueeze(2).to_broadcast([P, NG, EPG])
                gpen = g4b[:, t, :].unsqueeze(2).to_broadcast([P, NG, EPG])
                e3 = el2[:, t, :].rearrange("p (g e) -> p g e", g=NG)
                link(v.tensor_tensor(e3, el[:, t, :].rearrange("p (g e) -> p g e", g=NG), gsel, ALU.mult))
                link(v.tensor_tensor(e3, e3, gpen, ALU.add))
            first_max(one1, el2, NE, col2(30), iota_e[:], cand)
            link(v.scalar_tensor_tensor(out=el2, in0=one1, scalar=-2 * FAR, in1=el2, op0=ALU.mult, op1=ALU.add))
            first_max(one2, el2, NE, col2(24), iota_e[:], cand)
            v.tensor_tensor(assigned[:], one1, one2, ALU.add).then_inc(s["cs_in"], 1)
            v.tensor_tensor(col2(24), col2(24), col2(30), ALU.subtract).then_inc(s["eexp_in"], 1)
            wait_full(v, "cs")
            v.tensor_reduce(small[:, 54:55], bank("cs")[:, 64:96], AX.X, ALU.max)
            place = bank("cs")[:, 0:64].rearrange("p (t n) -> p t n", t=TT)
            need("cs_in", 1)
            free(v.tensor_tensor(cand, place, assigned[:].bitcast(F32), ALU.mult), "cs")
            link(v.tensor_scalar(el2, assigned[:].bitcast(F32), 1000.0, -1000.0, ALU.mult, ALU.add))
            wait_drained(v, "cs")
            link(v.tensor_tensor(cand, cand, el2, ALU.add))
            for r in range(ROUNDS):
                ins = v.tensor_scalar(pos[:, :, r * NE:(r + 1) * NE], cand, float(-CAP * r), None, ALU.add)
            link(ins)
            for b in range(2):
                for t in range(TT):
                    ins = v.tensor_scalar(selp[:, t, b, :], iota_slot[:, 0, :], pos[:, t, b:b + 1], None, ALU.is_equal)
            ins.then_inc(s["selp_ok"], 1)
            link(v.tensor_scalar(small[:, 55:56], small[:, 54:55], CAP + 0.5, float(NE // 4), ALU.is_gt, ALU.mult))
            for r in range(2, ROUNDS):
                link(v.tensor_scalar(small[:, 56:57], small[:, 54:55], CAP * r + 0.5, float(NE // 4), ALU.is_gt, ALU.mult))
                link(v.tensor_tensor(small[:, 55:56], small[:, 55:56], small[:, 56:57], ALU.add))
            v.tensor_scalar(last_quad_i[:], small[:, 55:56], float(NE // 4 - 1), None, ALU.add).then_inc(s["quads_ok"], 1)
            need("eexp_ok", 1)
            link(v.tensor_reduce(col2(50), small[:, 32:40].rearrange("p (t n) -> p t n", t=TT), AX.X, ALU.add))
            need("eexp_ok", 2)
            link(v.tensor_scalar(col2(52), col2(24), 1.0, None, ALU.add))
            link(v.tensor_tensor(col2(50), col2(50), col2(52), ALU.mult))
            link(v.reciprocal(col2(50), col2(50)))
            link(v.tensor_tensor(col2(52), col2(50), col2(24), ALU.mult))
            link(v.tensor_tensor(one1, one1, wide(col2(50), NE), ALU.mult))
            link(v.tensor_tensor(one2, one2, wide(col2(52), NE), ALU.mult))
            link(v.tensor_tensor(gw, one1, one2, ALU.add))
            for r in range(ROUNDS):
                ins = v.tensor_copy(wts[:, :, r * NE:(r + 1) * NE], gw)
            ins.then_inc(s["wts_ok"], 1)

            need("fold_ok", 1)
            need("quads_ok", 1)
            last_quad = v.value_load(last_quad_i[0:1, 0:1], min_val=NE // 4 - 1, max_val=NE // 4 * ROUNDS - 1)

            def step(i, c, tail=False):
                n, e = i * 4 + c, i * 4 + (c + 1)
                first, final = c < 0, tail and c == 3
                b = (c + 1) % 2
                q = 4 + HALVES * c

                def split_ahead(j):
                    if not (tail and q + j + SPLIT >= 24):
                        low_part(q + j + SPLIT, i, tail)

                if not first:
                    v.wait_ge(s["folded"], n * 2 + 2)
                    v.tensor_tensor(hid, silu, ps[:, 6, T:2 * T], ALU.mult).then_inc(s["hid_ok"], 1)
                    v.wait_ge(s["hidhi_ok"], n + 1)
                    v.tensor_tensor(hidden[:, :, 1, :], hid.rearrange("p (k c) -> p k c", k=HC),
                                    hidden[:, :, 0, :].bitcast(F32), ALU.subtract).then_inc(s["hidlo_ok"], 1)
                    split_ahead(-1)
                if not final:
                    split_ahead(2 if first else 0)
                    v.wait_ge(s["selT_full"], e + 1)
                    v.tensor_scalar(foldw[b][:], fold[:], ps[:, 7, T:T + 1], None, ALU.mult)
                    v.tensor_copy(selT[b][:], ps[:, 7, 0:T]).then_inc(s["selT_ok"], 1)
                    split_ahead(3 if first else 1)
                for half in range(0 if first else 2):
                    v.wait_ge(s["yhi_ok"], n * 2 + (half + 1))
                    v.tensor_tensor(ylo[:, half * 512:(half + 1) * 512], ps[:, 5 - half, :],
                                    yhi[:, half * 512:(half + 1) * 512].bitcast(F32), ALU.subtract).then_inc(
                        s["ylo_ok"], 1)
                    split_ahead(2 + half)
                split_ahead(4)

            step(0, -1)
            with v.Fori(0, last_quad) as i:
                for c in range(4):
                    step(i, c)
            for c in range(4):
                step(last_quad, c, tail=True)
            need("bcastf_ok", 1)
            for t in range(TT):
                need("fssq", 2 * t + 2)
                link(v.reciprocal(small[:, 18 + t:19 + t], small[:, 18 + t:19 + t]))
                v.scalar_tensor_tensor(out=out_sb[:, t, :], in0=ps[:, 2 * t:2 * t + 2, :].rearrange("p b c -> p (b c)"),
                                       scalar=small[:, 18 + t:19 + t], in1=final_b, op0=ALU.mult, op1=ALU.mult).then_inc(
                    s["out_ok"], 1)


def attn_heads(n):
    return ((0, 2), (1, 3), (4, 6), (5, 7), (0, 2, 4, 6), (1, 3, 5, 7))[n]


NAMES = ("x norm1_g w_in rwkv_mu w0 w_decay_up a0 w_iclr_up w_gate_up k_k k_a r_k lnx_g lnx_b pool_w pool_scale "
         "w_branch w_out norm2_g router_grp_w router_grp_b router_exp_w router_exp_b exp_w1 exp_w3 exp_w2 "
         "final_norm_g").split()


def kernel(**inputs):
    import numpy as _np
    import concourse.bacc as _bacc
    from concourse import mybir as _mybir
    from concourse.bass_utils import run_bass_kernel_spmd as _run

    nc = _bacc.Bacc("TRN2", target_bir_lowering=False, num_devices=1)
    arrays, args = {}, {}
    for name in NAMES:
        a = _np.ascontiguousarray(inputs[name])
        arrays[f"in_{name}_dram"] = a
        args[name] = nc.dram_tensor(f"in_{name}_dram", a.shape, _mybir.dt.from_np(a.dtype), kind="ExternalInput").ap()
    out = nc.dram_tensor("out_0_dram", (1, T, D), _mybir.dt.float32, kind="ExternalOutput").ap()
    trunk_and_experts(nc, out=out, **args)
    r = _run(nc, [arrays], core_ids=[0])
    return r.results[0]["out_0_dram"]
```
